# Optimizing a Trainium2 kernel written in Bass

```python
import jax, jax.numpy as jnp
from jax import lax
import numpy as np

D_MODEL = 1024
BATCH = 1
SEQ = 1024
DEPTH = 1

N_HEADS = 8
HEAD_DK = 128
HEAD_DV = 128
KEY_DIM = N_HEADS * HEAD_DK
VAL_DIM = N_HEADS * HEAD_DV
QKV_CONV = 4
CHUNK = 64
SC_DIM = D_MODEL
SC_CONV = 3
N_GROUPS = 4
EXPERTS_PER_GROUP = 8
N_EXPERTS = N_GROUPS * EXPERTS_PER_GROUP
TOP_K = 2
D_EXPERT = 512
MOE_BLOCK = 128
N_MOD = 6
EPS = 1e-6
IN_WIDTHS = (2 * KEY_DIM + VAL_DIM, VAL_DIM, N_HEADS, N_HEADS, SC_DIM, SC_DIM, SC_DIM, D_MODEL, D_MODEL)
IN_TOTAL = 2 * KEY_DIM + 2 * VAL_DIM + 2 * N_HEADS + 3 * SC_DIM + 2 * D_MODEL

kernel_name = "hybrid_gdn_shortconv_hmoe_adaln"

def rmsnorm(x, g):
    xf = x.astype(jnp.float32)
    y = xf * lax.rsqrt(jnp.mean(xf * xf, axis=-1, keepdims=True) + EPS)
    return (y * g.astype(jnp.float32)).astype(x.dtype)

def l2norm(x):
    return x * lax.rsqrt(jnp.sum(x * x, axis=-1, keepdims=True) + EPS)

def causal_depthwise_conv(x, w):
    k_w, ch = w.shape
    return lax.conv_general_dilated(
        x, w[:, None, :].astype(x.dtype), window_strides=(1,), padding=((k_w - 1, 0),),
        dimension_numbers=("NWC", "WIO", "NWC"), feature_group_count=ch)

def split_cols(y):
    idx = np.cumsum(np.array(IN_WIDTHS))[:-1].tolist()
    return jnp.split(y, idx, axis=-1)

def gated_delta_rule_chunked(q, k, v, g, beta):
    bsz, t_len, h, dk = q.shape
    dv = v.shape[-1]
    n = t_len // CHUNK
    q = l2norm(q) * (dk ** -0.5)
    k = l2norm(k)

    def to_chunks(t):
        return t.reshape(bsz, n, CHUNK, h, -1).transpose(0, 3, 1, 2, 4)

    q, k, v = to_chunks(q), to_chunks(k), to_chunks(v)
    g = jnp.cumsum(g.reshape(bsz, n, CHUNK, h).transpose(0, 3, 1, 2), axis=-1)
    beta = beta.reshape(bsz, n, CHUNK, h).transpose(0, 3, 1, 2)[..., None]
    causal = jnp.tril(jnp.ones((CHUNK, CHUNK), bool))
    strict = jnp.tril(jnp.ones((CHUNK, CHUNK), bool), k=-1)
    diff = g[..., :, None] - g[..., None, :]
    decay = jnp.where(causal, jnp.exp(jnp.where(causal, diff, 0.0)), 0.0)
    k_beta = k * beta
    a = jnp.where(strict, jnp.einsum('bhnik,bhnjk->bhnij', k_beta, k) * decay, 0.0)
    eye = jnp.eye(CHUNK, dtype=a.dtype)
    t_inv = lax.linalg.triangular_solve(eye + a, jnp.broadcast_to(eye, a.shape),
                                        left_side=True, lower=True, unit_diagonal=True)
    u = jnp.einsum('bhnij,bhnjv->bhniv', t_inv, v * beta)
    w = jnp.einsum('bhnij,bhnjk->bhnik', t_inv, k_beta * jnp.exp(g)[..., None])
    intra = jnp.einsum('bhnik,bhnjk->bhnij', q, k) * decay
    q_dec = q * jnp.exp(g)[..., None]
    g_last = g[..., -1]
    k_dec = k * jnp.exp(g_last[..., None] - g)[..., None]

    def step(state, inp):
        u_n, w_n, q_n, intra_n, k_n, dec_n = inp
        v_new = u_n - jnp.einsum('bhck,bhkv->bhcv', w_n, state)
        o_n = jnp.einsum('bhck,bhkv->bhcv', q_n, state) + jnp.einsum('bhcs,bhsv->bhcv', intra_n, v_new)
        state = state * dec_n[..., None, None] + jnp.einsum('bhck,bhcv->bhkv', k_n, v_new)
        return state, o_n

    xs = tuple(jnp.moveaxis(t, 2, 0) for t in (u, w, q_dec, intra, k_dec, jnp.exp(g_last)))
    s0 = jnp.zeros((bsz, h, dk, dv), jnp.float32)
    _, o = lax.scan(step, s0, xs)
    return o.transpose(1, 0, 3, 2, 4).reshape(bsz, t_len, h, dv)

def hybrid_mixer(h, w_in, conv_qkv_w, a_log, dt_bias, onorm_g, w_proj_a, conv_sc_w, w_proj_b, w_out):
    bsz, t_len, _ = h.shape
    qkv, z, b_lg, a_lg, s_b, s_c, s_x, g_a, g_b = split_cols(h @ w_in)
    qkv = jax.nn.silu(causal_depthwise_conv(qkv, conv_qkv_w)).astype(jnp.float32)
    q, k, v = jnp.split(qkv, [KEY_DIM, 2 * KEY_DIM], axis=-1)
    q = q.reshape(bsz, t_len, N_HEADS, HEAD_DK)
    k = k.reshape(bsz, t_len, N_HEADS, HEAD_DK)
    v = v.reshape(bsz, t_len, N_HEADS, HEAD_DV)
    beta = jax.nn.sigmoid(b_lg.astype(jnp.float32))
    g = -jnp.exp(a_log.astype(jnp.float32)) * jax.nn.softplus(a_lg.astype(jnp.float32) + dt_bias.astype(jnp.float32))
    o = gated_delta_rule_chunked(q, k, v, g, beta)
    o = o * lax.rsqrt(jnp.mean(o * o, axis=-1, keepdims=True) + EPS) * onorm_g.astype(jnp.float32)
    o = o * jax.nn.silu(z.astype(jnp.float32).reshape(bsz, t_len, N_HEADS, HEAD_DV))
    y_a = o.reshape(bsz, t_len, VAL_DIM).astype(h.dtype) @ w_proj_a
    y_b = (s_b * causal_depthwise_conv(s_c * s_x, conv_sc_w)) @ w_proj_b
    merged = jax.nn.sigmoid(g_a) * y_a + jax.nn.sigmoid(g_b) * y_b
    return merged @ w_out

def hierarchical_moe(h, w_group, b_group, w_expert, b_expert, w1, w3, w2):
    bsz, t_len, d = h.shape
    tok = h.reshape(-1, d)
    m = tok.shape[0]
    g_logits = (tok @ w_group).astype(jnp.float32) + b_group.astype(jnp.float32)
    g_sel = jnp.argmax(g_logits, axis=-1)
    p_group = jnp.take_along_axis(jax.nn.softmax(g_logits, axis=-1), g_sel[:, None], axis=-1)
    e_logits = ((tok @ w_expert).astype(jnp.float32) + b_expert.astype(jnp.float32)).reshape(m, N_GROUPS, EXPERTS_PER_GROUP)
    e_logits = jnp.take_along_axis(e_logits, g_sel[:, None, None], axis=1)[:, 0]
    top_v, top_i = lax.top_k(e_logits, TOP_K)
    wts = p_group * jax.nn.softmax(top_v, axis=-1)
    flat_e = (g_sel[:, None] * EXPERTS_PER_GROUP + top_i).reshape(-1)
    n_rows = m * TOP_K
    order = jnp.argsort(flat_e)
    sorted_e = flat_e[order]
    tok_idx = order // TOP_K
    wts_sorted = wts.reshape(-1)[order]
    sizes = jnp.bincount(flat_e, length=N_EXPERTS)
    padded = ((sizes + MOE_BLOCK - 1) // MOE_BLOCK) * MOE_BLOCK
    pad_end = jnp.cumsum(padded)
    pad_start = pad_end - padded
    start = jnp.cumsum(sizes) - sizes
    dest = pad_start[sorted_e] + (jnp.arange(n_rows) - start[sorted_e])
    n_blocks = -(-n_rows // MOE_BLOCK) + N_EXPERTS
    cap = n_blocks * MOE_BLOCK
    buf_tok = jnp.full((cap,), m, jnp.int32).at[dest].set(tok_idx.astype(jnp.int32))
    buf_w = jnp.zeros((cap,), tok.dtype).at[dest].set(wts_sorted.astype(tok.dtype))
    block_expert = jnp.clip(jnp.searchsorted(pad_end, jnp.arange(n_blocks) * MOE_BLOCK, side='right'), 0, N_EXPERTS - 1)
    tok_pad = jnp.concatenate([tok, jnp.zeros((1, d), tok.dtype)], axis=0)
    xs = tok_pad[buf_tok].reshape(n_blocks, MOE_BLOCK, d)

    def expert_block(args):
        xb, e = args
        hid = jax.nn.silu(xb @ w1[e]) * (xb @ w3[e])
        return hid @ w2[e]

    ys = lax.map(expert_block, (xs, block_expert)).reshape(cap, d)
    out = jax.ops.segment_sum(ys * buf_w[:, None], buf_tok, num_segments=m + 1)[:m]
    return out.reshape(bsz, t_len, d)

def setup_inputs(seed: int = 0) -> dict:
    key = jax.random.key(seed)
    ks = jax.random.split(key, 32)
    f32 = jnp.float32
    L, D = DEPTH, D_MODEL

    def nrm(k, shape, fan_in, gain=1.0):
        return gain * (fan_in ** -0.5) * jax.random.normal(k, shape, f32)

    def gain_init(k, shape):
        return 1.0 + 0.02 * jax.random.normal(k, shape, f32)

    dt = jnp.exp(jax.random.uniform(ks[8], (L, N_HEADS), f32, float(np.log(1e-3)), float(np.log(1e-1))))
    return {
        "x": jax.random.normal(ks[0], (BATCH, SEQ, D), f32),
        "c": jax.random.normal(ks[1], (BATCH, D), f32),
        "w_ada": nrm(ks[2], (L, D, N_MOD * D), D, 0.5),
        "b_ada": 0.02 * jax.random.normal(ks[3], (L, N_MOD * D), f32),
        "norm1_g": gain_init(ks[4], (L, D)),
        "w_in": nrm(ks[5], (L, D, IN_TOTAL), D),
        "conv_qkv_w": nrm(ks[6], (L, QKV_CONV, 2 * KEY_DIM + VAL_DIM), QKV_CONV),
        "a_log": jnp.log(jax.random.uniform(ks[7], (L, N_HEADS), f32, 1.0, 16.0)),
        "dt_bias": dt + jnp.log(-jnp.expm1(-dt)),
        "onorm_g": gain_init(ks[9], (L, HEAD_DV)),
        "w_proj_a": nrm(ks[10], (L, VAL_DIM, D), VAL_DIM),
        "conv_sc_w": nrm(ks[11], (L, SC_CONV, SC_DIM), SC_CONV),
        "w_proj_b": nrm(ks[12], (L, SC_DIM, D), SC_DIM),
        "w_out": nrm(ks[13], (L, D, D), D),
        "norm2_g": gain_init(ks[14], (L, D)),
        "w_group": nrm(ks[15], (L, D, N_GROUPS), D),
        "b_group": 0.01 * jax.random.normal(ks[16], (L, N_GROUPS), f32),
        "w_expert": nrm(ks[17], (L, D, N_EXPERTS), D),
        "b_expert": 0.01 * jax.random.normal(ks[18], (L, N_EXPERTS), f32),
        "w1": nrm(ks[19], (L, N_EXPERTS, D, D_EXPERT), D),
        "w3": nrm(ks[20], (L, N_EXPERTS, D, D_EXPERT), D),
        "w2": nrm(ks[21], (L, N_EXPERTS, D_EXPERT, D), D_EXPERT),
        "normf_g": gain_init(ks[22], (D,)),
    }

def reference(x, c, w_ada, b_ada, norm1_g, w_in, conv_qkv_w, a_log, dt_bias, onorm_g, w_proj_a,
              conv_sc_w, w_proj_b, w_out, norm2_g, w_group, b_group, w_expert, b_expert, w1, w3, w2, normf_g):
    c_act = jax.nn.silu(c)
    for l in range(DEPTH):
        mod = (c_act @ w_ada[l] + b_ada[l])[:, None, :]
        sh1, sc1, gt1, sh2, sc2, gt2 = jnp.split(mod, N_MOD, axis=-1)
        h = rmsnorm(x, norm1_g[l]) * (1.0 + sc1) + sh1
        x = x + gt1 * hybrid_mixer(h, w_in[l], conv_qkv_w[l], a_log[l], dt_bias[l], onorm_g[l],
                                   w_proj_a[l], conv_sc_w[l], w_proj_b[l], w_out[l])
        h = rmsnorm(x, norm2_g[l]) * (1.0 + sc2) + sh2
        x = x + gt2 * hierarchical_moe(h, w_group[l], b_group[l], w_expert[l], b_expert[l], w1[l], w3[l], w2[l])
    return rmsnorm(x, normf_g)


_drawn_inputs = setup_inputs


def setup_inputs(seed=0):
    import zlib

    import numpy as np

    out = dict(_drawn_inputs(seed))
    spreads = {}
    factors = {'norm1_g': 5.88,
     'onorm_g': 64.0,
     'norm2_g': 27.997,
     'b_group': 64.0,
     'b_expert': 64.0,
     'normf_g': 7.878}
    for name, (base, spread) in spreads.items():
        noise = np.random.default_rng([zlib.crc32(name.encode()), seed]).standard_normal(out[name].shape)
        drawn = base * np.exp(spread * noise) if base else spread * noise
        out[name] = __import__('jax').numpy.asarray(drawn.astype(out[name].dtype))
    for name, factor in factors.items():
        out[name] = (out[name] * factor).astype(out[name].dtype)
    return out
```

```python
from contextlib import ExitStack

import concourse.bass as bass
from concourse import mybir

ALU = mybir.AluOpType
ACT = mybir.ActivationFunctionType
AX = mybir.AxisListType
F32 = mybir.dt.float32
F32R = mybir.dt.float32r
I32 = mybir.dt.int32

P = 128
HALF = 512
N_MOD = 6
TOP_K = 2
HUGE = 3e38
EPS = 1e-6


def weight_stream():
    phases = {"conv": (8, (0, 1, 2)), "gate_b": (8, (0, 1)), "head": (8, (0, 1, 2, 0, 1)), "merge": (4, (0, 1))}
    stream, base, arrivals = {}, 0, [0, 0, 0]
    for name, (iters, slots) in phases.items():
        per, tiles = len(slots), []
        for p, slot in enumerate(slots):
            back = next(d for d in range(1, per + 1) if slots[(p - d) % per] == slot)
            tiles.append(dict(slot=slot, back=back, first_arrival=arrivals[slot] + slots[:p].count(slot) + 1,
                              arrivals_per=slots.count(slot)))
        stream[name] = dict(base=base, per=per, tiles=tiles)
        base += iters * per
        for slot in slots:
            arrivals[slot] += iters
    return stream


def decoder_block(nc, x, c, w_ada, b_ada, norm1_g, w_in, conv_qkv_w, a_log, dt_bias, onorm_g, w_proj_a,
                  conv_sc_w, w_proj_b, w_out, norm2_g, w_group, b_group, w_expert, b_expert, w1, w3, w2,
                  normf_g, out):
    _, T, D = x.shape
    KD = D // P
    TT = T // P
    H = a_log.shape[1]
    QKV_TAPS = conv_qkv_w.shape[1]
    SC_TAPS = conv_sc_w.shape[1]
    VAL0 = 3 * D
    GATE0 = 4 * D
    SC0 = GATE0 + 2 * H
    NG = w_group.shape[2]
    NE = w_expert.shape[2]
    F = w1.shape[3]
    FT = F // P
    MAX_OVER = TOP_K * T // P - 1
    BLOCKS = NE + MAX_OVER + 2
    SLOTS = 3
    LEVELS = [1, 2, 4, 8, 16, 32, 64]
    stream = weight_stream()

    x_d = x[0]
    w_in_d = w_in[0].rearrange("(k p) n -> p k n", p=P)
    w_a_d = w_proj_a[0].rearrange("(k p) n -> p k n", p=P)
    w_b_d = w_proj_b[0].rearrange("(k p) n -> p k n", p=P)
    w_o_d = w_out[0].rearrange("(k p) n -> p k n", p=P)
    w_ada_d = w_ada[0].rearrange("(k p) n -> p k n", p=P)

    merged_b_d = nc.dram_tensor("merged_b_d", [D, T], F32, kind="Internal").ap()
    gate_a_d = nc.dram_tensor("gate_a_d", [D, T], F32, kind="Internal").ap()
    o_hi_d = nc.dram_tensor("o_hi_d", [D, T], F32, kind="Internal").ap()
    o_lo_d = nc.dram_tensor("o_lo_d", [D, T], F32, kind="Internal").ap()
    m_hi_d = nc.dram_tensor("m_hi_d", [D, T], F32, kind="Internal").ap()
    mod_d = nc.dram_tensor("mod_d", [N_MOD * D // P, P], F32, kind="Internal").ap()
    h2_d = nc.dram_tensor("h2_d", [T, D], F32, kind="Internal").ap()
    token_d = nc.dram_tensor("token_d", [BLOCKS * P, 1], F32, kind="Internal").ap()
    y_d = nc.dram_tensor("y_d", [BLOCKS * P, D], F32, kind="Internal").ap()
    m_lo_d = nc.dram_tensor("m_lo_d", [D, T], F32, kind="Internal").ap()

    SB0, CONST, REGION = 16512, 10400, 65536
    top = [SB0]

    def at(name, shape, dt=F32):
        n = 4
        for s in shape[1:]:
            n *= s
        t = nc.alloc_sbuf_tensor_at(name, shape, dt, offset=top[0])
        top[0] += (n + 31) // 32 * 32
        return t

    ident = at("ident", [P, P])
    ones = at("ones", [P, P])
    incl = at("incl", [P, P])
    later = at("later", [P, P])
    level_mask = at("level_mask", [P, len(LEVELS), P])
    params = at("params", [P, 97])
    conv_w = at("conv_w", [P, QKV_TAPS, 3, H])
    c_act = at("c_act", [P, KD])
    mod = at("mod", [P, N_MOD, KD])
    scale1 = at("scale1", [P, KD])
    eps_col = at("eps_col", [P, 1])
    gates = at("gates", [P, 6, TT, H])
    G_LOG, G_BETA, G_NBETA, G_KBG, G_KDEC, G_LAST = range(6)
    slot_i = at("slot_i", [P, TOP_K, TT], I32)
    wts = at("wts", [P, TOP_K, TT])
    ids = at("ids", [P, BLOCKS], I32)
    ids_now = at("ids_now", [P, 2, 2], I32)
    over = at("over", [P, 2 + MAX_OVER], I32)
    logits = at("logits", [P, TT, NG + NE])
    mod_rows = at("mod_rows", [N_MOD * KD, P])
    assert top[0] <= SB0 + CONST
    top[0] = SB0 + CONST
    h_hi = at("h_hi", [P, KD, T], F32R)
    h_lo = at("h_lo", [P, KD, T], F32R)
    R1 = top[0]
    R2 = R1 + REGION
    END = 229376
    top[0] = R1
    s_hi = at("s_hi", [P, KD, T], F32R)
    s_lo = at("s_lo", [P, KD, T], F32R)
    top[0] = R2
    w_raw = at("w_raw", [P, SLOTS, KD, P])
    w_hi = at("w_hi", [P, SLOTS, KD, P], F32R)
    w_lo = at("w_lo", [P, SLOTS, KD, P], F32R)
    SCRATCH = top[0]
    sc_sb = at("sc_sb", [P, T])
    prod = at("prod", [P, T + SC_TAPS - 1])
    sc_acc = at("sc_acc", [P, T])
    sc_y = at("sc_y", [P, T])
    ada_b = at("ada_b", [P, KD, 4 * P])
    assert top[0] <= END
    top[0] = R1
    ada = at("ada", [P, 2, KD, 4 * P])
    x_t = at("x_t", [P, 2, D])
    x_n = at("x_n", [P, 2, D])
    x_sq = at("x_sq", [P, D])
    ssq = at("ssq", [P, 3, TT])
    h_tmp = at("h_tmp", [P, KD, P])
    assert top[0] <= R2
    top[0] = SCRATCH
    rows_a = at("rows_a", [97, P])
    rows_b = at("rows_b", [96, P])
    w_gate = at("w_gate", [P, KD, 2 * H])
    w_gate_hi = at("w_gate_hi", [P, KD, 2 * H], F32R)
    w_gate_lo = at("w_gate_lo", [P, KD, 2 * H], F32R)
    dt_row = at("dt_row", [P, 2, H])
    graw = at("graw", [P, 2, TT, H])
    gtmp = at("gtmp", [P, 3, TT, H])

    top[0] = R1
    QPAD = QKV_TAPS - 1
    conv_in = at("conv_in", [P, 2, T + QPAD])
    qk = at("qk", [P, 2, T])
    vv = at("vv", [P, T])
    X = at("X", [P, TT, P])
    Y = at("Y", [P, TT, P])
    LX = at("LX", [P, TT, P])
    decay = at("decay", [P, TT, P])
    grow = at("grow", [P, TT, P])
    q_dec = at("q_dec", [P, TT, P])
    kk_decay = at("kk_decay", [P, TT, P])
    intra = at("intra", [P, TT, P])
    k_bg = at("k_bg", [P, TT, P])
    k_dec = at("k_dec", [P, TT, P])
    S = at("S", [P, P])
    v_new = at("v_new", [P, 2, P])
    hgate = at("hgate", [P, 6, TT])
    hconv = at("hconv", [P, QKV_TAPS, 3])
    assert top[0] <= R2
    top[0] = SCRATCH
    v_beta = at("v_beta", [P, TT, P])
    w_neg = at("w_neg", [P, TT, P])
    o_raw = at("o_raw", [P, T])
    z_act = at("z_act", [P, T])
    gate_a = at("gate_a", [P, T])
    norm = at("norm", [P, T])
    o_hi = at("o_hi", [P, T], F32R)
    o_lo = at("o_lo", [P, T], F32R)
    assert top[0] <= END
    top[0] = SCRATCH
    ga_in = at("ga_in", [P, 2, T])
    mb_in = at("mb_in", [P, 2, T])
    m_hi = at("m_hi", [P, 2, T], F32R)
    m_lo = at("m_lo", [P, 2, T], F32R)
    assert top[0] <= END
    top[0] = SB0 + CONST
    wo_hi = at("wo_hi", [P, KD, D], F32R)
    wo_lo = at("wo_lo", [P, KD, D], F32R)
    top[0] = R1
    x1 = at("x1", [P, TT, D])
    R1B = top[0]
    gt1_row = at("gt1_row", [P, D])
    g2_row = at("g2_row", [P, D])
    sh2_row = at("sh2_row", [P, D])
    w_route = at("w_route", [P, KD, NG + NE])
    b_route = at("b_route", [P, NG + NE])
    stat2 = at("stat2", [P, 3, TT])
    h2 = at("h2", [P, 2, D])
    assert top[0] <= R2
    top[0] = R2
    mt_hi = at("mt_hi", [P, 2, KD, P], F32R)
    mt_lo = at("mt_lo", [P, 2, KD, P], F32R)
    xr = at("xr", [P, 2, D])
    sq2 = at("sq2", [P, D])
    h2T = at("h2T", [P, 2, KD, P])
    R_E = [P, TT, NE]
    g_cand = at("g_cand", [P, TT, NG])
    g_exp = at("g_exp", [P, TT, NG])
    g_one = at("g_one", [P, TT, NG])
    e_log = at("e_log", R_E)
    e_cand = at("e_cand", R_E)
    e_one = [at(f"e_one{k}", R_E) for k in range(TOP_K)]
    e_both = at("e_both", R_E)
    e_tmp = at("e_tmp", R_E)
    iota_g = at("iota_g", [P, NG])
    iota_e = at("iota_e", [P, NE])
    iota_b = at("iota_b", [P, MAX_OVER + 1])
    mults = at("mults", [P, MAX_OVER])
    over_tmp = at("over_tmp", [P, NE, MAX_OVER])
    over_cum = at("over_cum", [P, 2, NE])
    over_f = at("over_f", [P, 2 + MAX_OVER])
    r_small = at("r_small", [P, 16, TT])
    token_f = at("token_f", [P, TT])
    zeros = at("zeros", [P, P])
    id_rows = at("id_rows", [BLOCKS, P])
    assert top[0] <= END
    top[0] = SB0 + CONST
    ew = [None, None]
    ew[0] = [at("e0_w1", [P, KD, F]), at("e0_w3", [P, KD, F]), at("e0_w2", [P, FT, D])]
    y_sb = at("y_sb", [P, 2, D])
    hidT = at("hidT", [P, FT, P])
    hid = at("hid", [P, F])
    gate_act = at("gate_act", [P, F])
    assert top[0] <= R1
    top[0] = R1B
    xg = at("xg", [P, 2, D])
    xT = at("xT", [P, 2, KD, P])
    assert top[0] <= R2
    top[0] = R2
    ew[1] = [at("e1_w1", [P, KD, F]), at("e1_w3", [P, KD, F]), at("e1_w2", [P, FT, D])]
    E_END = top[0]
    assert top[0] <= END
    top[0] = SB0 + CONST
    y_g = at("y_g", [P, TOP_K, 2, D])
    y_acc = at("y_acc", [P, 2, D])
    y_sq = at("y_sq", [P, D])
    res = at("res", [P, 2, D])
    gt2_row = at("gt2_row", [P, D])
    nf_row = at("nf_row", [P, D])
    stat3 = at("stat3", [P, 3, TT])
    assert top[0] <= R1

    ctx = ExitStack()
    with ctx:
        def sem(name):
            return ctx.enter_context(nc.semaphore(name))

        ps = ctx.enter_context(nc.psum_tensor("ps", [P, 8, HALF], F32))

        waits_passed = sem("waits_passed")
        params_in = sem("params_in")
        masks_done = sem("masks_done")
        pool_step = sem("pool_step")
        rows_turned = sem("rows_turned")
        cols_ready = sem("cols_ready")
        ada_in = [sem(f"ada_in{s}") for s in range(3)]
        ada_used = sem("ada_used")
        mod_ready = sem("mod_ready")
        x_in = [sem(f"x_in{s}") for s in range(2)]
        x_squared = sem("x_squared")
        x_root = sem("x_root")
        x_mean = sem("x_mean")
        x_normed = sem("x_normed")
        x_turned = sem("x_turned")
        h_summed = sem("h_summed")
        h_hi_done = sem("h_hi_done")
        h_lo_done = sem("h_lo_done")
        gate_w_in = sem("gate_w_in")
        gate_w_split = sem("gate_w_split")
        gate_logits = sem("gate_logits")
        gate_raw = sem("gate_raw")
        gate_exp = sem("gate_exp")
        gate_step = sem("gate_step")
        gate_sums = sem("gate_sums")
        gates_done = sem("gates_done")
        w_in_sem = [sem(f"w_arrived{s}") for s in range(SLOTS)]
        w_hi_done = sem("w_hi_done")
        w_lo_done = sem("w_lo_done")
        proj_done = sem("proj_done")
        sc_copied = sem("sc_copied")
        prod_done = sem("prod_done")
        conv_step = sem("conv_step")
        sc_y_done = sem("sc_y_done")
        s_hi_done = sem("s_hi_done")
        s_lo_done = sem("s_lo_done")
        gb_sig = sem("gb_sig")
        mb_done = sem("mb_done")
        mb_out = sem("mb_out")
        bank_free = sem("bank_free")
        hgate_done = sem("hgate_done")
        pool_rows = sem("pool_rows")
        xy_init = sem("xy_init")
        decay_mm = sem("decay_mm")
        decay_exp = sem("decay_exp")
        hconv_step = sem("hconv_step")
        silu_done = sem("silu_done")
        squared = sem("squared")
        norm_mm = sem("norm_mm")
        root_done = sem("root_done")
        inv_root = sem("inv_root")
        qk_normed = sem("qk_normed")
        decay_masked = sem("decay_masked")
        q_dec_done = sem("q_dec_done")
        kt_mm = sem("kt_mm")
        vt_mm = sem("vt_mm")
        k_bg_done = sem("k_bg_done")
        k_dec_done = sem("k_dec_done")
        v_beta_done = sem("v_beta_done")
        kk_mm = sem("kk_mm")
        kk_done = sem("kk_done")
        lx_mm = sem("lx_mm")
        lx_done = sem("lx_done")
        xl_mm = sem("xl_mm")
        yl_mm = sem("yl_mm")
        x_upd = sem("x_upd")
        y_upd = sem("y_upd")
        w_mm = sem("w_mm")
        w_neg_done = sem("w_neg_done")
        s_ready = sem("s_ready")
        vn_mm = sem("vn_mm")
        vn_done = sem("vn_done")
        ds_mm = sem("ds_mm")
        o_mm = sem("o_mm")
        o_copied = sem("o_copied")
        o_step = sem("o_step")
        o_hi_done = sem("o_hi_done")
        head_out = sem("head_out")
        o_in = sem("o_in")
        ga_arrived = [sem(f"ga_arrived{n}") for n in range(2)]
        mb_arrived = [sem(f"mb_arrived{n}") for n in range(2)]
        ga_sig = sem("ga_sig")
        m_step = sem("m_step")
        m_hi_done = sem("m_hi_done")
        m_lo_done = sem("m_lo_done")
        m_out = [sem(f"m_out{n}") for n in range(2)]
        mod_turned = sem("mod_turned")
        mod_out = sem("mod_out")
        wo_in = sem("wo_in")
        wo_hi_done = sem("wo_hi_done")
        wo_lo_done = sem("wo_lo_done")
        merge_over = sem("merge_over")
        rows_in = sem("rows_in")
        mt_in = [sem(f"mt_in{n}") for n in range(2)]
        xr_in = [sem(f"xr_in{n}") for n in range(2)]
        out_mm = sem("out_mm")
        x1_scaled = sem("x1_scaled")
        x1_done = sem("x1_done")
        x1_squared = sem("x1_squared")
        x1_mean = sem("x1_mean")
        x1_root = sem("x1_root")
        x1_inv = sem("x1_inv")
        h2_scaled = sem("h2_scaled")
        h2_done = sem("h2_done")
        h2_turned = sem("h2_turned")
        h2T_done = sem("h2T_done")
        h2_out = [sem(f"h2_out{n}") for n in range(2)]
        logits_done = sem("logits_done")
        iotas = sem("iotas")
        r_step = sem("r_step")
        r_exp = sem("r_exp")
        counts_mm = sem("counts_mm")
        slots_ready = sem("slots_ready")
        tokens_out = sem("tokens_out")
        id_rows_in = sem("id_rows_in")
        ids_turned = sem("ids_turned")
        ids_ready = sem("ids_ready")
        ew_in = [[sem(f"ew_in{s_}_{j}") for j in range(3)] for s_ in range(2)]
        ids_now_ready = sem("ids_now_ready")
        xg_in = [sem(f"xg_in{n}") for n in range(2)]
        xT_mm = sem("xT_mm")
        xT_done = sem("xT_done")
        gu_mm = sem("gu_mm")
        gate_silu = sem("gate_silu")
        hid_done = sem("hid_done")
        hT_mm = sem("hT_mm")
        hT_done = sem("hT_done")
        dn_mm = sem("dn_mm")
        y_copied = [sem(f"y_copied{n}") for n in range(2)]
        y_out = [sem(f"y_out{n}") for n in range(2)]
        y_all = sem("y_all")
        pair_ids = sem("pair_ids")
        yg_in = [sem(f"yg_in{n}") for n in range(2)]
        acc_step = sem("acc_step")
        res_done = sem("res_done")
        res_out = [sem(f"res_out{n}") for n in range(2)]

        R_GEXP, R_EEXP, R_BOTH = 7, 21, 22

        block = ctx.enter_context(nc.Block())

        def y_count(b, s):
            return 8 * (b - s)

        def over_blocks(eng, body):
            count = eng.value_load(over[0:1, 0:1], min_val=0, max_val=MAX_OVER)
            with eng.Fori(0, (MAX_OVER + 1) // 2) as i:
                for s in range(2):
                    with eng.If(2 * i + s < count):
                        body(2 * i + s + NE, s, 2 * i + s)
            return count

        def w_index(phase, i, p):
            s = stream[phase]
            return s["base"] + s["per"] * i + p

        def group(phase, i, p, half):
            return 2 * (SLOTS + w_index(phase, i, p)) + half + 1

        def slot_of(phase, p):
            return stream[phase]["tiles"][p % stream[phase]["per"]]["slot"]

        def load_w(eng, phase, i, p, src, col):
            t = stream[phase]["tiles"][p]
            last_split = w_index(phase, i, p) - t["back"] + 1
            col = eng.snap(col) if not isinstance(col, int) else col
            last_split = eng.snap(SLOTS + last_split) if not isinstance(last_split, int) else SLOTS + last_split
            eng.wait_ge(w_hi_done, last_split)
            eng.wait_ge(w_lo_done, last_split)
            eng.sem_inc(waits_passed, 1)
            eng.dma_start(w_raw[:, t["slot"]], src[:, :, bass.ds(col, P)]).then_inc(w_in_sem[t["slot"]], 16)

        def wait_raw(eng, phase, i, p):
            t = stream[phase]["tiles"][p]
            eng.wait_ge(w_in_sem[t["slot"]], 16 * (t["first_arrival"] + t["arrivals_per"] * i))

        def split_w_hi(act, phase, i, p):
            t = stream[phase]["tiles"][p]
            wait_raw(act, phase, i, p)
            act.wait_ge(proj_done, 2 * (SLOTS + w_index(phase, i, p) - t["back"] + 1))
            act.activation(w_hi[:, t["slot"]], w_raw[:, t["slot"]], ACT.Copy).then_inc(w_hi_done, 1)

        def split_w_lo(dve, phase, i, p):
            t = stream[phase]["tiles"][p]
            dve.wait_ge(w_hi_done, SLOTS + w_index(phase, i, p) + 1)
            dve.tensor_tensor(w_lo[:, t["slot"]], w_raw[:, t["slot"]], w_hi[:, t["slot"]],
                              ALU.subtract).then_inc(w_lo_done, 1)

        def next_tile(phase, i, p):
            return (phase, i, p + 1) if p + 1 < stream[phase]["per"] else (phase, i + 1, 0)

        def wait_w(pe, phase, i, p):
            pe.wait_ge(w_hi_done, SLOTS + w_index(phase, i, p) + 1)
            pe.wait_ge(w_lo_done, SLOTS + w_index(phase, i, p) + 1)

        def project(pe, dst, phase, p, hi, lo, half, ks=None, parts=range(3)):
            s = slot_of(phase, p)
            last = None
            ks = range(KD) if ks is None else ks
            cols = slice(half * HALF, (half + 1) * HALF)
            for k in ks:
                for part in range(3):
                    lhs = w_lo if part == 0 else w_hi
                    rhs = lo if part == 1 else hi
                    last = pe.matmul(dst, lhs[:, s, k], rhs[:, k, cols], start=(k == 0 and part == 0),
                                     stop=(k == KD - 1 and part == 2))
            return last

        @block.gpsimd
        def _(pool):
            pool.memset(ident[:], 0.0).then_inc(pool_step, 1)
            pool.memset(ones[:], 1.0).then_inc(pool_step, 1)
            pool.memset(eps_col[:], EPS).then_inc(pool_step, 1)
            pool.memset(level_mask[:], 0.0).then_inc(pool_step, 1)
            pool.wait_ge(pool_step, 4)
            pool.affine_select(out=ident[:], in_=ident[:], compare_op=ALU.not_equal, fill=1.0, base=0,
                               pattern=[[-1, P]], channel_multiplier=1)
            pool.affine_select(out=incl[:], in_=ones[:], compare_op=ALU.is_ge, fill=0.0, base=0,
                               pattern=[[1, P]], channel_multiplier=-1)
            pool.affine_select(out=later[:], in_=ones[:], compare_op=ALU.is_gt, fill=0.0, base=0,
                               pattern=[[-1, P]], channel_multiplier=1).then_inc(masks_done, 1)
            for n, b in enumerate(LEVELS):
                even = level_mask[:, n].rearrange("p (m s r) -> p m s r", s=2, r=b)[:, :, 0, :]
                src = ones[:].rearrange("p (m s r) -> p m s r", s=2, r=b)[:, :, 0, :]
                m = P // (2 * b)
                pool.affine_select(out=even, in_=src, compare_op=ALU.is_ge, fill=0.0, base=-b,
                                   pattern=[[-2 * b, m], [0, b]], channel_multiplier=1).then_inc(pool_step, 1)
                pool.wait_ge(pool_step, 5 + n)
                pool.affine_select(out=even, in_=even, compare_op=ALU.is_ge, fill=0.0, base=2 * b - 1,
                                   pattern=[[2 * b, m], [0, b]], channel_multiplier=-1).then_inc(masks_done, 1)

            with pool.Fori(0, H) as h:
                pool.wait_ge(hgate_done, 2 * h + 2)
                logs = hgate[:, G_LOG, :, None].to_broadcast([P, TT, P])
                pool.tensor_tensor(X[:], later[:, None, :].to_broadcast([P, TT, P]), logs, ALU.mult)\
                    .then_inc(pool_rows, 1)
                pool.tensor_tensor(Y[:], ones[:, None, :].to_broadcast([P, TT, P]), logs, ALU.mult)\
                    .then_inc(pool_rows, 1)
                pool.wait_ge(decay_mm, 4 * h + 4)
                eye = ident[:, None, :].to_broadcast([P, TT, P])
                pool.tensor_tensor(X[:], eye, eye, ALU.mult).then_inc(xy_init, 1)
                pool.tensor_tensor(Y[:], eye, eye, ALU.mult).then_inc(xy_init, 1)

            pool.wait_ge(merge_over, 1)
            pool.iota(iota_g[:], pattern=[[1, NG]], base=0, channel_multiplier=0, allow_small_or_imprecise_dtypes=True)
            pool.iota(iota_e[:], pattern=[[1, NE]], base=0, channel_multiplier=0, allow_small_or_imprecise_dtypes=True)
            pool.iota(iota_b[:], pattern=[[1, MAX_OVER + 1]], base=0, channel_multiplier=0,
                      allow_small_or_imprecise_dtypes=True)
            pool.iota(mults[:], pattern=[[P, MAX_OVER]], base=P, channel_multiplier=0,
                      allow_small_or_imprecise_dtypes=True)
            pool.iota(token_f[:], pattern=[[P, TT]], base=0, channel_multiplier=1,
                      allow_small_or_imprecise_dtypes=True)
            pool.memset(zeros[:], 0.0).then_inc(iotas, 1)
            pool.wait_ge(iotas, 1)
            pool.dma_start(token_d.rearrange("(b p) o -> b (p o)", p=P), zeros[0:BLOCKS]).then_inc(tokens_out, 16)
            for b in range(NE, BLOCKS):
                pool.dma_start(y_d[b * P:(b + 1) * P, :].rearrange("p (k c) -> p k c", c=P),
                               zeros[:, None, :].to_broadcast([P, KD, P])).then_inc(tokens_out, 16)
            pool.wait_ge(tokens_out, 16 * (1 + BLOCKS - NE))
            pool.wait_ge(slots_ready, 1)
            for k in range(TOP_K):
                for t in range(TT):
                    pool.indirect_dma_start(token_d, bass.IndirectOffsetOnAxis(slot_i[:, k, t:t + 1], axis=0),
                                            token_f[:, t:t + 1], None, bounds_check=BLOCKS * P - 1)\
                        .then_inc(tokens_out, 16)
            def gather(b, s):
                want = b + 1
                for n in range(2):
                    pool.wait_ge(h2_out[n], 16 * TT // 2)
                pool.wait_ge(ids_now_ready, want)
                pool.sem_inc(waits_passed, 1)
                pool.indirect_dma_start(xg[:, s], None, h2_d, bass.IndirectOffsetOnAxis(ids_now[:, s, 0:1], axis=0),
                                        bounds_check=T - 1).then_inc(xg_in[s], 16)
            gather(0, 0)
            with pool.Fori(0, NE // 2) as i:
                for s in range(2):
                    gather(2 * i + s + 1, 1 - s)
            over_blocks(pool, lambda b, s, j: gather(b + 1, 1 - s))
            with pool.Fori(0, TT // 2) as i:
                for s in range(2):
                    pool.wait_ge(y_all, 1)
                    pool.wait_ge(pair_ids, 2 * i + s + 1)
                    pool.sem_inc(waits_passed, 1)
                    for k in range(TOP_K):
                        pool.indirect_dma_start(y_g[:, k, s], None, y_d,
                                                bass.IndirectOffsetOnAxis(ids_now[:, s, k:k + 1], axis=0),
                                                bounds_check=BLOCKS * P - 1).then_inc(yg_in[s], 16)

        N_MASKS = 1 + len(LEVELS)

        @block.sync
        def _(sp):
            row = 0
            for src in (c[0], norm1_g[0], norm2_g[0], b_ada[0], conv_sc_w[0].rearrange("t n -> (t n)"), onorm_g[0]):
                n = src.shape[0] // P
                sp.dma_start(rows_a[row:row + n, :], src.rearrange("(a b) -> a b", b=P)).then_inc(params_in, 16)
                row += n
            sp.dma_start(rows_b[:], conv_qkv_w[0].rearrange("t (a b) -> (t a) b", b=P)).then_inc(params_in, 16)
            sp.dma_start(dt_row[:, 0], a_log[0:1, :].to_broadcast([P, H])).then_inc(params_in, 16)
            sp.dma_start(dt_row[:, 1], dt_bias[0:1, :].to_broadcast([P, H])).then_inc(params_in, 16)
            for n in range(2):
                sp.dma_start(ada[:, n], w_ada_d[:, :, n * 4 * P:(n + 1) * 4 * P]).then_inc(ada_in[n], 16)
            sp.dma_start(w_gate[:], w_in_d[:, :, GATE0:SC0]).then_inc(gate_w_in, 16)
            for n in range(2):
                sp.dma_start(x_t[:, n], x_d[n * P:(n + 1) * P, :]).then_inc(x_in[n], 16)
            for n in range(2, 4):
                sp.wait_ge(ada_used, n - 1)
                sp.dma_start(ada[:, n - 2], w_ada_d[:, :, n * 4 * P:(n + 1) * 4 * P]).then_inc(ada_in[n - 2], 16)
            with sp.Fori(1, TT // 2) as i:
                for s in range(2):
                    row = sp.snap((2 * i + s) * P)
                    sp.wait_ge(x_normed, 2 * i + s - 1)
                    sp.dma_start(x_t[:, s], x_d[bass.ds(row, P), :]).then_inc(x_in[s], 16)
            with sp.Fori(0, KD) as i:
                for p, col in enumerate((SC0 + D, SC0 + 2 * D, SC0)):
                    load_w(sp, "conv", i, p, w_in_d, i * P + col)
                ada_col = sp.snap((4 + i) * 4 * P)
                sp.wait_ge(ada_used, 4 + i)
                sp.wait_ge(gates_done, 1)
                sp.dma_start(ada_b[:], w_ada_d[:, :, bass.ds(ada_col, 4 * P)]).then_inc(ada_in[2], 16)
            with sp.Fori(0, KD) as i:
                load_w(sp, "gate_b", i, 0, w_in_d, i * P + SC0 + 4 * D)
                load_w(sp, "gate_b", i, 1, w_b_d, i * P)
            with sp.Fori(0, H) as h:
                for p, col in enumerate((0, D, 2 * D, VAL0, SC0 + 3 * D)):
                    load_w(sp, "head", h, p, w_in_d, h * P + col)
            for p in range(2):
                load_w(sp, "merge", 0, p, w_a_d, p * P)
            sp.wait_ge(head_out, 48 * H)
            sp.dma_start(s_hi[:].bitcast(F32), o_hi_d.rearrange("(k p) t -> p k t", p=P)).then_inc(o_in, 16)
            sp.dma_start(s_lo[:].bitcast(F32), o_lo_d.rearrange("(k p) t -> p k t", p=P)).then_inc(o_in, 16)

            def load_merge(i, p):
                row, free, lo_free = (2 * i + p) * P, 2 * i + p + 1, 2 * i + p
                if not isinstance(i, int):
                    row, free, lo_free = sp.snap(row), sp.snap(free), sp.snap(lo_free)
                sp.wait_ge(m_lo_done, free)
                sp.dma_start(ga_in[:, p], gate_a_d[bass.ds(row, P), :]).then_inc(ga_arrived[p], 16)
                sp.dma_start(mb_in[:, p], merged_b_d[bass.ds(row, P), :]).then_inc(mb_arrived[p], 16)
                sp.wait_ge(wo_lo_done, lo_free)
                sp.sem_inc(waits_passed, 1)
                sp.dma_start(w_raw[:, 2], w_o_d[:, :, bass.ds(row, P)]).then_inc(wo_in, 16)

            with sp.Fori(0, KD // 2 - 1) as i:
                for p in range(2):
                    load_merge(i, p)
                    load_w(sp, "merge", i + 1, p, w_a_d, (2 * i + 2 + p) * P)
            for p in range(2):
                load_merge(KD // 2 - 1, p)
            for n in range(2):
                sp.wait_ge(m_out[n], 32 * KD // 2)
            sp.wait_ge(proj_done, group("merge", KD // 2 - 1, 1, 1))
            sp.wait_ge(wo_lo_done, KD)
            sp.wait_ge(m_lo_done, 2 + KD)
            sp.wait_ge(mod_out, 16)
            sp.sem_inc(merge_over, 1)
            def mod_row(kind):
                return mod_d[kind * KD:(kind + 1) * KD, :].rearrange("(o k) p -> o (k p)", o=1).to_broadcast([P, D])
            for dst, src in ((gt1_row[:], mod_row(2)), (g2_row[:], mod_row(4)), (sh2_row[:], mod_row(3)),
                             (w_route[:, :, 0:NG], w_group[0].rearrange("(k p) n -> p k n", p=P)),
                             (w_route[:, :, NG:], w_expert[0].rearrange("(k p) n -> p k n", p=P)),
                             (b_route[:, 0:NG], b_group[0:1, :].to_broadcast([P, NG])),
                             (b_route[:, NG:], b_expert[0:1, :].to_broadcast([P, NE]))):
                sp.dma_start(dst, src).then_inc(rows_in, 16)
            with sp.Fori(0, TT // 2) as i:
                for s in range(2):
                    row, used = sp.snap((2 * i + s) * P), sp.snap(2 * (2 * i + s))
                    sp.wait_ge(out_mm, used)
                    sp.dma_start(mt_hi[:, s].bitcast(F32), m_hi_d.rearrange("(k p) t -> p k t", p=P)
                                 [:, :, bass.ds(row, P)]).then_inc(mt_in[s], 16)
                    sp.dma_start(mt_lo[:, s].bitcast(F32), m_lo_d.rearrange("(k p) t -> p k t", p=P)
                                 [:, :, bass.ds(row, P)]).then_inc(mt_in[s], 16)
                    sp.wait_ge(x1_done, used)
                    sp.dma_start(xr[:, s], x_d[bass.ds(row, P), :]).then_inc(xr_in[s], 16)
            def load_expert(e, b, s):
                gu, dn = (4 * b, 2 * b) if isinstance(b, int) else (sp.snap(4 * b), sp.snap(2 * b))
                if not isinstance(e, int):
                    e = sp.snap(e)
                sp.wait_ge(gu_mm, gu)
                for j, w in enumerate((w1, w3)):
                    sp.dma_start(ew[s][j][:], w[0, bass.ds(e, 1)].rearrange("o (k p) f -> p (o k) f", p=P))\
                        .then_inc(ew_in[s][j], 16)
                sp.wait_ge(dn_mm, dn)
                sp.dma_start(ew[s][2][:], w2[0, bass.ds(e, 1)].rearrange("o (k p) f -> p (o k) f", p=P))\
                    .then_inc(ew_in[s][2], 16)
            sp.wait_ge(out_mm, 2 + 2 * TT)
            load_expert(0, 0, 0)
            sp.wait_ge(tokens_out, 16 * (1 + BLOCKS - NE + TOP_K * TT))
            sp.dma_start(id_rows[:], token_d.rearrange("(b p) o -> b (p o)", p=P)).then_inc(id_rows_in, 16)
            sp.wait_ge(ids_ready, 2)
            load_expert(1, 1, 1)
            with sp.Fori(1, NE // 2) as i:
                for s in range(2):
                    load_expert(2 * i + s, 2 * i + s, s)
            over_blocks(sp, lambda b, s, j: load_expert(
                sp.value_load(over[0:1, bass.ds(j + 1, 1)], min_val=0, max_val=NE - 1), b, s))
            sp.wait_ge(y_all, 1)
            sp.dma_start(gt2_row[:], mod_row(5)).then_inc(rows_in, 16)
            sp.dma_start(nf_row[:], normf_g.rearrange("(o n) -> o n", o=1).to_broadcast([P, D])).then_inc(rows_in, 16)
            with sp.Fori(0, TT // 2) as i:
                for s in range(2):
                    row, want = sp.snap((2 * i + s) * P), sp.snap(2 * i + s + 1)
                    sp.wait_ge(res_done, want)
                    sp.dma_start(out[0, bass.ds(row, P), :], res[:, s]).then_inc(res_out[s], 16)
            for s in range(2):
                sp.wait_ge(res_out[s], 16 * TT // 2)

        @block.scalar
        def _(act):
            act.wait_ge(rows_turned, 1)
            act.activation(params[:], ps[:, 0, 0:97], ACT.Copy).then_inc(cols_ready, 1)
            act.activation(conv_w[:].rearrange("p t k h -> p (t k h)"), ps[:, 1, 0:96], ACT.Copy)\
               .then_inc(cols_ready, 1)
            act.activation(c_act[:], ps[:, 0, 0:KD], ACT.Silu).then_inc(cols_ready, 1)
            act.wait_ge(gate_w_in, 16)
            act.activation(w_gate_hi[:], w_gate[:], ACT.Copy).then_inc(gate_w_split, 1)
            with act.Fori(0, TT // 2) as i:
                for s in range(2):
                    act.wait_ge(x_in[s], 16 * i + 16)
                    act.activation(x_sq[:], x_t[:, s], ACT.Square,
                                   accum_out=ssq[:, 0, bass.ds(2 * i + s, 1)]).then_inc(x_squared, 1)
                    act.wait_ge(x_mean, 2 * i + s + 1)
                    act.activation(ssq[:, 1, bass.ds(2 * i + s, 1)], ssq[:, 2, bass.ds(2 * i + s, 1)],
                                   ACT.Sqrt).then_inc(x_root, 1)
                    act.wait_ge(h_summed, 8 * (2 * i + s) + 8)
                    act.activation(h_hi[:, :, bass.ds((2 * i + s) * P, P)], h_tmp[:], ACT.Copy)\
                       .then_inc(h_hi_done, 1)
            split_w_hi(act, "conv", 0, 0)
            act.wait_ge(gate_raw, 2)
            act.activation(gtmp[:, 0], graw[:, 0], ACT.Exp, scale=-1.0).then_inc(gate_exp, 1)
            act.activation(dt_row[:, 0], dt_row[:, 0], ACT.Exp).then_inc(gate_exp, 1)
            act.wait_ge(gate_step, 1)
            act.activation(gtmp[:, 2], gtmp[:, 1], ACT.Exp, scale=-1.0).then_inc(gate_exp, 1)
            act.wait_ge(gate_exp, 3)
            act.activation(gtmp[:, 2], gtmp[:, 2], ACT.Ln, bias=1.0).then_inc(gate_exp, 1)
            act.wait_ge(gate_sums, 1)
            for n, kind in enumerate((G_KBG, G_KDEC, G_LAST)):
                act.activation(gates[:, kind].rearrange("p t h -> p (t h)"),
                               ps[:, 3, n * TT * H:(n + 1) * TT * H], ACT.Exp).then_inc(gate_exp, 1)
            with act.Fori(0, KD) as i:
                split_w_hi(act, "conv", i, 1)
                act.wait_ge(prod_done, 2 * i)
                for n in range(2):
                    act.wait_ge(proj_done, group("conv", i, 0, n))
                    act.activation(sc_sb[:, n * HALF:(n + 1) * HALF], ps[:, n], ACT.Copy).then_inc(sc_copied, 1)
                split_w_hi(act, "conv", i, 2)
                split_w_hi(act, *next_tile("conv", i, 2))
                act.wait_ge(sc_y_done, 2 * i + 2)
                act.activation(s_hi[:, bass.ds(i, 1)].rearrange("p a t -> p (a t)"), sc_y[:], ACT.Copy)\
                   .then_inc(s_hi_done, 1)
            act.wait_ge(mod_turned, 1)
            act.activation(mod_rows[:], ps[0:N_MOD * KD, 7, 0:P], ACT.Copy).then_inc(cols_ready, 1)
            act.wait_ge(cols_ready, 4)
            act.dma_start(mod_d, mod_rows[:]).then_inc(mod_out, 16)
            with act.Fori(0, KD) as i:
                split_w_hi(act, "gate_b", i, 1)
                act.wait_ge(mb_done, 2 * i)
                for n in range(2):
                    act.wait_ge(proj_done, group("gate_b", i, 0, n))
                    act.activation(sc_sb[:, n * HALF:(n + 1) * HALF], ps[:, n], ACT.Sigmoid).then_inc(gb_sig, 1)
                split_w_hi(act, *next_tile("gate_b", i, 1))
                act.wait_ge(mb_done, 2 * i + 2)
                act.dma_start(merged_b_d[bass.ds(i * P, P), :], sc_y[:]).then_inc(mb_out, 16)
            act.wait_ge(mb_out, 16 * KD)
            with act.Fori(0, H) as h:
                def evac(p, half, dst, func):
                    act.wait_ge(proj_done, group("head", h, p, half))
                    act.activation(dst, ps[:, half], func).then_inc(bank_free, 1)

                def evac_conv(p, slot):
                    for half in range(2):
                        evac(p, half, conv_in[:, slot, QPAD + half * HALF:QPAD + (half + 1) * HALF], ACT.Copy)

                def root(n, banks):
                    for half in range(2):
                        act.wait_ge(norm_mm, 6 * h + 2 * n + half + 1)
                        act.activation(norm[:, half * HALF:(half + 1) * HALF], ps[:, banks + half], ACT.Sqrt,
                                       bias=eps_col[:], scale=(1.0 / P if n == 2 else 1.0)).then_inc(root_done, 1)

                split_w_hi(act, "head", h, 1)
                evac_conv(0, 0)
                act.wait_ge(q_dec_done, h)
                for n in range(4):
                    act.wait_ge(decay_mm, 4 * h + n + 1)
                    act.activation((decay, grow)[n // 2][:, (n % 2) * 4:(n % 2) * 4 + 4].rearrange("p t i -> p (t i)"),
                                   ps[:, 4 + n], ACT.Exp).then_inc(decay_exp, 1)
                split_w_hi(act, "head", h, 2)
                evac_conv(1, 1)
                act.wait_ge(hconv_step, 12 * h + 4)
                act.activation(qk[:, 0], qk[:, 0], ACT.Silu).then_inc(silu_done, 1)
                act.wait_ge(silu_done, 3 * h + 1)
                lx_flat = LX[:].rearrange("p t i -> p (t i)")
                act.activation(lx_flat, qk[:, 0], ACT.Square).then_inc(squared, 1)
                split_w_hi(act, "head", h, 3)
                evac_conv(2, 0)
                act.wait_ge(hconv_step, 12 * h + 8)
                act.activation(qk[:, 1], qk[:, 1], ACT.Silu).then_inc(silu_done, 1)
                root(0, 4)
                act.wait_ge(silu_done, 3 * h + 2)
                act.activation(lx_flat, qk[:, 1], ACT.Square).then_inc(squared, 1)
                split_w_hi(act, "head", h, 4)
                act.wait_ge(qk_normed, 2 * h + 1)
                root(1, 6)
                act.wait_ge(hconv_step, 12 * h + 12)
                act.activation(vv[:], vv[:], ACT.Silu).then_inc(silu_done, 1)
                for t in range(TT):
                    if t % 4 == 0:
                        act.wait_ge(kt_mm, 2 * h + t // 4 + 1)
                    if t == 4:
                        act.wait_ge(k_dec_done, TT * h + 4)
                    act.activation(k_bg[:, t], ps[:, 4 + t // 4, (t % 4) * P:(t % 4 + 1) * P], ACT.Copy,
                                   scale=hgate[:, G_KBG, t:t + 1]).then_inc(k_bg_done, 1)
                for t in range(TT):
                    if t % 4 == 0:
                        act.wait_ge(vt_mm, 2 * h + t // 4 + 1)
                    act.activation(v_beta[:, t], ps[:, 4 + t // 4, (t % 4) * P:(t % 4 + 1) * P], ACT.Copy,
                                   scale=hgate[:, G_BETA, t:t + 1]).then_inc(v_beta_done, 1)
                for n in range(2):
                    act.wait_ge(w_mm, 2 * h + n + 1)
                    act.activation(w_neg[:, 4 * n:4 * n + 4].rearrange("p t i -> p (t i)"), ps[:, 6 + n], ACT.Copy,
                                   scale=-1.0).then_inc(w_neg_done, 1)
                act.wait_ge(head_out, 48 * h)
                for t in range(TT):
                    act.wait_ge(vn_mm, TT * h + t + 1)
                    act.activation(v_new[:, t % 2], ps[:, 2, 0:P], ACT.Copy).then_inc(vn_done, 1)
                    act.wait_ge(o_mm, TT * h + t + 1)
                    act.activation(o_raw[:, t * P:(t + 1) * P], ps[:, 3 + t % 2, 0:P], ACT.Copy)\
                       .then_inc(o_copied, 1)
                    if t in (1, 3):
                        evac(3, t // 2, z_act[:, (t // 2) * HALF:(t // 2 + 1) * HALF], ACT.Silu)
                    if t == 5:
                        evac(4, 0, gate_a[:, 0:HALF], ACT.Copy)
                        split_w_hi(act, *next_tile("head", h, 4))
                evac(4, 1, gate_a[:, HALF:T], ACT.Copy)
                act.wait_ge(o_copied, TT * h + TT)
                act.activation(lx_flat, o_raw[:], ACT.Square).then_inc(squared, 1)
                act.wait_ge(bank_free, 2 + 10 * h + 10)
                act.dma_start(gate_a_d[bass.ds(h * P, P), :], gate_a[:]).then_inc(head_out, 16)
                root(2, 4)
                act.wait_ge(o_step, 2 * h + 2)
                act.activation(o_hi[:], o_raw[:], ACT.Copy).then_inc(o_hi_done, 1)
                act.wait_ge(o_hi_done, 2 * h + 1)
                act.dma_start(o_hi_d[bass.ds(h * P, P), :], o_hi[:].bitcast(F32)).then_inc(head_out, 16)
                act.wait_ge(o_hi_done, 2 * h + 2)
                act.dma_start(o_lo_d[bass.ds(h * P, P), :], o_lo[:].bitcast(F32)).then_inc(head_out, 16)

            def merge_hi(i, last):
                for p in range(2):
                    if p == 0 or not last:
                        split_w_hi(act, *next_tile("merge", i, p))
                    act.wait_ge(ga_arrived[p], 16 * i + 16)
                    act.activation(ga_in[:, p], ga_in[:, p], ACT.Sigmoid).then_inc(ga_sig, 1)
                    act.wait_ge(wo_in, 16 * (2 * i + p) + 16)
                    act.activation(wo_hi[:, :, bass.ds((2 * i + p) * P, P)], w_raw[:, 2], ACT.Copy)\
                       .then_inc(wo_hi_done, 1)
                    act.wait_ge(m_step, 3 * (2 * i + p) + 3)
                    act.wait_ge(m_out[p], 32 * i)
                    act.activation(m_hi[:, p], ga_in[:, p], ACT.Copy).then_inc(m_hi_done, 1)
                    act.wait_ge(m_hi_done, 2 * i + p + 1)
                    act.dma_start(m_hi_d[bass.ds((2 * i + p) * P, P), :], m_hi[:, p].bitcast(F32)).then_inc(m_out[p], 16)
                    act.wait_ge(m_lo_done, 2 * i + p + 1 + 2)
                    act.dma_start(m_lo_d[bass.ds((2 * i + p) * P, P), :], m_lo[:, p].bitcast(F32)).then_inc(m_out[p], 16)

            act.wait_ge(proj_done, group("head", H - 1, 4, 1))
            with act.Fori(0, KD // 2 - 1) as i:
                merge_hi(i, False)
            merge_hi(KD // 2 - 1, True)
            act.wait_ge(rows_in, 16 * 7)
            with act.Fori(0, TT // 2) as i:
                for s in range(2):
                    n = 2 * i + s
                    act.wait_ge(x1_done, 2 + 2 * n + 2)
                    act.activation(sq2[:], x1[:, bass.ds(n, 1)].rearrange("p o d -> p (o d)"), ACT.Square,
                                   accum_out=stat2[:, 0, bass.ds(n, 1)]).then_inc(x1_squared, 1)
                    act.wait_ge(x1_mean, n + 1)
                    act.activation(stat2[:, 1, bass.ds(n, 1)], stat2[:, 2, bass.ds(n, 1)], ACT.Sqrt)\
                       .then_inc(x1_root, 1)
                    act.wait_ge(h2_done, n + 1)
                    act.dma_start(h2_d[bass.ds(n * P, P), :], h2[:, s]).then_inc(h2_out[s], 16)
                    act.wait_ge(logits_done, n)
                    for half in range(2):
                        act.wait_ge(h2_turned, 2 + 2 * n + half + 1)
                        act.activation(h2T[:, s, 4 * half:4 * half + 4].rearrange("p k t -> p (k t)"),
                                       ps[:, 4 + half], ACT.Copy).then_inc(h2T_done, 1)
            act.wait_ge(r_step, R_GEXP)
            act.activation(g_exp[:], g_cand[:], ACT.Exp).then_inc(r_exp, 1)
            act.wait_ge(r_step, R_EEXP)
            act.activation(r_small[:, 8], r_small[:, 7], ACT.Exp).then_inc(r_exp, 1)
            act.wait_ge(h2_out[0], 16 * TT // 2)
            act.wait_ge(h2_out[1], 16 * TT // 2)

            def copy_xT(b, s):
                for half in range(2):
                    act.wait_ge(xT_mm, 2 * b + half + 1)
                    act.activation(xT[:, s, 4 * half:4 * half + 4].rearrange("p k t -> p (k t)"), ps[:, half],
                                   ACT.Copy).then_inc(xT_done, 1)

            def block_act(b, s):
                for part in range(2):
                    act.wait_ge(gu_mm, 4 + 4 * b + 2 * part + 1)
                    act.wait_ge(hid_done, 2 * b + part - (1 if part else 0))
                    act.activation(gate_act[:, part * 2 * P:(part + 1) * 2 * P], ps[:, 2 * part, 0:2 * P], ACT.Silu)\
                       .then_inc(gate_silu, 1)
                for part in range(2):
                    act.wait_ge(hT_mm, 2 * b + part + 1)
                    act.activation(hidT[:, 2 * part:2 * part + 2].rearrange("p f t -> p (f t)"),
                                   ps[:, 4 + part, 0:2 * P], ACT.Copy).then_inc(hT_done, 1)
                copy_xT(b + 1, 1 - s)
                act.wait_ge(dn_mm, 2 + 2 * b + 1)
                act.wait_ge(y_out[s], y_count(b, s))
                act.activation(y_sb[:, s, 0:HALF], ps[:, 6], ACT.Copy).then_inc(y_copied[0], 1)
                act.wait_ge(y_copied[0], b + 1)
                act.wait_ge(y_copied[1], b + 1)
                act.dma_start(y_d[bass.ds(b * P, P), :], y_sb[:, s]).then_inc(y_out[s], 16)

            act.wait_ge(ids_ready, 2)
            copy_xT(0, 0)
            with act.Fori(0, NE // 2) as i:
                for s in range(2):
                    block_act(2 * i + s, s)
            count = over_blocks(act, lambda b, s, j: block_act(b, s))
            for s in range(2):
                act.wait_ge(y_out[s], 16 * (NE // 2) + 16 * ((count + 1 - s) // 2))
            act.sem_inc(y_all, 1)
            act.wait_ge(rows_in, 16 * 9)
            with act.Fori(0, TT // 2) as i:
                for s in range(2):
                    n = 2 * i + s
                    act.wait_ge(acc_step, 4 * n + 4)
                    act.activation(y_sq[:], y_acc[:, s], ACT.Square, accum_out=stat3[:, 0, bass.ds(n, 1)])\
                       .then_inc(x1_squared, 1)
                    act.wait_ge(x1_mean, TT + n + 1)
                    act.activation(stat3[:, 1, bass.ds(n, 1)], stat3[:, 2, bass.ds(n, 1)], ACT.Sqrt)\
                       .then_inc(x1_root, 1)

        @block.vector
        def _(dve):
            dve.wait_ge(cols_ready, 2)
            dve.wait_ge(ada_used, 4)
            flat = mod[:].rearrange("p a k -> p (a k)")
            dve.tensor_tensor(flat[:, 0:2 * KD], ps[:, 7, 0:2 * KD], params[:, 3 * KD:5 * KD], ALU.add)\
               .then_inc(mod_ready, 1)
            dve.wait_ge(mod_ready, 1)
            dve.scalar_tensor_tensor(out=scale1[:], in0=mod[:, 1], scalar=1.0, in1=params[:, KD:2 * KD],
                                     op0=ALU.add, op1=ALU.mult).then_inc(mod_ready, 1)
            dve.wait_ge(gate_w_split, 1)
            dve.tensor_tensor(w_gate_lo[:], w_gate[:], w_gate_hi[:], ALU.subtract).then_inc(gate_w_split, 1)
            dve.wait_ge(mod_ready, 2)
            with dve.Fori(0, TT // 2) as i:
                for s in range(2):
                    n = 2 * i + s
                    col = bass.ds(n, 1)
                    dve.wait_ge(x_squared, n + 1)
                    dve.tensor_scalar(ssq[:, 2, col], ssq[:, 0, col], 1.0 / D, EPS, ALU.mult, ALU.add)\
                       .then_inc(x_mean, 1)
                    dve.wait_ge(x_root, n + 1)
                    dve.reciprocal(ssq[:, 2, col], ssq[:, 1, col]).then_inc(conv_step, 1)
                    dve.wait_ge(conv_step, n + 1)
                    dve.wait_ge(x_turned, 4 * i)
                    dve.tensor_scalar(x_n[:, s], x_t[:, s], ssq[:, 2, col], None, ALU.mult).then_inc(x_normed, 1)
                    dve.wait_ge(h_hi_done, n)
                    for k in range(KD):
                        if k % 4 == 0:
                            dve.wait_ge(x_turned, 2 * n + k // 4 + 1)
                        dve.tensor_scalar(h_tmp[:, k], ps[:, 2 * s + k // 4, (k % 4) * P:(k % 4 + 1) * P],
                                          scale1[:, k:k + 1], mod[:, 0, k:k + 1], ALU.mult, ALU.add)\
                           .then_inc(h_summed, 1)
                    dve.wait_ge(h_hi_done, n + 1)
                    dve.wait_ge(h_summed, 8 * n + 8)
                    dve.tensor_tensor(h_lo[:, :, bass.ds(n * P, P)], h_tmp[:],
                                      h_hi[:, :, bass.ds(n * P, P)], ALU.subtract).then_inc(h_lo_done, 1)
            split_w_lo(dve, "conv", 0, 0)
            dve.wait_ge(gate_logits, 1)
            dve.wait_ge(params_in, 16 * 9)
            lg = ps[:, 2, 0:TT * 2 * H].rearrange("p (t z h) -> p z t h", t=TT, z=2)
            dve.tensor_copy(graw[:, 0], lg[:, 0]).then_inc(gate_raw, 1)
            dve.tensor_tensor(graw[:, 1], lg[:, 1],
                              dt_row[:, 1:2].to_broadcast([P, TT, H]), ALU.add).then_inc(gate_raw, 1)
            dve.wait_ge(gate_raw, 2)
            dve.scalar_tensor_tensor(out=gtmp[:, 1], in0=graw[:, 1], scalar=-1.0, in1=graw[:, 1],
                                     op0=ALU.mult, op1=ALU.max).then_inc(gate_step, 1)
            dve.wait_ge(gate_exp, 1)
            dve.tensor_scalar(gtmp[:, 0], gtmp[:, 0], 1.0, None, ALU.add).then_inc(gate_step, 1)
            dve.wait_ge(gate_step, 2)
            dve.reciprocal(gates[:, G_BETA], gtmp[:, 0]).then_inc(gate_step, 1)
            dve.wait_ge(gate_step, 3)
            dve.tensor_scalar(gates[:, G_NBETA], gates[:, G_BETA], -1.0, None, ALU.mult).then_inc(gate_step, 1)
            dve.wait_ge(gate_exp, 4)
            dve.scalar_tensor_tensor(out=gtmp[:, 0], in0=graw[:, 1], scalar=0.0, in1=gtmp[:, 2],
                                     op0=ALU.max, op1=ALU.add).then_inc(gate_step, 1)
            dve.wait_ge(gate_step, 5)
            dve.scalar_tensor_tensor(out=gates[:, G_LOG], in0=gtmp[:, 0], scalar=-1.0,
                                     in1=dt_row[:, 0:1].to_broadcast([P, TT, H]),
                                     op0=ALU.mult, op1=ALU.mult).then_inc(gate_step, 1)
            dve.wait_ge(gate_exp, 5)
            dve.tensor_tensor(gates[:, G_KBG], gates[:, G_KBG], gates[:, G_BETA], ALU.mult).then_inc(gate_step, 1)
            dve.wait_ge(gate_step, 7)
            dve.wait_ge(gate_exp, 7)
            dve.memset(prod[:, 0:SC_TAPS - 1], 0.0).then_inc(gates_done, 1)
            CS = TT
            taps = [params[:, 9 * KD + t * KD:9 * KD + (t + 1) * KD] for t in range(SC_TAPS)]
            with dve.Fori(0, KD) as i:
                split_w_lo(dve, "conv", i, 1)
                split_w_lo(dve, "conv", i, 2)
                for n in range(2):
                    cols = slice(n * HALF, (n + 1) * HALF)
                    dve.wait_ge(sc_copied, 2 * i + n + 1)
                    dve.wait_ge(proj_done, group("conv", i, 1, n))
                    dve.tensor_tensor(prod[:, SC_TAPS - 1 + n * HALF:SC_TAPS - 1 + (n + 1) * HALF], ps[:, 2 + n],
                                      sc_sb[:, cols], ALU.mult).then_inc(prod_done, 1)
                dve.wait_ge(prod_done, 2 * i + 2)
                dve.tensor_scalar(sc_acc[:], prod[:, 0:T], taps[0][:, bass.ds(i, 1)], None, ALU.mult)\
                   .then_inc(conv_step, 1)
                for t in range(1, SC_TAPS):
                    dve.wait_ge(conv_step, CS + SC_TAPS * i + t)
                    dve.scalar_tensor_tensor(out=sc_acc[:], in0=prod[:, t:t + T], scalar=taps[t][:, bass.ds(i, 1)],
                                             in1=sc_acc[:], op0=ALU.mult, op1=ALU.add).then_inc(conv_step, 1)
                split_w_lo(dve, *next_tile("conv", i, 2))
                dve.wait_ge(conv_step, CS + SC_TAPS * i + SC_TAPS)
                dve.wait_ge(s_hi_done, i)
                for n in range(2):
                    cols = slice(n * HALF, (n + 1) * HALF)
                    dve.wait_ge(proj_done, group("conv", i, 2, n))
                    dve.tensor_tensor(sc_y[:, cols], ps[:, 4 + n], sc_acc[:, cols], ALU.mult).then_inc(sc_y_done, 1)
                dve.wait_ge(s_hi_done, i + 1)
                dve.wait_ge(sc_y_done, 2 * i + 2)
                dve.tensor_tensor(s_lo[:, bass.ds(i, 1)].rearrange("p a t -> p (a t)"), sc_y[:],
                                  s_hi[:, bass.ds(i, 1)].rearrange("p a t -> p (a t)"), ALU.subtract)\
                   .then_inc(s_lo_done, 1)
            dve.wait_ge(ada_used, 2 * N_MOD)
            dve.tensor_tensor(flat[:, 2 * KD:], ps[:, 7, 2 * KD:N_MOD * KD], params[:, 5 * KD:9 * KD], ALU.add)\
               .then_inc(mod_ready, 1)
            dve.wait_ge(mod_ready, 3)
            dve.scalar_tensor_tensor(out=mod[:, 4], in0=mod[:, 4], scalar=1.0, in1=params[:, 2 * KD:3 * KD],
                                     op0=ALU.add, op1=ALU.mult).then_inc(mod_ready, 1)
            with dve.Fori(0, KD) as i:
                split_w_lo(dve, "gate_b", i, 1)
                dve.wait_ge(mb_out, 16 * i)
                for n in range(2):
                    cols = slice(n * HALF, (n + 1) * HALF)
                    dve.wait_ge(gb_sig, 2 * i + n + 1)
                    dve.wait_ge(proj_done, group("gate_b", i, 1, n))
                    dve.tensor_tensor(sc_y[:, cols], ps[:, 2 + n], sc_sb[:, cols], ALU.mult).then_inc(mb_done, 1)
                split_w_lo(dve, *next_tile("gate_b", i, 1))
            dve.wait_ge(mb_out, 16 * KD)
            dve.memset(conv_in[:, :, 0:QPAD], 0.0)
            with dve.Fori(0, H) as h:
                one = bass.ds(h, 1)

                def conv(p, slot, dst):
                    dve.wait_ge(bank_free, 2 + 10 * h + 2 * p + 2)
                    for t in range(QKV_TAPS):
                        src = conv_in[:, slot, t:t + T]
                        w = hconv[:, t, p:p + 1]
                        if t == 0:
                            ins = dve.tensor_scalar(dst, src, w, None, ALU.mult)
                        else:
                            dve.wait_ge(hconv_step, 12 * h + 4 * p + t)
                            ins = dve.scalar_tensor_tensor(out=dst, in0=src, scalar=w, in1=dst,
                                                           op0=ALU.mult, op1=ALU.add)
                        ins.then_inc(hconv_step, 1)

                def invert_root(n):
                    dve.wait_ge(root_done, 6 * h + 2 * n + 2)
                    dve.reciprocal(norm[:], norm[:]).then_inc(inv_root, 1)
                    dve.wait_ge(inv_root, 3 * h + n + 1)

                dve.wait_ge(o_copied, TT * h)
                dve.tensor_copy(hgate[:], gates[:, :, :, one].rearrange("p a t h -> p a (t h)")).then_inc(hgate_done, 1)
                dve.tensor_copy(hconv[:], conv_w[:, :, :, one].rearrange("p a t h -> p a (t h)")).then_inc(hgate_done, 1)
                dve.memset(S[:], 0.0).then_inc(s_ready, 1)
                split_w_lo(dve, "head", h, 1)
                dve.wait_ge(hgate_done, 2 * h + 2)
                conv(0, 0, qk[:, 0])
                split_w_lo(dve, "head", h, 2)
                conv(1, 1, qk[:, 1])
                split_w_lo(dve, "head", h, 3)
                dve.wait_ge(decay_exp, 4 * h + 4)
                dve.tensor_tensor(decay[:], decay[:], incl[:, None, :].to_broadcast([P, TT, P]), ALU.mult)\
                   .then_inc(decay_masked, 1)
                invert_root(0)
                dve.wait_ge(silu_done, 3 * h + 1)
                dve.scalar_tensor_tensor(out=qk[:, 0], in0=qk[:, 0], scalar=float(P) ** -0.5, in1=norm[:],
                                         op0=ALU.mult, op1=ALU.mult).then_inc(qk_normed, 1)
                conv(2, 0, vv[:])
                dve.tensor_tensor(q_dec[:].rearrange("p t i -> p (t i)"), qk[:, 0],
                                  grow[:].rearrange("p t i -> p (t i)"), ALU.mult).then_inc(q_dec_done, 1)
                split_w_lo(dve, "head", h, 4)
                invert_root(1)
                dve.tensor_tensor(qk[:, 1], qk[:, 1], norm[:], ALU.mult).then_inc(qk_normed, 1)
                for n, bank in enumerate((6, 2)):
                    dve.wait_ge(kk_mm, 2 * h + n + 1)
                    pair = ps[:, bank:bank + 2].rearrange("p b (t z i) -> p (b t) z i", z=2, i=P)
                    tiles = slice(4 * n, 4 * n + 4)
                    dve.tensor_tensor(kk_decay[:, tiles], pair[:, :, 1], decay[:, tiles], ALU.mult)\
                       .then_inc(kk_done, 1)
                    dve.tensor_tensor(intra[:, tiles], pair[:, :, 0], decay[:, tiles], ALU.mult).then_inc(kk_done, 1)
                for n, t in enumerate((4, 5, 6, 7, 0, 1, 2, 3)):
                    if n == 0:
                        dve.wait_ge(kt_mm, 2 * h + 2)
                    if n == 4:
                        dve.wait_ge(k_bg_done, TT * h + 4)
                    dve.tensor_scalar(k_dec[:, t], ps[:, 4 + t // 4, (t % 4) * P:(t % 4 + 1) * P],
                                      hgate[:, G_KDEC, t:t + 1], None, ALU.mult).then_inc(k_dec_done, 1)
                NL = len(LEVELS)
                for n in range(NL):
                    for a in range(2):
                        dve.wait_ge(lx_mm, 2 * NL * h + 2 * n + a + 1)
                        for t in range(4 * a, 4 * a + 4):
                            last = dve.scalar_tensor_tensor(
                                out=LX[:, t], in0=ps[:, 6 + a, (t % 4) * P:(t % 4 + 1) * P],
                                scalar=hgate[:, G_NBETA, t:t + 1], in1=level_mask[:, n], op0=ALU.mult, op1=ALU.mult)
                        last.then_inc(lx_done, 1)
                    for a in range(2):
                        tiles = slice(4 * a, 4 * a + 4)
                        if n < NL - 1:
                            dve.wait_ge(xl_mm, 2 * (NL - 1) * h + 2 * n + a + 1)
                        dve.wait_ge(yl_mm, 2 * NL * h + 2 * n + a + 1)
                        if n < NL - 1:
                            dve.tensor_tensor(X[:, tiles], X[:, tiles],
                                              ps[:, 4 + a].rearrange("p (t i) -> p t i", i=P), ALU.add)\
                               .then_inc(x_upd, 1)
                        dve.tensor_tensor(Y[:, tiles], Y[:, tiles],
                                          ps[:, 2 + a].rearrange("p (t i) -> p t i", i=P), ALU.add).then_inc(y_upd, 1)
                for t in range(TT):
                    dve.wait_ge(ds_mm, TT * h + t + 1)
                    dve.scalar_tensor_tensor(out=S[:], in0=S[:], scalar=hgate[:, G_LAST, t:t + 1],
                                             in1=ps[:, 2, P:2 * P], op0=ALU.mult, op1=ALU.add).then_inc(s_ready, 1)
                    if t == 6:
                        split_w_lo(dve, *next_tile("head", h, 4))
                invert_root(2)
                dve.wait_ge(o_copied, TT * h + TT)
                dve.scalar_tensor_tensor(out=o_raw[:], in0=o_raw[:], scalar=params[:, 12 * KD:12 * KD + 1],
                                         in1=norm[:], op0=ALU.mult, op1=ALU.mult).then_inc(o_step, 1)
                dve.wait_ge(o_step, 2 * h + 1)
                dve.tensor_tensor(o_raw[:], o_raw[:], z_act[:], ALU.mult).then_inc(o_step, 1)
                dve.wait_ge(o_hi_done, 2 * h + 1)
                dve.wait_ge(o_step, 2 * h + 2)
                dve.tensor_tensor(o_lo[:], o_raw[:], o_hi[:], ALU.subtract).then_inc(o_hi_done, 1)

            def merge_lo(i, last):
                for p in range(2):
                    if p == 0 or not last:
                        split_w_lo(dve, *next_tile("merge", i, p))
                    step = 3 * (2 * i + p)
                    dve.wait_ge(wo_hi_done, 2 * i + p + 1)
                    dve.tensor_tensor(wo_lo[:, :, bass.ds((2 * i + p) * P, P)], w_raw[:, 2],
                                      wo_hi[:, :, bass.ds((2 * i + p) * P, P)], ALU.subtract).then_inc(wo_lo_done, 1)
                    dve.wait_ge(ga_sig, 2 * i + p + 1)
                    for half in range(2):
                        cols = slice(half * HALF, (half + 1) * HALF)
                        dve.wait_ge(proj_done, group("merge", i, p, half))
                        dve.tensor_tensor(ga_in[:, p, cols], ps[:, 2 * p + half], ga_in[:, p, cols], ALU.mult)\
                           .then_inc(m_step, 1)
                    dve.wait_ge(m_step, step + 2)
                    dve.wait_ge(mb_arrived[p], 16 * i + 16)
                    dve.tensor_tensor(ga_in[:, p], ga_in[:, p], mb_in[:, p], ALU.add).then_inc(m_step, 1)
                    dve.wait_ge(m_hi_done, 2 * i + p + 1)
                    dve.wait_ge(m_out[p], 32 * i)
                    dve.tensor_tensor(m_lo[:, p], ga_in[:, p], m_hi[:, p], ALU.subtract).then_inc(m_lo_done, 1)

            with dve.Fori(0, KD // 2 - 1) as i:
                merge_lo(i, False)
            merge_lo(KD // 2 - 1, True)
            dve.wait_ge(rows_in, 16 * 7)
            with dve.Fori(0, TT // 2) as i:
                for s in range(2):
                    n = 2 * i + s
                    tile = x1[:, bass.ds(n, 1)].rearrange("p o d -> p (o d)")
                    dve.wait_ge(xr_in[s], 16 * i + 16)
                    for half in range(2):
                        cols = slice(half * HALF, (half + 1) * HALF)
                        dve.wait_ge(out_mm, 2 + 2 * n + half + 1)
                        dve.tensor_tensor(tile[:, cols], ps[:, 2 * s + half], gt1_row[:, cols], ALU.mult)\
                           .then_inc(x1_scaled, 1)
                    for half in range(2):
                        cols = slice(half * HALF, (half + 1) * HALF)
                        dve.wait_ge(x1_scaled, 2 * n + half + 1)
                        dve.tensor_tensor(tile[:, cols], tile[:, cols], xr[:, s, cols], ALU.add).then_inc(x1_done, 1)
                    col = bass.ds(n, 1)
                    dve.wait_ge(x1_squared, n + 1)
                    dve.tensor_scalar(stat2[:, 2, col], stat2[:, 0, col], 1.0 / D, EPS, ALU.mult, ALU.add)\
                       .then_inc(x1_mean, 1)
                    dve.wait_ge(x1_root, n + 1)
                    dve.reciprocal(stat2[:, 2, col], stat2[:, 1, col]).then_inc(x1_inv, 1)
                    dve.wait_ge(x1_inv, n + 1)
                    dve.wait_ge(h2_turned, 2 * n)
                    dve.wait_ge(h2_out[s], 16 * i)
                    dve.scalar_tensor_tensor(out=h2[:, s], in0=tile, scalar=stat2[:, 2, col], in1=g2_row[:],
                                             op0=ALU.mult, op1=ALU.mult).then_inc(h2_scaled, 1)
                    dve.wait_ge(h2_scaled, n + 1)
                    dve.tensor_tensor(h2[:, s], h2[:, s], sh2_row[:], ALU.add).then_inc(h2_done, 1)
            dve.wait_ge(logits_done, TT)
            dve.wait_ge(iotas, 1)
            steps = [0]

            def link(ins):
                steps[0] += 1
                ins.then_inc(r_step, 1)
                dve.wait_ge(r_step, steps[0])

            def over_groups(x):
                return x[:, :, None].to_broadcast([P, TT, NG])

            def over_experts(x):
                return x[:, :, None].to_broadcast([P, TT, NE])

            def first_max(one, cand, values, iota, best, at_):
                n = values.shape[2]
                link(dve.tensor_reduce(best, values, AX.X, ALU.max))
                link(dve.tensor_tensor(cand, values, best[:, :, None].to_broadcast([P, TT, n]), ALU.is_equal))
                link(dve.scalar_tensor_tensor(out=cand, in0=cand, scalar=-1000.0,
                                              in1=iota[:, None, :].to_broadcast([P, TT, n]),
                                              op0=ALU.mult, op1=ALU.add))
                link(dve.tensor_reduce(at_, cand, AX.X, ALU.min))
                link(dve.tensor_tensor(one, cand, at_[:, :, None].to_broadcast([P, TT, n]), ALU.is_equal))

            def of_pair(dst, one, table):
                link(dve.tensor_tensor(e_tmp[:], one[:], table, ALU.mult))
                link(dve.tensor_reduce(dst, e_tmp[:], AX.X, ALU.add))

            S_ = [r_small[:, n] for n in range(16)]
            link(dve.tensor_tensor(logits[:], ps[:, 6, 0:TT * (NG + NE)].rearrange("p (t n) -> p t n", t=TT),
                                   b_route[:, None, :].to_broadcast([P, TT, NG + NE]), ALU.add))
            first_max(g_one[:], g_cand[:], logits[:, :, 0:NG], iota_g, S_[0], S_[1])
            link(dve.tensor_tensor(g_cand[:], logits[:, :, 0:NG], over_groups(S_[0]), ALU.subtract))
            assert steps[0] == R_GEXP
            link(dve.tensor_scalar(g_one[:], g_one[:], -1.0, None, ALU.add))
            link(dve.scalar_tensor_tensor(
                out=e_log[:].rearrange("p t (g e) -> p t g e", g=NG),
                in0=g_one[:, :, :, None].to_broadcast([P, TT, NG, NE // NG]), scalar=HUGE,
                in1=logits[:, :, NG:].rearrange("p t (g e) -> p t g e", g=NG), op0=ALU.mult, op1=ALU.add))
            first_max(e_one[0][:], e_cand[:], e_log[:], iota_e, S_[3], S_[4])
            link(dve.scalar_tensor_tensor(out=e_log[:], in0=e_one[0][:], scalar=-HUGE, in1=e_log[:],
                                          op0=ALU.mult, op1=ALU.add))
            first_max(e_one[1][:], e_cand[:], e_log[:], iota_e, S_[5], S_[6])
            link(dve.tensor_tensor(S_[7], S_[5], S_[3], ALU.subtract))
            assert steps[0] == R_EEXP
            link(dve.tensor_tensor(e_both[:], e_one[0][:], e_one[1][:], ALU.add))
            assert steps[0] == R_BOTH
            dve.wait_ge(r_exp, 2)
            link(dve.tensor_reduce(S_[2], g_exp[:], AX.X, ALU.add))
            link(dve.scalar_tensor_tensor(out=S_[9], in0=S_[8], scalar=1.0, in1=S_[2], op0=ALU.add, op1=ALU.mult))
            link(dve.reciprocal(wts[:, 0], S_[9]))
            link(dve.tensor_tensor(wts[:, 1], wts[:, 0], S_[8], ALU.mult))
            dve.wait_ge(counts_mm, 1)
            count = ps[:, 7, TT * NE:(TT + 1) * NE]
            link(dve.tensor_tensor(over_tmp[:], count[:, :, None].to_broadcast([P, NE, MAX_OVER]),
                                   mults[:, None, :].to_broadcast([P, NE, MAX_OVER]), ALU.is_gt))
            link(dve.tensor_reduce(over_cum[:, 0], over_tmp[:], AX.X, ALU.add))
            link(dve.tensor_copy(e_tmp[:, 0], over_cum[:, 0]))
            src, step = 0, 1
            while step < NE:
                link(dve.tensor_copy(over_cum[:, 1 - src, 0:step], over_cum[:, src, 0:step]))
                link(dve.tensor_tensor(over_cum[:, 1 - src, step:], over_cum[:, src, step:],
                                       over_cum[:, src, 0:NE - step], ALU.add))
                src, step = 1 - src, 2 * step
            link(dve.memset(over_f[:], 0.0))
            link(dve.tensor_copy(over_f[:, 0:1], over_cum[:, src, NE - 1:NE]))
            link(dve.tensor_tensor(over_tmp[:].rearrange("p e b -> p (e b)").rearrange("p (b e) -> p b e", b=MAX_OVER),
                                   over_cum[:, src, None, :].to_broadcast([P, MAX_OVER, NE]),
                                   iota_b[:, 0:MAX_OVER, None].to_broadcast([P, MAX_OVER, NE]), ALU.is_le))
            link(dve.tensor_reduce(over_f[:, 1:1 + MAX_OVER], over_tmp[:].rearrange("p e b -> p (e b)")
                                   .rearrange("p (b e) -> p b e", b=MAX_OVER), AX.X, ALU.add))
            link(dve.tensor_scalar(over_f[:, 1:1 + MAX_OVER], over_f[:, 1:1 + MAX_OVER], float(NE - 1), None, ALU.min))
            link(dve.tensor_copy(over[:], over_f[:]))
            link(dve.tensor_tensor(over_cum[:, 1 - src], over_cum[:, src], e_tmp[:, 0], ALU.subtract))
            first = over_cum[:, 1 - src]
            m_tmp = over_tmp[:].rearrange("p e b -> p (e b)")[:, 0:TT * MAX_OVER].rearrange("p (t b) -> p t b", t=TT)
            for k in range(TOP_K):
                of_pair(S_[10], e_one[k], ps[:, 7, 0:TT * NE].rearrange("p (t e) -> p t e", t=TT))
                link(dve.tensor_scalar(S_[10], S_[10], -1.0, None, ALU.add))
                link(dve.tensor_tensor(m_tmp, S_[10][:, :, None].to_broadcast([P, TT, MAX_OVER]),
                                       mults[:, None, :].to_broadcast([P, TT, MAX_OVER]), ALU.is_ge))
                link(dve.tensor_reduce(S_[11], m_tmp, AX.X, ALU.add))
                of_pair(S_[12], e_one[k], iota_e[:, None, :].to_broadcast([P, TT, NE]))
                of_pair(S_[13], e_one[k], first[:, None, :].to_broadcast([P, TT, NE]))
                link(dve.tensor_tensor(S_[13], S_[13], S_[11], ALU.add))
                link(dve.scalar_tensor_tensor(out=S_[13], in0=S_[13], scalar=float(NE - 1), in1=S_[12],
                                              op0=ALU.add, op1=ALU.subtract))
                link(dve.tensor_scalar(S_[14], S_[11], 1.0, None, ALU.min))
                link(dve.tensor_tensor(S_[13], S_[13], S_[14], ALU.mult))
                link(dve.tensor_tensor(S_[12], S_[12], S_[13], ALU.add))
                link(dve.tensor_tensor(S_[12], S_[12], S_[11], ALU.subtract))
                link(dve.scalar_tensor_tensor(out=S_[12], in0=S_[12], scalar=float(P), in1=S_[10],
                                              op0=ALU.mult, op1=ALU.add))
                link(dve.tensor_copy(slot_i[:, k], S_[12]))
            dve.sem_inc(slots_ready, 1)
            dve.wait_ge(ids_turned, 1)
            dve.tensor_copy(ids[:], ps[:, 7, 0:BLOCKS]).then_inc(ids_ready, 1)
            dve.wait_ge(ids_ready, 1)
            dve.sem_inc(ids_ready, 1)

            def next_ids(b, s):
                dve.tensor_copy(ids_now[:, s, 0:1], ids[:, bass.ds(b, 1)]).then_inc(ids_now_ready, 1)

            def block_dve(b, s):
                dve.wait_ge(xT_mm, 2 * b + 2)
                next_ids(b + 1, 1 - s)
                for part in range(2):
                    dve.wait_ge(gate_silu, 2 * b + part + 1)
                    dve.wait_ge(gu_mm, 4 + 4 * b + 2 * part + 2)
                    dve.wait_ge(hT_mm, 2 * b)
                    cols = slice(part * 2 * P, (part + 1) * 2 * P)
                    dve.tensor_tensor(hid[:, cols], ps[:, 2 * part + 1, 0:2 * P], gate_act[:, cols], ALU.mult)\
                       .then_inc(hid_done, 1)
                dve.wait_ge(dn_mm, 2 + 2 * b + 2)
                dve.wait_ge(y_out[s], y_count(b, s))
                dve.tensor_copy(y_sb[:, s, HALF:D], ps[:, 7]).then_inc(y_copied[1], 1)

            dve.tensor_copy(ids_now[:, 0, 0:1], ids[:, 0:1]).then_inc(ids_now_ready, 1)
            with dve.Fori(0, NE // 2) as i:
                for s in range(2):
                    block_dve(2 * i + s, s)
            over_blocks(dve, lambda b, s, j: block_dve(b, s))
            dve.wait_ge(y_all, 1)
            dve.wait_ge(rows_in, 16 * 9)
            with dve.Fori(0, TT // 2) as i:
                for s in range(2):
                    n = 2 * i + s
                    col = bass.ds(n, 1)
                    dve.wait_ge(yg_in[s], 32 * i)
                    dve.tensor_copy(ids_now[:, s], slot_i[:, :, col].rearrange("p k o -> p (k o)"))\
                       .then_inc(pair_ids, 1)
                for s in range(2):
                    n = 2 * i + s
                    col = bass.ds(n, 1)
                    dve.wait_ge(yg_in[s], 32 * i + 32)
                    dve.tensor_scalar(y_acc[:, s], y_g[:, 0, s], wts[:, 0, col], None, ALU.mult).then_inc(acc_step, 1)
                    dve.wait_ge(acc_step, 4 * n + 1)
                    dve.scalar_tensor_tensor(out=y_acc[:, s], in0=y_g[:, 1, s], scalar=wts[:, 1, col],
                                             in1=y_acc[:, s], op0=ALU.mult, op1=ALU.add).then_inc(acc_step, 1)
                    dve.wait_ge(acc_step, 4 * n + 2)
                    dve.tensor_tensor(y_acc[:, s], y_acc[:, s], gt2_row[:], ALU.mult).then_inc(acc_step, 1)
                    dve.wait_ge(acc_step, 4 * n + 3)
                    dve.tensor_tensor(y_acc[:, s], y_acc[:, s], x1[:, col].rearrange("p o d -> p (o d)"), ALU.add)\
                       .then_inc(acc_step, 1)
                    dve.wait_ge(x1_squared, TT + n + 1)
                    dve.tensor_scalar(stat3[:, 2, col], stat3[:, 0, col], 1.0 / D, EPS, ALU.mult, ALU.add)\
                       .then_inc(x1_mean, 1)
                    dve.wait_ge(x1_root, TT + n + 1)
                    dve.reciprocal(stat3[:, 2, col], stat3[:, 1, col]).then_inc(x1_inv, 1)
                    dve.wait_ge(x1_inv, TT + n + 1)
                    dve.wait_ge(res_out[s], 16 * i)
                    dve.scalar_tensor_tensor(out=res[:, s], in0=y_acc[:, s], scalar=stat3[:, 2, col], in1=nf_row[:],
                                             op0=ALU.mult, op1=ALU.mult).then_inc(res_done, 1)

        @block.tensor
        def _(pe):
            pe.sem_inc(proj_done, 2 * SLOTS)
            pe.sem_inc(w_hi_done, SLOTS)
            pe.sem_inc(w_lo_done, SLOTS)
            pe.sem_inc(bank_free, 2)
            pe.sem_inc(m_lo_done, 2)
            pe.sem_inc(out_mm, 2)
            pe.sem_inc(x1_done, 2)
            pe.sem_inc(h2_turned, 2)
            pe.sem_inc(gu_mm, 4)
            pe.sem_inc(dn_mm, 2)
            pe.wait_ge(masks_done, N_MASKS)
            pe.wait_ge(params_in, 16 * 9)
            pe.transpose(ps[:, 0, 0:97], rows_a[:], ident[0:97, 0:97])
            pe.transpose(ps[:, 1, 0:96], rows_b[:], ident[0:96, 0:96]).then_inc(rows_turned, 1)
            pe.wait_ge(cols_ready, 3)

            def ada_chunk(buf, chunk, inc=True):
                for m in range(4):
                    for k in range(KD):
                        last = pe.matmul(ps[:, 7, bass.ds(chunk * 4 + m, 1)] if not isinstance(chunk, int)
                                         else ps[:, 7, chunk * 4 + m:chunk * 4 + m + 1],
                                         buf[:, k, m * P:(m + 1) * P], c_act[:, k:k + 1],
                                         start=(k == 0), stop=(k == KD - 1))
                last.then_inc(ada_used, 1)
                return last

            for n in range(4):
                pe.wait_ge(ada_in[n % 2], 16 * (n // 2 + 1))
                ada_chunk(ada[:, n % 2], n)
            with pe.Fori(0, TT // 2) as i:
                for s in range(2):
                    n = 2 * i + s
                    pe.wait_ge(x_normed, n + 1)
                    pe.wait_ge(h_summed, 16 * i)
                    for k in range(KD):
                        last = pe.transpose(ps[:, 2 * s + k // 4, (k % 4) * P:(k % 4 + 1) * P],
                                            x_n[:, s, k * P:(k + 1) * P], ident[:])
                        if k % 4 == 3:
                            last.then_inc(x_turned, 1)
            pe.wait_ge(h_lo_done, TT)
            pe.wait_ge(h_hi_done, TT)
            pe.wait_ge(gate_w_split, 2)
            for t in range(TT):
                for k in range(KD):
                    for part in range(3):
                        lhs = h_lo if part == 0 else h_hi
                        rhs = w_gate_lo if part == 1 else w_gate_hi
                        last = pe.matmul(ps[:, 2, t * 2 * H:(t + 1) * 2 * H], lhs[:, k, t * P:(t + 1) * P], rhs[:, k],
                                         start=(k == 0 and part == 0), stop=(k == KD - 1 and part == 2))
            last.then_inc(gate_logits, 1)
            pe.wait_ge(gate_step, 6)
            g_flat = gates[:, G_LOG].rearrange("p t h -> p (t h)")
            for n, mask in enumerate((incl, later, ones)):
                last = pe.matmul(ps[:, 3, n * TT * H:(n + 1) * TT * H], mask[:], g_flat, start=True, stop=True)
            last.then_inc(gate_sums, 1)
            pe.wait_ge(gate_exp, 7)
            pe.wait_ge(gates_done, 1)
            with pe.Fori(0, KD) as i:
                for p, (freed, per) in enumerate(((sc_copied, 2), (prod_done, 2), (sc_y_done, 2))):
                    wait_w(pe, "conv", i, p)
                    pe.wait_ge(freed, per * i)
                    for n in range(2):
                        last = project(pe, ps[:, 2 * p + n], "conv", p, h_hi, h_lo, n)
                        last.then_inc(proj_done, 1)
                pe.wait_ge(ada_in[2], 16 * i + 16)
                ada_chunk(ada_b, 4 + i)
            pe.wait_ge(s_lo_done, KD)
            pe.wait_ge(s_hi_done, KD)
            pe.wait_ge(mod_ready, 4)
            pe.transpose(ps[0:N_MOD * KD, 7, 0:P], mod[:].rearrange("p a k -> p (a k)"), ident[:])\
              .then_inc(mod_turned, 1)
            with pe.Fori(0, KD) as i:
                for p, freed in enumerate((gb_sig, mb_done)):
                    wait_w(pe, "gate_b", i, p)
                    pe.wait_ge(freed, 2 * i)
                    for n in range(2):
                        last = project(pe, ps[:, 2 * p + n], "gate_b", p, (h_hi, s_hi)[p], (h_lo, s_lo)[p], n)
                        last.then_inc(proj_done, 1)
            pe.wait_ge(mb_done, 2 * KD)
            NL = len(LEVELS)
            with pe.Fori(0, H) as h:
                def head_tile(p):
                    wait_w(pe, "head", h, p)
                    for half in range(2):
                        pe.wait_ge(bank_free, 2 + 10 * h + 2 * p + half - 1)
                        project(pe, ps[:, half], "head", p, h_hi, h_lo, half).then_inc(proj_done, 1)

                def square_sums(n, banks, src):
                    pe.wait_ge(squared, 3 * h + n + 1)
                    for half in range(2):
                        pe.matmul(ps[:, banks + half], ones[:], src[:, half * HALF:(half + 1) * HALF],
                                  start=True, stop=True).then_inc(norm_mm, 1)

                lx_flat = LX[:].rearrange("p t i -> p (t i)")
                head_tile(0)
                pe.wait_ge(pool_rows, 2 * h + 2)
                pe.wait_ge(root_done, 6 * h)
                for n in range(4):
                    src = (X, Y)[n // 2]
                    for t in range(4):
                        last = pe.matmul(ps[:, 4 + n, t * P:(t + 1) * P], src[:, (n % 2) * 4 + t], incl[:],
                                         start=True, stop=True)
                    last.then_inc(decay_mm, 1)
                head_tile(1)
                pe.wait_ge(decay_exp, 4 * h + 2)
                square_sums(0, 4, lx_flat)
                head_tile(2)
                pe.wait_ge(decay_exp, 4 * h + 4)
                square_sums(1, 6, lx_flat)
                pe.wait_ge(root_done, 6 * h + 2)
                pe.wait_ge(qk_normed, 2 * h + 2)
                for t in range(TT):
                    last = pe.transpose(ps[:, 4 + t // 4, (t % 4) * P:(t % 4 + 1) * P],
                                        qk[:, 1, t * P:(t + 1) * P], ident[:])
                    if t % 4 == 3:
                        last.then_inc(kt_mm, 1)
                pe.wait_ge(root_done, 6 * h + 4)
                for n, bank in enumerate((6, 2)):
                    for t in range(4):
                        tok = slice((4 * n + t) * P, (4 * n + t + 1) * P)
                        last = pe.matmul(ps[:, bank + t // 2, (t % 2) * 2 * P:(t % 2 + 1) * 2 * P],
                                         qk[:, 1, tok], qk[:, :, tok], start=True, stop=True)
                    last.then_inc(kk_mm, 1)
                pe.wait_ge(silu_done, 3 * h + 3)
                pe.wait_ge(k_bg_done, TT * h + TT)
                pe.wait_ge(k_dec_done, TT * h + TT)
                for t in range(TT):
                    last = pe.transpose(ps[:, 4 + t // 4, (t % 4) * P:(t % 4 + 1) * P],
                                        vv[:, t * P:(t + 1) * P], ident[:])
                    if t % 4 == 3:
                        last.then_inc(vt_mm, 1)
                pe.wait_ge(xy_init, 2 * h + 2)
                for n in range(NL):
                    for a in range(2):
                        if n == 0:
                            pe.wait_ge(kk_done, 4 * h + 4)
                        else:
                            pe.wait_ge(x_upd, 2 * (NL - 1) * h + 2 * (n - 1) + a + 1)
                        for t in range(4 * a, 4 * a + 4):
                            last = pe.matmul(ps[:, 6 + a, (t % 4) * P:(t % 4 + 1) * P], kk_decay[:, t], X[:, t],
                                             start=True, stop=True)
                        last.then_inc(lx_mm, 1)
                    for a in range(2):
                        pe.wait_ge(lx_done, 2 * NL * h + 2 * n + a + 1)
                        if n > 0:
                            pe.wait_ge(y_upd, 2 * NL * h + 2 * (n - 1) + a + 1)
                        else:
                            pe.wait_ge(v_beta_done, TT * h + TT)
                        if n < NL - 1:
                            for t in range(4 * a, 4 * a + 4):
                                last = pe.matmul(ps[:, 4 + a, (t % 4) * P:(t % 4 + 1) * P], Y[:, t], LX[:, t],
                                                 start=True, stop=True)
                            last.then_inc(xl_mm, 1)
                        for t in range(4 * a, 4 * a + 4):
                            last = pe.matmul(ps[:, 2 + a, (t % 4) * P:(t % 4 + 1) * P], LX[:, t], Y[:, t],
                                             start=True, stop=True)
                        last.then_inc(yl_mm, 1)
                for a in range(2):
                    pe.wait_ge(y_upd, 2 * NL * h + 2 * (NL - 1) + a + 1)
                    for t in range(4 * a, 4 * a + 4):
                        last = pe.matmul(ps[:, 6 + a, (t % 4) * P:(t % 4 + 1) * P], k_bg[:, t], Y[:, t],
                                         start=True, stop=True)
                    last.then_inc(w_mm, 1)
                pe.wait_ge(q_dec_done, h + 1)
                def filler(n):
                    p, half, quarter = 3 + n // 8, n // 4 % 2, n % 4
                    if quarter == 0:
                        wait_w(pe, "head", h, p)
                        pe.wait_ge(bank_free, 2 + 10 * h + 2 * p + half - 1)
                    last = project(pe, ps[:, half], "head", p, h_hi, h_lo, half, ks=range(2 * quarter, 2 * quarter + 2))
                    if quarter == 3:
                        last.then_inc(proj_done, 1)

                for t in range(TT):
                    pe.wait_ge(s_ready, (TT + 1) * h + t + 1)
                    if t % 4 == 0:
                        pe.wait_ge(w_neg_done, 2 * h + t // 4 + 1)
                    pe.matmul(ps[:, 2, 0:P], Y[:, t], v_beta[:, t], start=True, stop=False)
                    pe.matmul(ps[:, 2, 0:P], w_neg[:, t], S[:], start=False, stop=True).then_inc(vn_mm, 1)
                    if t >= 2:
                        pe.wait_ge(o_copied, TT * h + t - 1)
                    o_t = ps[:, 3 + t % 2, 0:P]
                    pe.matmul(o_t, S[:], q_dec[:, t], start=True, stop=False)
                    filler(2 * t)
                    pe.wait_ge(vn_done, TT * h + t + 1)
                    pe.matmul(ps[:, 2, P:2 * P], k_dec[:, t], v_new[:, t % 2], start=True, stop=True)\
                      .then_inc(ds_mm, 1)
                    pe.matmul(o_t, v_new[:, t % 2], intra[:, t], start=False, stop=True).then_inc(o_mm, 1)
                    filler(2 * t + 1)
                square_sums(2, 4, lx_flat)
            pe.wait_ge(o_in, 32)
            pe.wait_ge(root_done, 6 * H)
            with pe.Fori(0, KD // 2) as i:
                for p in range(2):
                    wait_w(pe, "merge", i, p)
                    pe.wait_ge(m_step, 6 * i + 3 * p - 3 * p)
                    for half in range(2):
                        project(pe, ps[:, 2 * p + half], "merge", p, s_hi, s_lo, half).then_inc(proj_done, 1)
            def project_out(n, s):
                pe.wait_ge(mt_in[s], 16 * n - 16 * s + 32)
                pe.wait_ge(x1_done, 2 * n)
                for half in range(2):
                    for k in range(KD):
                        for part in range(3):
                            lhs = mt_lo if part == 0 else mt_hi
                            rhs = wo_lo if part == 1 else wo_hi
                            last = pe.matmul(ps[:, 2 * s + half], lhs[:, s, k], rhs[:, k, half * HALF:(half + 1) * HALF],
                                             start=(k == 0 and part == 0), stop=(k == KD - 1 and part == 2))
                    last.then_inc(out_mm, 1)

            def route(n, s):
                pe.wait_ge(h2_done, n + 1)
                pe.wait_ge(h2T_done, 2 * n)
                for k in range(KD):
                    last = pe.transpose(ps[:, 4 + k // 4, (k % 4) * P:(k % 4 + 1) * P], h2[:, s, k * P:(k + 1) * P],
                                        ident[:])
                    if k % 4 == 3:
                        last.then_inc(h2_turned, 1)
                pe.wait_ge(h2T_done, 2 * n + 2)
                for k in range(KD):
                    last = pe.matmul(ps[:, 6, bass.ds(n * (NG + NE), NG + NE)], h2T[:, s, k], w_route[:, k],
                                     start=(k == 0), stop=(k == KD - 1))
                last.then_inc(logits_done, 1)

            pe.wait_ge(rows_in, 16 * 7)
            pe.wait_ge(m_step, 3 * KD)
            pe.wait_ge(wo_lo_done, KD)
            project_out(0, 0)
            with pe.Fori(0, TT // 2 - 1) as i:
                project_out(2 * i + 1, 1)
                route(2 * i, 0)
                project_out(2 * i + 2, 0)
                route(2 * i + 1, 1)
            project_out(TT - 1, 1)
            route(TT - 2, 0)
            route(TT - 1, 1)
            pe.wait_ge(r_step, R_BOTH)
            for t in range(TT):
                for u in range(t + 1):
                    pe.matmul(ps[:, 7, t * NE:(t + 1) * NE], (incl if u == t else ones)[:], e_both[:, u],
                              start=(u == 0), stop=(u == t))
            for u in range(TT):
                last = pe.matmul(ps[:, 7, TT * NE:(TT + 1) * NE], ones[:], e_both[:, u],
                                 start=(u == 0), stop=(u == TT - 1))
            last.then_inc(counts_mm, 1)
            pe.wait_ge(id_rows_in, 16)
            pe.wait_ge(slots_ready, 1)
            pe.transpose(ps[:, 7, 0:BLOCKS], id_rows[:], ident[0:BLOCKS, 0:BLOCKS]).then_inc(ids_turned, 1)

            def turn_rows(b, s, first=False):
                pe.wait_ge(xg_in[s], y_count(b, s) + 16)
                for k in range(KD):
                    last = pe.transpose(ps[:, k // 4, (k % 4) * P:(k % 4 + 1) * P], xg[:, s, k * P:(k + 1) * P],
                                        ident[:])
                    if k % 4 == 3:
                        last.then_inc(xT_mm, 1)

            def block_pe(b, s):
                wa, wb, wc = ew[s]

                def up(part, which):
                    for k in range(KD):
                        last = pe.matmul(ps[:, 2 * part + which, 0:2 * P], xT[:, s, k],
                                         (wa, wb)[which][:, k, part * 2 * P:(part + 1) * 2 * P],
                                         start=(k == 0), stop=(k == KD - 1))
                    last.then_inc(gu_mm, 1)

                def turn_hidden(part):
                    pe.wait_ge(hid_done, 2 * b + part + 1)
                    for f in range(2):
                        col = (2 * part + f) * P
                        last = pe.transpose(ps[:, 4 + part, f * P:(f + 1) * P], hid[:, col:col + P], ident[:])
                    last.then_inc(hT_mm, 1)

                def down(part):
                    pe.wait_ge(hT_done, 2 * b + part + 1)
                    for half in range(2):
                        for f in range(2 * part, 2 * part + 2):
                            last = pe.matmul(ps[:, 6 + half], hidT[:, f], wc[:, f, half * HALF:(half + 1) * HALF],
                                             start=(f == 0), stop=(f == FT - 1))
                        if part == 1:
                            last.then_inc(dn_mm, 1)

                pe.wait_ge(xT_done, 2 * b + 2)
                pe.wait_ge(ew_in[s][0], y_count(b, s) + 16)
                up(0, 0)
                pe.wait_ge(ew_in[s][1], y_count(b, s) + 16)
                up(0, 1)
                up(1, 0)
                turn_hidden(0)
                up(1, 1)
                pe.wait_ge(ew_in[s][2], y_count(b, s) + 16)
                pe.wait_ge(y_copied[0], b)
                pe.wait_ge(y_copied[1], b)
                down(0)
                turn_hidden(1)
                turn_rows(b + 1, 1 - s)
                down(1)

            pe.wait_ge(ids_ready, 2)
            turn_rows(0, 0)
            with pe.Fori(0, NE // 2) as i:
                for s in range(2):
                    block_pe(2 * i + s, s)
            over_blocks(pe, lambda b, s, j: block_pe(b, s))


_INS = ['x', 'c', 'w_ada', 'b_ada', 'norm1_g', 'w_in', 'conv_qkv_w', 'a_log', 'dt_bias', 'onorm_g', 'w_proj_a',
        'conv_sc_w', 'w_proj_b', 'w_out', 'norm2_g', 'w_group', 'b_group', 'w_expert', 'b_expert', 'w1', 'w3', 'w2',
        'normf_g']
_OUTS = [((1, 1024, 1024), 'float32')]


def kernel(**inputs):
    import numpy as _np
    import concourse.bacc as _bacc
    from concourse import mybir as _mybir
    from concourse.bass_utils import run_bass_kernel_spmd as _run

    nc = _bacc.Bacc("TRN2", target_bir_lowering=False, num_devices=1)
    arrays, args = {}, []
    for name in _INS:
        a = _np.ascontiguousarray(inputs[name])
        arrays[f"in_{name}_dram"] = a
        args.append(nc.dram_tensor(f"in_{name}_dram", a.shape, _mybir.dt.from_np(a.dtype), kind="ExternalInput").ap())
    for i, (shape, dtype) in enumerate(_OUTS):
        dt = _mybir.dt.from_np(_np.dtype(dtype))
        args.append(nc.dram_tensor(f"out_{i}_dram", shape, dt, kind="ExternalOutput").ap())
    decoder_block(nc, *args)
    r = _run(nc, [arrays], core_ids=[0])
    got = tuple(r.results[0][f"out_{i}_dram"] for i in range(len(_OUTS)))
    return got[0]
```

```python
from contextlib import ExitStack

import concourse.bass as bass
from concourse import mybir

ALU = mybir.AluOpType
ACT = mybir.ActivationFunctionType
AX = mybir.AxisListType
F32 = mybir.dt.float32
F32R = mybir.dt.float32r
I32 = mybir.dt.int32

P = 128
HALF = 512
N_MOD = 6
TOP_K = 2
HUGE = 3e38
EPS = 1e-6


def weight_stream():
    phases = {"conv": (8, (0, 1, 2)), "gate_b": (8, (0, 1)), "head": (8, (0, 1, 2, 0, 1)), "merge": (4, (0, 1))}
    stream, base, arrivals = {}, 0, [0, 0, 0]
    for name, (iters, slots) in phases.items():
        per, tiles = len(slots), []
        for p, slot in enumerate(slots):
            back = next(d for d in range(1, per + 1) if slots[(p - d) % per] == slot)
            tiles.append(dict(slot=slot, back=back, first_arrival=arrivals[slot] + slots[:p].count(slot) + 1,
                              arrivals_per=slots.count(slot)))
        stream[name] = dict(base=base, per=per, tiles=tiles)
        base += iters * per
        for slot in slots:
            arrivals[slot] += iters
    return stream


def decoder_block(nc, x, c, w_ada, b_ada, norm1_g, w_in, conv_qkv_w, a_log, dt_bias, onorm_g, w_proj_a,
                  conv_sc_w, w_proj_b, w_out, norm2_g, w_group, b_group, w_expert, b_expert, w1, w3, w2,
                  normf_g, out):
    _, T, D = x.shape
    KD = D // P
    TT = T // P
    H = a_log.shape[1]
    QKV_TAPS = conv_qkv_w.shape[1]
    SC_TAPS = conv_sc_w.shape[1]
    VAL0 = 3 * D
    GATE0 = 4 * D
    SC0 = GATE0 + 2 * H
    NG = w_group.shape[2]
    NE = w_expert.shape[2]
    F = w1.shape[3]
    FT = F // P
    MAX_OVER = TOP_K * T // P - 1
    BLOCKS = NE + MAX_OVER + 2
    SLOTS = 3
    LEVELS = [1, 2, 4, 8, 16, 32, 64]
    stream = weight_stream()

    x_d = x[0]
    w_in_d = w_in[0].rearrange("(k p) n -> p k n", p=P)
    w_a_d = w_proj_a[0].rearrange("(k p) n -> p k n", p=P)
    w_b_d = w_proj_b[0].rearrange("(k p) n -> p k n", p=P)
    w_o_d = w_out[0].rearrange("(k p) n -> p k n", p=P)
    w_ada_d = w_ada[0].rearrange("(k p) n -> p k n", p=P)

    merged_b_d = nc.dram_tensor("merged_b_d", [D, T], F32, kind="Internal").ap()
    gate_a_d = nc.dram_tensor("gate_a_d", [D, T], F32, kind="Internal").ap()
    o_hi_d = nc.dram_tensor("o_hi_d", [D, T], F32, kind="Internal").ap()
    o_lo_d = nc.dram_tensor("o_lo_d", [D, T], F32, kind="Internal").ap()
    m_hi_d = nc.dram_tensor("m_hi_d", [D, T], F32, kind="Internal").ap()
    mod_d = nc.dram_tensor("mod_d", [N_MOD * D // P, P], F32, kind="Internal").ap()
    h2_d = nc.dram_tensor("h2_d", [T, D], F32, kind="Internal").ap()
    token_d = nc.dram_tensor("token_d", [BLOCKS * P, 1], F32, kind="Internal").ap()
    y_d = nc.dram_tensor("y_d", [BLOCKS * P, D], F32, kind="Internal").ap()
    m_lo_d = nc.dram_tensor("m_lo_d", [D, T], F32, kind="Internal").ap()

    SB0, CONST, REGION = 16512, 10400, 65536
    top = [SB0]

    def at(name, shape, dt=F32):
        n = 4
        for s in shape[1:]:
            n *= s
        t = nc.alloc_sbuf_tensor_at(name, shape, dt, offset=top[0])
        top[0] += (n + 31) // 32 * 32
        return t

    ident = at("ident", [P, P])
    ones = at("ones", [P, P])
    incl = at("incl", [P, P])
    later = at("later", [P, P])
    level_mask = at("level_mask", [P, len(LEVELS), P])
    params = at("params", [P, 97])
    conv_w = at("conv_w", [P, QKV_TAPS, 3, H])
    c_act = at("c_act", [P, KD])
    mod = at("mod", [P, N_MOD, KD])
    scale1 = at("scale1", [P, KD])
    eps_col = at("eps_col", [P, 1])
    gates = at("gates", [P, 6, TT, H])
    G_LOG, G_BETA, G_NBETA, G_KBG, G_KDEC, G_LAST = range(6)
    slot_i = at("slot_i", [P, TOP_K, TT], I32)
    wts = at("wts", [P, TOP_K, TT])
    ids = at("ids", [P, BLOCKS], I32)
    ids_now = at("ids_now", [P, 2, 2], I32)
    over = at("over", [P, 2 + MAX_OVER], I32)
    logits = at("logits", [P, TT, NG + NE])
    mod_rows = at("mod_rows", [N_MOD * KD, P])
    assert top[0] <= SB0 + CONST
    top[0] = SB0 + CONST
    h_hi = at("h_hi", [P, KD, T], F32R)
    h_lo = at("h_lo", [P, KD, T], F32R)
    R1 = top[0]
    R2 = R1 + REGION
    END = 229376
    top[0] = R1
    s_hi = at("s_hi", [P, KD, T], F32R)
    s_lo = at("s_lo", [P, KD, T], F32R)
    top[0] = R2
    w_raw = at("w_raw", [P, SLOTS, KD, P])
    w_hi = at("w_hi", [P, SLOTS, KD, P], F32R)
    W_HI = top[0] - SLOTS * KD * P * 4
    w_lo = at("w_lo", [P, SLOTS, KD, P], F32R)
    SCRATCH = top[0]
    sc_sb = at("sc_sb", [P, T])
    prod = at("prod", [P, T + SC_TAPS - 1])
    sc_acc = at("sc_acc", [P, T])
    sc_y = at("sc_y", [P, T])
    ADA_B = top[0]
    ada_b = at("ada_b", [P, KD, 4 * P])
    assert top[0] <= END
    top[0] = R1
    ada = at("ada", [P, 2, KD, 4 * P])
    x_t = at("x_t", [P, 2, D])
    x_n = at("x_n", [P, 2, D])
    x_sq = at("x_sq", [P, D])
    ssq = at("ssq", [P, 3, TT])
    h_tmp = at("h_tmp", [P, KD, P])
    assert top[0] <= R2
    top[0] = W_HI
    ada_c = at("ada_c", [P, KD, 4 * P])
    assert top[0] <= SCRATCH
    ada_chunks = [ada[:, 0], ada[:, 1], ada_c[:], ada_b[:]]
    top[0] = SCRATCH
    rows_a = at("rows_a", [97, P])
    rows_b = at("rows_b", [96, P])
    w_gate = at("w_gate", [P, KD, 2 * H])
    w_gate_hi = at("w_gate_hi", [P, KD, 2 * H], F32R)
    w_gate_lo = at("w_gate_lo", [P, KD, 2 * H], F32R)
    dt_row = at("dt_row", [P, 2, H])
    graw = at("graw", [P, 2, TT, H])
    gtmp = at("gtmp", [P, 3, TT, H])
    gate_rows = at("gate_rows", [2 * H, T])
    assert top[0] <= ADA_B

    top[0] = R1
    QPAD = QKV_TAPS - 1
    conv_in = at("conv_in", [P, 2, T + QPAD])
    qk = at("qk", [P, 2, T])
    vv = at("vv", [P, T])
    X = at("X", [P, TT, P])
    Y = at("Y", [P, TT, P])
    LX = at("LX", [P, TT, P])
    decay = at("decay", [P, TT, P])
    grow = at("grow", [P, TT, P])
    q_dec = at("q_dec", [P, TT, P])
    kk_decay = at("kk_decay", [P, TT, P])
    intra = at("intra", [P, TT, P])
    k_bg = at("k_bg", [P, TT, P])
    k_dec = at("k_dec", [P, TT, P])
    S = at("S", [P, P])
    v_new = at("v_new", [P, 2, P])
    hgate = at("hgate", [P, 6, TT])
    hconv = at("hconv", [P, QKV_TAPS, 3])
    assert top[0] <= R2
    top[0] = SCRATCH
    v_beta = at("v_beta", [P, TT, P])
    w_neg = at("w_neg", [P, TT, P])
    o_raw = at("o_raw", [P, T])
    z_act = at("z_act", [P, T])
    gate_a = at("gate_a", [P, T])
    norm = at("norm", [P, T])
    o_hi = at("o_hi", [P, T], F32R)
    o_lo = at("o_lo", [P, T], F32R)
    assert top[0] <= END
    top[0] = SCRATCH
    ga_in = at("ga_in", [P, 2, T])
    mb_in = at("mb_in", [P, 2, T])
    m_hi = at("m_hi", [P, 2, T], F32R)
    m_lo = at("m_lo", [P, 2, T], F32R)
    assert top[0] <= END
    top[0] = SB0 + CONST
    wo_hi = at("wo_hi", [P, KD, D], F32R)
    wo_lo = at("wo_lo", [P, KD, D], F32R)
    top[0] = R1
    x1 = at("x1", [P, TT, D])
    R1B = top[0]
    gt1_row = at("gt1_row", [P, D])
    g2_row = at("g2_row", [P, D])
    sh2_row = at("sh2_row", [P, D])
    w_route = at("w_route", [P, KD, NG + NE])
    b_route = at("b_route", [P, NG + NE])
    stat2 = at("stat2", [P, 3, TT])
    h2 = at("h2", [P, 2, D])
    assert top[0] <= R2
    top[0] = R2
    mt_hi = at("mt_hi", [P, 2, KD, P], F32R)
    mt_lo = at("mt_lo", [P, 2, KD, P], F32R)
    xr = at("xr", [P, 2, D])
    sq2 = at("sq2", [P, D])
    h2T = at("h2T", [P, 2, KD, P])
    R_E = [P, TT, NE]
    g_cand = at("g_cand", [P, TT, NG])
    g_exp = at("g_exp", [P, TT, NG])
    g_one = at("g_one", [P, TT, NG])
    e_log = at("e_log", R_E)
    e_cand = at("e_cand", R_E)
    e_one = [at(f"e_one{k}", R_E) for k in range(TOP_K)]
    e_both = at("e_both", R_E)
    e_before = at("e_before", [P, TT + 1, NE])
    e_tmp = at("e_tmp", R_E)
    iota_g = at("iota_g", [P, NG])
    iota_e = at("iota_e", [P, NE])
    iota_b = at("iota_b", [P, MAX_OVER + 1])
    mults = at("mults", [P, MAX_OVER])
    over_tmp = at("over_tmp", [P, NE, MAX_OVER])
    over_cum = at("over_cum", [P, 2, NE])
    over_f = at("over_f", [P, 2 + MAX_OVER])
    r_small = at("r_small", [P, 16, TT])
    token_f = at("token_f", [P, TT])
    zeros = at("zeros", [P, P])
    id_rows = at("id_rows", [BLOCKS, P])
    assert top[0] <= END
    top[0] = SB0 + CONST
    ew = [None, None]
    ew[0] = [at("e0_w1", [P, KD, F]), at("e0_w3", [P, KD, F]), at("e0_w2", [P, FT, D])]
    y_sb = at("y_sb", [P, 2, D])
    hidT = at("hidT", [P, FT, P])
    hid = at("hid", [P, F])
    gate_act = at("gate_act", [P, F])
    assert top[0] <= R1
    top[0] = R1B
    xg = at("xg", [P, 2, D])
    xT = at("xT", [P, 2, KD, P])
    assert top[0] <= R2
    top[0] = R2
    ew[1] = [at("e1_w1", [P, KD, F]), at("e1_w3", [P, KD, F]), at("e1_w2", [P, FT, D])]
    E_END = top[0]
    assert top[0] <= END
    top[0] = SB0 + CONST
    Y_AHEAD = 4
    y_g = at("y_g", [P, TOP_K, Y_AHEAD, D])
    y_acc = at("y_acc", [P, 2, D])
    y_sq = at("y_sq", [P, D])
    res = at("res", [P, 2, D])
    gt2_row = at("gt2_row", [P, D])
    nf_row = at("nf_row", [P, D])
    stat3 = at("stat3", [P, 3, TT])
    assert top[0] <= R1

    ctx = ExitStack()
    with ctx:
        def sem(name):
            return ctx.enter_context(nc.semaphore(name))

        ps = ctx.enter_context(nc.psum_tensor("ps", [P, 8, HALF], F32))

        waits_passed = sem("waits_passed")
        params_in = sem("params_in")
        masks_done = sem("masks_done")
        pool_step = sem("pool_step")
        rows_turned = sem("rows_turned")
        cols_ready = sem("cols_ready")
        ada_in = [sem(f"ada_in{s}") for s in range(3)]
        ada_step = sem("ada_step")
        ada_used = sem("ada_used")
        mod_ready = sem("mod_ready")
        x_in = [sem(f"x_in{s}") for s in range(2)]
        x_squared = sem("x_squared")
        x_root = sem("x_root")
        x_mean = sem("x_mean")
        x_normed = sem("x_normed")
        x_turned = sem("x_turned")
        h_summed = sem("h_summed")
        h_hi_done = sem("h_hi_done")
        h_lo_done = sem("h_lo_done")
        gate_w_split = sem("gate_w_split")
        gate_logits = sem("gate_logits")
        gate_raw = sem("gate_raw")
        gate_exp = sem("gate_exp")
        gate_step = sem("gate_step")
        gates_done = sem("gates_done")
        w_in_sem = [sem(f"w_arrived{s}") for s in range(SLOTS)]
        w_hi_done = sem("w_hi_done")
        w_lo_done = sem("w_lo_done")
        proj_done = sem("proj_done")
        sc_copied = sem("sc_copied")
        prod_done = sem("prod_done")
        conv_step = sem("conv_step")
        sc_y_done = sem("sc_y_done")
        s_hi_done = sem("s_hi_done")
        s_lo_done = sem("s_lo_done")
        gb_sig = sem("gb_sig")
        mb_done = sem("mb_done")
        mb_out = sem("mb_out")
        bank_free = sem("bank_free")
        hgate_done = sem("hgate_done")
        pool_rows = sem("pool_rows")
        xy_init = sem("xy_init")
        decay_mm = sem("decay_mm")
        decay_exp = sem("decay_exp")
        hconv_step = sem("hconv_step")
        silu_done = sem("silu_done")
        squared = sem("squared")
        norm_mm = sem("norm_mm")
        root_done = sem("root_done")
        inv_root = sem("inv_root")
        qk_normed = sem("qk_normed")
        q_dec_done = sem("q_dec_done")
        kt_mm = sem("kt_mm")
        vt_mm = sem("vt_mm")
        k_bg_done = sem("k_bg_done")
        k_dec_done = sem("k_dec_done")
        v_beta_done = sem("v_beta_done")
        kk_mm = sem("kk_mm")
        kk_done = sem("kk_done")
        lx_mm = sem("lx_mm")
        lx_done = sem("lx_done")
        xl_mm = sem("xl_mm")
        yl_mm = sem("yl_mm")
        x_upd = sem("x_upd")
        y_upd = sem("y_upd")
        w_mm = sem("w_mm")
        w_neg_done = sem("w_neg_done")
        s_ready = sem("s_ready")
        vn_mm = sem("vn_mm")
        vn_done = sem("vn_done")
        ds_mm = sem("ds_mm")
        o_mm = sem("o_mm")
        o_copied = sem("o_copied")
        o_step = sem("o_step")
        o_hi_done = sem("o_hi_done")
        head_out = sem("head_out")
        o_in = sem("o_in")
        ga_arrived = [sem(f"ga_arrived{n}") for n in range(2)]
        mb_arrived = [sem(f"mb_arrived{n}") for n in range(2)]
        ga_sig = sem("ga_sig")
        m_step = sem("m_step")
        m_hi_done = sem("m_hi_done")
        m_lo_done = sem("m_lo_done")
        m_out = [sem(f"m_out{n}") for n in range(2)]
        mod_out = sem("mod_out")
        wo_in = sem("wo_in")
        wo_hi_done = sem("wo_hi_done")
        wo_lo_done = sem("wo_lo_done")
        merge_over = sem("merge_over")
        rows_in = sem("rows_in")
        mt_in = [sem(f"mt_in{n}") for n in range(2)]
        xr_in = [sem(f"xr_in{n}") for n in range(2)]
        out_mm = sem("out_mm")
        x1_scaled = sem("x1_scaled")
        x1_done = sem("x1_done")
        x1_squared = sem("x1_squared")
        x1_mean = sem("x1_mean")
        x1_root = sem("x1_root")
        x1_inv = sem("x1_inv")
        h2_scaled = sem("h2_scaled")
        h2_done = sem("h2_done")
        h2_turned = sem("h2_turned")
        h2T_done = sem("h2T_done")
        h2_out = [sem(f"h2_out{n}") for n in range(2)]
        logits_done = sem("logits_done")
        iotas = sem("iotas")
        r_step = sem("r_step")
        r_exp = sem("r_exp")
        counts_mm = sem("counts_mm")
        slots_ready = sem("slots_ready")
        tokens_out = sem("tokens_out")
        id_rows_in = sem("id_rows_in")
        ids_turned = sem("ids_turned")
        ids_ready = sem("ids_ready")
        ew_in = [[sem(f"ew_in{s_}_{j}") for j in range(3)] for s_ in range(2)]
        ids_now_ready = sem("ids_now_ready")
        xg_in = [sem(f"xg_in{n}") for n in range(2)]
        xT_mm = sem("xT_mm")
        xT_done = sem("xT_done")
        gu_mm = sem("gu_mm")
        gate_silu = sem("gate_silu")
        hid_done = sem("hid_done")
        hT_mm = sem("hT_mm")
        hT_done = sem("hT_done")
        dn_mm = sem("dn_mm")
        y_copied = [sem(f"y_copied{n}") for n in range(2)]
        y_out = [sem(f"y_out{n}") for n in range(2)]
        y_all = sem("y_all")
        yg_in = [sem(f"yg_in{n}") for n in range(4)]
        y_scaled = sem("y_scaled")
        y_summed = sem("y_summed")
        acc_step = sem("acc_step")
        res_done = sem("res_done")
        res_out = [sem(f"res_out{n}") for n in range(2)]

        R_GEXP, R_EEXP, R_BOTH = 7, 21, 23 + TT

        block = ctx.enter_context(nc.Block())

        ahead = [hid_done, x_turned, hT_mm, h_summed, m_step, wo_lo_done, out_mm, x1_done, prod_done, mb_done,
                 q_dec_done, head_out, logits_done, h_hi_done, s_hi_done, h_lo_done, mb_out, o_copied, h2_turned,
                 sc_copied, sc_y_done, gb_sig, root_done, h2T_done, *m_out, *y_out, *h2_out, *y_copied]

        def past(n):
            return n + 1

        def y_count(b, s):
            return 8 * (b - s)

        def over_blocks(eng, body):
            count = eng.value_load(over[0:1, 0:1], min_val=0, max_val=MAX_OVER)
            with eng.Fori(0, (MAX_OVER + 1) // 2) as i:
                for s in range(2):
                    with eng.If(2 * i + s < count):
                        body(2 * i + s + NE, s, 2 * i + s)
            return count

        def w_index(phase, i, p):
            s = stream[phase]
            return s["base"] + s["per"] * i + p

        def group(phase, i, p, half):
            return 2 * (SLOTS + w_index(phase, i, p)) + half + 1

        def slot_of(phase, p):
            return stream[phase]["tiles"][p % stream[phase]["per"]]["slot"]

        def load_w(eng, phase, i, p, src, col):
            t = stream[phase]["tiles"][p]
            last_split = w_index(phase, i, p) - t["back"] + 1
            col = eng.snap(col) if not isinstance(col, int) else col
            last_split = eng.snap(SLOTS + last_split) if not isinstance(last_split, int) else SLOTS + last_split
            eng.wait_ge(w_hi_done, last_split)
            eng.wait_ge(w_lo_done, last_split)
            eng.sem_inc(waits_passed, 1)
            eng.dma_start(w_raw[:, t["slot"]], src[:, :, bass.ds(col, P)]).then_inc(w_in_sem[t["slot"]], 16)

        def wait_raw(eng, phase, i, p):
            t = stream[phase]["tiles"][p]
            eng.wait_ge(w_in_sem[t["slot"]], 16 * (t["first_arrival"] + t["arrivals_per"] * i))

        def split_w_hi(act, phase, i, p):
            t = stream[phase]["tiles"][p]
            wait_raw(act, phase, i, p)
            act.wait_ge(proj_done, 2 * (SLOTS + w_index(phase, i, p) - t["back"] + 1))
            act.activation(w_hi[:, t["slot"]], w_raw[:, t["slot"]], ACT.Copy).then_inc(w_hi_done, 1)

        def split_w_lo(dve, phase, i, p):
            t = stream[phase]["tiles"][p]
            dve.wait_ge(w_hi_done, SLOTS + w_index(phase, i, p) + 1)
            dve.tensor_tensor(w_lo[:, t["slot"]], w_raw[:, t["slot"]], w_hi[:, t["slot"]],
                              ALU.subtract).then_inc(w_lo_done, 1)

        def next_tile(phase, i, p):
            return (phase, i, p + 1) if p + 1 < stream[phase]["per"] else (phase, i + 1, 0)

        def wait_w(pe, phase, i, p):
            pe.wait_ge(w_hi_done, SLOTS + w_index(phase, i, p) + 1)
            pe.wait_ge(w_lo_done, SLOTS + w_index(phase, i, p) + 1)

        def project(pe, dst, phase, p, hi, lo, half, ks=None, parts=range(3)):
            s = slot_of(phase, p)
            last = None
            ks = range(KD) if ks is None else ks
            cols = slice(half * HALF, (half + 1) * HALF)
            for k in ks:
                for part in range(3):
                    lhs = w_lo if part == 0 else w_hi
                    rhs = lo if part == 1 else hi
                    last = pe.matmul(dst, lhs[:, s, k], rhs[:, k, cols], start=(k == 0 and part == 0),
                                     stop=(k == KD - 1 and part == 2))
            return last

        def blocks_of(tile, n, odd):
            return tile.rearrange("p (m s r) -> p m s r", s=2, r=LEVELS[n])[:, :, odd, :]

        def half_dst(bank, t, n):
            return ps[:, bank, (t % 4) * P // 2:(t % 4 + 1) * P // 2].rearrange("p (m r) -> p m r", r=LEVELS[n])

        @block.gpsimd
        def _(pool):
            pool.memset(ident[:], 0.0).then_inc(pool_step, 1)
            pool.memset(ones[:], 1.0).then_inc(pool_step, 1)
            pool.memset(eps_col[:], EPS).then_inc(pool_step, 1)
            pool.memset(level_mask[:], 0.0).then_inc(pool_step, 1)
            pool.wait_ge(pool_step, 4)
            pool.affine_select(out=ident[:], in_=ident[:], compare_op=ALU.not_equal, fill=1.0, base=0,
                               pattern=[[-1, P]], channel_multiplier=1)
            pool.affine_select(out=incl[:], in_=ones[:], compare_op=ALU.is_ge, fill=0.0, base=0,
                               pattern=[[1, P]], channel_multiplier=-1)
            pool.affine_select(out=later[:], in_=ones[:], compare_op=ALU.is_gt, fill=0.0, base=0,
                               pattern=[[-1, P]], channel_multiplier=1).then_inc(masks_done, 1)
            for n, b in enumerate(LEVELS):
                even = level_mask[:, n].rearrange("p (m s r) -> p m s r", s=2, r=b)[:, :, 0, :]
                src = ones[:].rearrange("p (m s r) -> p m s r", s=2, r=b)[:, :, 0, :]
                m = P // (2 * b)
                pool.affine_select(out=even, in_=src, compare_op=ALU.is_ge, fill=0.0, base=-b,
                                   pattern=[[-2 * b, m], [0, b]], channel_multiplier=1).then_inc(pool_step, 1)
                pool.wait_ge(pool_step, 5 + n)
                pool.affine_select(out=even, in_=even, compare_op=ALU.is_ge, fill=0.0, base=2 * b - 1,
                                   pattern=[[2 * b, m], [0, b]], channel_multiplier=-1).then_inc(masks_done, 1)

            with pool.Fori(0, H) as h:
                pool.wait_ge(hgate_done, 2 * h + 2)
                logs = hgate[:, G_LOG, :, None].to_broadcast([P, TT, P])
                pool.tensor_tensor(X[:], later[:, None, :].to_broadcast([P, TT, P]), logs, ALU.mult)\
                    .then_inc(pool_rows, 1)
                pool.tensor_tensor(Y[:], ones[:, None, :].to_broadcast([P, TT, P]), logs, ALU.mult)\
                    .then_inc(pool_rows, 1)
                pool.wait_ge(decay_mm, 4 * h + 4)
                eye = ident[:, None, :].to_broadcast([P, TT, P])
                pool.tensor_tensor(X[:], eye, eye, ALU.mult).then_inc(xy_init, 1)
                pool.tensor_tensor(Y[:], eye, eye, ALU.mult).then_inc(xy_init, 1)

            pool.wait_ge(merge_over, 1)
            pool.iota(iota_g[:], pattern=[[1, NG]], base=0, channel_multiplier=0, allow_small_or_imprecise_dtypes=True)
            pool.iota(iota_e[:], pattern=[[1, NE]], base=0, channel_multiplier=0, allow_small_or_imprecise_dtypes=True)
            pool.iota(iota_b[:], pattern=[[1, MAX_OVER + 1]], base=0, channel_multiplier=0,
                      allow_small_or_imprecise_dtypes=True)
            pool.iota(mults[:], pattern=[[P, MAX_OVER]], base=P, channel_multiplier=0,
                      allow_small_or_imprecise_dtypes=True)
            pool.iota(token_f[:], pattern=[[P, TT]], base=0, channel_multiplier=1,
                      allow_small_or_imprecise_dtypes=True)
            pool.memset(zeros[:], 0.0).then_inc(iotas, 1)
            pool.wait_ge(iotas, 1)
            pool.dma_start(token_d.rearrange("(b p) o -> b (p o)", p=P), zeros[0:BLOCKS]).then_inc(tokens_out, 16)
            for b in range(NE, BLOCKS):
                pool.dma_start(y_d[b * P:(b + 1) * P, :].rearrange("p (k c) -> p k c", c=P),
                               zeros[:, None, :].to_broadcast([P, KD, P])).then_inc(tokens_out, 16)
            pool.wait_ge(tokens_out, 16 * (1 + BLOCKS - NE))
            for k in range(TOP_K):
                pool.wait_ge(slots_ready, k + 1)
                for t in range(TT):
                    pool.indirect_dma_start(token_d, bass.IndirectOffsetOnAxis(slot_i[:, k, t:t + 1], axis=0),
                                            token_f[:, t:t + 1], None, bounds_check=BLOCKS * P - 1)\
                        .then_inc(tokens_out, 16)
            def gather(b, s):
                want = b + 1
                for n in range(2):
                    pool.wait_ge(h2_out[n], past(16 * TT // 2))
                pool.wait_ge(ids_now_ready, want)
                pool.sem_inc(waits_passed, 1)
                pool.indirect_dma_start(xg[:, s], None, h2_d, bass.IndirectOffsetOnAxis(ids_now[:, s, 0:1], axis=0),
                                        bounds_check=T - 1).then_inc(xg_in[s], 16)
            gather(0, 0)
            with pool.Fori(0, NE // 2) as i:
                for s in range(2):
                    gather(2 * i + s + 1, 1 - s)
            over_blocks(pool, lambda b, s, j: gather(b + 1, 1 - s))
            pool.wait_ge(y_all, 1)
            for t in range(TT + Y_AHEAD):
                if t < TT:
                    if t >= Y_AHEAD:
                        pool.wait_ge(acc_step, 3 * (t - Y_AHEAD) + 2)
                    for k in range(TOP_K):
                        pool.indirect_dma_start(y_g[:, k, t % Y_AHEAD], None, y_d,
                                                bass.IndirectOffsetOnAxis(slot_i[:, k, t:t + 1], axis=0),
                                                bounds_check=BLOCKS * P - 1).then_inc(yg_in[t % Y_AHEAD], 16)
                if t >= Y_AHEAD:
                    n = t - Y_AHEAD
                    pool.wait_ge(acc_step, 3 * n + 3)
                    pool.tensor_tensor(y_acc[:, n % 2], y_acc[:, n % 2], x1[:, n], ALU.add).then_inc(y_summed, 1)

        N_MASKS = 1 + len(LEVELS)

        @block.sync
        def _(sp):
            row = 0
            for src in (c[0], norm1_g[0], norm2_g[0], b_ada[0], conv_sc_w[0].rearrange("t n -> (t n)"), onorm_g[0]):
                n = src.shape[0] // P
                sp.dma_start(rows_a[row:row + n, :], src.rearrange("(a b) -> a b", b=P)).then_inc(params_in, 16)
                row += n
            sp.dma_start(rows_b[:], conv_qkv_w[0].rearrange("t (a b) -> (t a) b", b=P)).then_inc(params_in, 16)
            sp.dma_start(dt_row[:, 0], a_log[0:1, :].to_broadcast([P, H])).then_inc(params_in, 16)
            sp.dma_start(dt_row[:, 1], dt_bias[0:1, :].to_broadcast([P, H])).then_inc(params_in, 16)
            sp.dma_start(w_gate[:], w_in_d[:, :, GATE0:SC0]).then_inc(params_in, 16)
            for n in range(4):
                if n == 3:
                    for t in range(2):
                        sp.dma_start(x_t[:, t], x_d[t * P:(t + 1) * P, :]).then_inc(x_in[t], 16)
                    sp.wait_ge(ada_step, 1)
                sp.dma_start(ada_chunks[n], w_ada_d[:, :, n * 4 * P:(n + 1) * 4 * P]).then_inc(ada_in[n % 3], 16)
            with sp.Fori(1, TT // 2) as i:
                for s in range(2):
                    row = sp.snap((2 * i + s) * P)
                    sp.wait_ge(x_normed, 2 * i + s - 1)
                    sp.dma_start(x_t[:, s], x_d[bass.ds(row, P), :]).then_inc(x_in[s], 16)
            with sp.Fori(0, KD) as i:
                for p, col in enumerate((SC0 + D, SC0 + 2 * D, SC0)):
                    load_w(sp, "conv", i, p, w_in_d, i * P + col)
                ada_col = sp.snap((4 + i) * 4 * P)
                sp.wait_ge(ada_used, 4 + i)
                sp.wait_ge(gates_done, 1)
                sp.dma_start(ada_b[:], w_ada_d[:, :, bass.ds(ada_col, 4 * P)]).then_inc(ada_in[2], 16)
            with sp.Fori(0, KD) as i:
                load_w(sp, "gate_b", i, 0, w_in_d, i * P + SC0 + 4 * D)
                load_w(sp, "gate_b", i, 1, w_b_d, i * P)
            with sp.Fori(0, H) as h:
                for p, col in enumerate((0, D, 2 * D, VAL0, SC0 + 3 * D)):
                    load_w(sp, "head", h, p, w_in_d, h * P + col)
            for p in range(2):
                load_w(sp, "merge", 0, p, w_a_d, p * P)
            sp.wait_ge(head_out, past(48 * H))
            sp.dma_start(s_hi[:].bitcast(F32), o_hi_d.rearrange("(k p) t -> p k t", p=P)).then_inc(o_in, 16)
            sp.dma_start(s_lo[:].bitcast(F32), o_lo_d.rearrange("(k p) t -> p k t", p=P)).then_inc(o_in, 16)

            def load_merge(i, p):
                row, free, lo_free = (2 * i + p) * P, 2 * i + p + 1, 2 * i + p
                if not isinstance(i, int):
                    row, free, lo_free = sp.snap(row), sp.snap(free), sp.snap(lo_free)
                sp.wait_ge(m_lo_done, free)
                sp.dma_start(ga_in[:, p], gate_a_d[bass.ds(row, P), :]).then_inc(ga_arrived[p], 16)
                sp.dma_start(mb_in[:, p], merged_b_d[bass.ds(row, P), :]).then_inc(mb_arrived[p], 16)
                sp.wait_ge(wo_lo_done, past(lo_free))
                sp.sem_inc(waits_passed, 1)
                sp.dma_start(w_raw[:, 2], w_o_d[:, :, bass.ds(row, P)]).then_inc(wo_in, 16)

            with sp.Fori(0, KD // 2 - 1) as i:
                for p in range(2):
                    load_w(sp, "merge", i + 1, p, w_a_d, (2 * i + 2 + p) * P)
                    load_merge(i, p)
            for p in range(2):
                load_merge(KD // 2 - 1, p)
            sp.wait_ge(proj_done, group("merge", KD // 2 - 1, 1, 1))
            sp.wait_ge(mod_out, 16)
            def mod_row(kind):
                return mod_d[kind * KD:(kind + 1) * KD, :].rearrange("(o k) p -> o (k p)", o=1).to_broadcast([P, D])
            for dst, src in ((gt1_row[:], mod_row(2)), (g2_row[:], mod_row(4)), (sh2_row[:], mod_row(3)),
                             (w_route[:, :, 0:NG], w_group[0].rearrange("(k p) n -> p k n", p=P)),
                             (w_route[:, :, NG:], w_expert[0].rearrange("(k p) n -> p k n", p=P)),
                             (b_route[:, 0:NG], b_group[0:1, :].to_broadcast([P, NG])),
                             (b_route[:, NG:], b_expert[0:1, :].to_broadcast([P, NE]))):
                sp.dma_start(dst, src).then_inc(rows_in, 16)
            sp.wait_ge(wo_lo_done, past(KD))
            sp.wait_ge(m_lo_done, 2 + KD)
            for n in range(2):
                sp.wait_ge(m_out[n], past(32 * KD // 2))
            sp.sem_inc(merge_over, 1)
            with sp.Fori(0, TT // 2) as i:
                for s in range(2):
                    row, used = sp.snap((2 * i + s) * P), sp.snap(2 * (2 * i + s))
                    sp.wait_ge(out_mm, past(used))
                    sp.dma_start(mt_hi[:, s].bitcast(F32), m_hi_d.rearrange("(k p) t -> p k t", p=P)
                                 [:, :, bass.ds(row, P)]).then_inc(mt_in[s], 16)
                    sp.dma_start(mt_lo[:, s].bitcast(F32), m_lo_d.rearrange("(k p) t -> p k t", p=P)
                                 [:, :, bass.ds(row, P)]).then_inc(mt_in[s], 16)
                    sp.wait_ge(x1_done, past(used))
                    sp.dma_start(xr[:, s], x_d[bass.ds(row, P), :]).then_inc(xr_in[s], 16)
            def load_expert(e, b, s):
                gu, dn = (4 * b, 2 * b) if isinstance(b, int) else (sp.snap(4 * b), sp.snap(2 * b))
                if not isinstance(e, int):
                    e = sp.snap(e)
                sp.wait_ge(gu_mm, gu)
                for j, w in enumerate((w1, w3)):
                    sp.dma_start(ew[s][j][:], w[0, bass.ds(e, 1)].rearrange("o (k p) f -> p (o k) f", p=P))\
                        .then_inc(ew_in[s][j], 16)
                sp.wait_ge(dn_mm, dn)
                sp.dma_start(ew[s][2][:], w2[0, bass.ds(e, 1)].rearrange("o (k p) f -> p (o k) f", p=P))\
                    .then_inc(ew_in[s][2], 16)
            sp.wait_ge(out_mm, past(2 + 2 * TT))
            load_expert(0, 0, 0)
            sp.wait_ge(tokens_out, 16 * (1 + BLOCKS - NE + TOP_K * TT))
            sp.dma_start(id_rows[:], token_d.rearrange("(b p) o -> b (p o)", p=P)).then_inc(id_rows_in, 16)
            sp.wait_ge(ids_ready, 2)
            sp.wait_ge(xg_in[0], 16)
            load_expert(1, 1, 1)
            with sp.Fori(1, NE // 2) as i:
                for s in range(2):
                    load_expert(2 * i + s, 2 * i + s, s)
            over_blocks(sp, lambda b, s, j: load_expert(
                sp.value_load(over[0:1, bass.ds(j + 1, 1)], min_val=0, max_val=NE - 1), b, s))
            sp.wait_ge(y_all, 1)
            sp.dma_start(gt2_row[:], mod_row(5)).then_inc(rows_in, 16)
            sp.dma_start(nf_row[:], normf_g.rearrange("(o n) -> o n", o=1).to_broadcast([P, D])).then_inc(rows_in, 16)
            with sp.Fori(0, TT // 2) as i:
                for s in range(2):
                    row, want = sp.snap((2 * i + s) * P), sp.snap(2 * i + s + 1)
                    sp.wait_ge(res_done, want)
                    sp.dma_start(out[0, bass.ds(row, P), :], res[:, s]).then_inc(res_out[s], 16)
            for s in range(2):
                sp.wait_ge(res_out[s], 16 * TT // 2)

        @block.scalar
        def _(act):
            act.wait_ge(rows_turned, 1)
            act.activation(params[:], ps[:, 0, 0:97], ACT.Copy).then_inc(cols_ready, 1)
            act.activation(conv_w[:].rearrange("p t k h -> p (t k h)"), ps[:, 1, 0:96], ACT.Copy)\
               .then_inc(cols_ready, 1)
            act.activation(c_act[:], ps[:, 0, 0:KD], ACT.Silu).then_inc(cols_ready, 1)
            act.wait_ge(params_in, 16 * 10)
            act.activation(w_gate_hi[:], w_gate[:], ACT.Copy).then_inc(gate_w_split, 1)
            def x_stats(i, s):
                col = bass.ds(2 * i + s, 1)
                act.wait_ge(x_in[s], 16 * i + 16)
                act.activation(x_sq[:], x_t[:, s], ACT.Square, accum_out=ssq[:, 0, col]).then_inc(x_squared, 1)
                act.wait_ge(x_mean, 2 * i + s + 1)
                act.activation(ssq[:, 1, col], ssq[:, 2, col], ACT.Sqrt).then_inc(x_root, 1)

            def h_high(i, s):
                act.wait_ge(h_summed, past(8 * (2 * i + s) + 8))
                act.activation(h_hi[:, :, bass.ds((2 * i + s) * P, P)], h_tmp[:], ACT.Copy).then_inc(h_hi_done, 1)

            x_stats(0, 0)
            with act.Fori(0, TT // 2 - 1) as i:
                x_stats(i, 1)
                h_high(i, 0)
                x_stats(i + 1, 0)
                h_high(i, 1)
            x_stats(TT // 2 - 1, 1)
            h_high(TT // 2 - 1, 0)
            h_high(TT // 2 - 1, 1)
            split_w_hi(act, "conv", 0, 0)
            for half in range(2):
                act.wait_ge(gate_logits, half + 1)
                act.activation(gate_rows[:, half * HALF:(half + 1) * HALF], ps[0:2 * H, 4 + half], ACT.Copy)\
                   .then_inc(gate_w_split, 1)
            act.wait_ge(gate_raw, 2)
            act.activation(gtmp[:, 0], graw[:, 0], ACT.Exp, scale=-1.0).then_inc(gate_exp, 1)
            act.activation(dt_row[:, 0], dt_row[:, 0], ACT.Exp).then_inc(gate_exp, 1)
            act.wait_ge(gate_step, 1)
            act.activation(gtmp[:, 2], gtmp[:, 1], ACT.Exp, scale=-1.0).then_inc(gate_exp, 1)
            act.wait_ge(gate_exp, 3)
            act.activation(gtmp[:, 2], gtmp[:, 2], ACT.Ln, bias=1.0).then_inc(gate_exp, 1)
            act.wait_ge(gate_logits, 4)
            for n, kind in enumerate((G_KBG, G_KDEC, G_LAST)):
                act.activation(gates[:, kind].rearrange("p t h -> p (t h)"),
                               ps[:, 3, n * TT * H:(n + 1) * TT * H], ACT.Exp).then_inc(gate_exp, 1)
            with act.Fori(0, KD) as i:
                split_w_hi(act, "conv", i, 1)
                act.wait_ge(prod_done, past(2 * i))
                for n in range(2):
                    act.wait_ge(proj_done, group("conv", i, 0, n))
                    act.activation(sc_sb[:, n * HALF:(n + 1) * HALF], ps[:, n], ACT.Copy).then_inc(sc_copied, 1)
                split_w_hi(act, "conv", i, 2)
                split_w_hi(act, *next_tile("conv", i, 2))
                act.wait_ge(sc_y_done, past(2 * i + 2))
                act.activation(s_hi[:, bass.ds(i, 1)].rearrange("p a t -> p (a t)"), sc_y[:], ACT.Copy)\
                   .then_inc(s_hi_done, 1)
            act.wait_ge(rows_turned, 2)
            act.activation(mod_rows[:], ps[0:N_MOD * KD, 7, 0:P], ACT.Copy).then_inc(cols_ready, 1)
            act.wait_ge(cols_ready, 4)
            act.dma_start(mod_d, mod_rows[:]).then_inc(mod_out, 16)
            with act.Fori(0, KD) as i:
                split_w_hi(act, "gate_b", i, 1)
                act.wait_ge(mb_done, past(2 * i))
                for n in range(2):
                    act.wait_ge(proj_done, group("gate_b", i, 0, n))
                    act.activation(sc_sb[:, n * HALF:(n + 1) * HALF], ps[:, n], ACT.Sigmoid).then_inc(gb_sig, 1)
                split_w_hi(act, *next_tile("gate_b", i, 1))
                act.wait_ge(mb_done, past(2 * i + 2))
                act.dma_start(merged_b_d[bass.ds(i * P, P), :], sc_y[:]).then_inc(mb_out, 16)
            split_w_hi(act, "head", 0, 1)
            act.wait_ge(mb_out, past(16 * KD))
            with act.Fori(0, H) as h:
                def evac(p, half, dst, func):
                    act.wait_ge(proj_done, group("head", h, p, half))
                    act.activation(dst, ps[:, half], func).then_inc(bank_free, 1)

                def evac_conv(p, slot):
                    for half in range(2):
                        evac(p, half, conv_in[:, slot, QPAD + half * HALF:QPAD + (half + 1) * HALF], ACT.Copy)

                def log_sums(n, banks, dst):
                    for half in range(2):
                        act.wait_ge(norm_mm, 6 * h + 2 * n + half + 1)
                        act.activation(dst[:, half * HALF:(half + 1) * HALF], ps[:, banks + half], ACT.Ln,
                                       bias=eps_col[:], scale=(1.0 / P if n == 2 else 1.0)).then_inc(root_done, 1)

                def inverse_root(dst):
                    act.activation(dst, dst, ACT.Exp, scale=-0.5).then_inc(inv_root, 1)

                evac_conv(0, 0)
                split_w_hi(act, "head", h, 2)
                evac_conv(1, 1)
                act.wait_ge(hconv_step, 16 * h + 4)
                act.activation(qk[:, 0], qk[:, 0], ACT.Silu).then_inc(silu_done, 1)
                act.wait_ge(silu_done, 3 * h + 1)
                lx_flat = LX[:].rearrange("p t i -> p (t i)")
                act.activation(lx_flat, qk[:, 0], ACT.Square).then_inc(squared, 1)
                act.wait_ge(hconv_step, 16 * h + 8)
                act.activation(qk[:, 1], qk[:, 1], ACT.Silu).then_inc(silu_done, 1)
                act.wait_ge(silu_done, 3 * h + 2)
                act.activation(kk_decay[:].rearrange("p t i -> p (t i)"), qk[:, 1], ACT.Square).then_inc(squared, 1)
                split_w_hi(act, "head", h, 3)
                act.wait_ge(q_dec_done, past(h))
                for n in range(4):
                    act.wait_ge(decay_mm, 4 * h + n + 1)
                    act.activation((decay, grow)[n // 2][:, (n % 2) * 4:(n % 2) * 4 + 4].rearrange("p t i -> p (t i)"),
                                   ps[:, 4 + n], ACT.Exp).then_inc(decay_exp, 1)
                norm_k = intra[:].rearrange("p t i -> p (t i)")
                log_sums(0, 4, norm)
                log_sums(1, 6, norm_k)
                act.wait_ge(root_done, past(6 * h + 4))
                inverse_root(norm_k)
                inverse_root(norm[:])
                split_w_hi(act, "head", h, 4)
                evac_conv(2, 0)
                for t in range(TT):
                    if t % 4 == 0:
                        act.wait_ge(kt_mm, 2 * h + t // 4 + 1)
                    if t == 4:
                        act.wait_ge(k_dec_done, TT * h + 4)
                    act.activation(k_bg[:, t], ps[:, 4 + t // 4, (t % 4) * P:(t % 4 + 1) * P], ACT.Copy,
                                   scale=hgate[:, G_KBG, t:t + 1]).then_inc(k_bg_done, 1)
                act.wait_ge(hconv_step, 16 * h + 16)
                act.activation(vv[:], vv[:], ACT.Silu).then_inc(silu_done, 1)
                for t in range(TT):
                    if t % 4 == 0:
                        act.wait_ge(vt_mm, 2 * h + t // 4 + 1)
                    act.activation(v_beta[:, t], ps[:, 4 + t // 4, (t % 4) * P:(t % 4 + 1) * P], ACT.Copy,
                                   scale=hgate[:, G_BETA, t:t + 1]).then_inc(v_beta_done, 1)
                for n in range(2):
                    act.wait_ge(w_mm, 2 * h + n + 1)
                    act.activation(w_neg[:, 4 * n:4 * n + 4].rearrange("p t i -> p (t i)"), ps[:, 6 + n], ACT.Copy,
                                   scale=-1.0).then_inc(w_neg_done, 1)
                act.wait_ge(head_out, past(48 * h))
                for t in range(TT):
                    act.wait_ge(vn_mm, TT * h + t + 1)
                    act.activation(v_new[:, t % 2], ps[:, 2, 0:P], ACT.Copy).then_inc(vn_done, 1)
                    act.wait_ge(o_mm, TT * h + t + 1)
                    act.activation(o_raw[:, t * P:(t + 1) * P], ps[:, 3 + t % 2, 0:P], ACT.Copy)\
                       .then_inc(o_copied, 1)
                    if t in (1, 3):
                        evac(3, t // 2, z_act[:, (t // 2) * HALF:(t // 2 + 1) * HALF], ACT.Silu)
                    if t == 5:
                        evac(4, 0, gate_a[:, 0:HALF], ACT.Copy)
                        split_w_hi(act, *next_tile("head", h, 4))
                evac(4, 1, gate_a[:, HALF:T], ACT.Copy)
                split_w_hi(act, "head", h + 1, 1)
                act.wait_ge(o_copied, past(TT * h + TT))
                act.activation(lx_flat, o_raw[:], ACT.Square).then_inc(squared, 1)
                act.wait_ge(bank_free, 2 + 10 * h + 10)
                act.dma_start(gate_a_d[bass.ds(h * P, P), :], gate_a[:]).then_inc(head_out, 16)
                log_sums(2, 4, norm)
                act.wait_ge(root_done, past(6 * h + 6))
                inverse_root(norm[:])
                act.wait_ge(o_step, 2 * h + 2)
                act.activation(o_hi[:], o_raw[:], ACT.Copy).then_inc(o_hi_done, 1)
                act.wait_ge(o_hi_done, 2 * h + 1)
                act.dma_start(o_hi_d[bass.ds(h * P, P), :], o_hi[:].bitcast(F32)).then_inc(head_out, 16)
                act.wait_ge(o_hi_done, 2 * h + 2)
                act.dma_start(o_lo_d[bass.ds(h * P, P), :], o_lo[:].bitcast(F32)).then_inc(head_out, 16)

            def merge_hi(i, last):
                for p in range(2):
                    if not last:
                        split_w_hi(act, "merge", i + 1, p)
                    act.wait_ge(ga_arrived[p], 16 * i + 16)
                    act.activation(ga_in[:, p], ga_in[:, p], ACT.Sigmoid).then_inc(ga_sig, 1)
                    act.wait_ge(wo_in, 16 * (2 * i + p) + 16)
                    act.activation(wo_hi[:, :, bass.ds((2 * i + p) * P, P)], w_raw[:, 2], ACT.Copy)\
                       .then_inc(wo_hi_done, 1)
                    act.wait_ge(m_step, past(3 * (2 * i + p) + 3))
                    act.wait_ge(m_out[p], past(32 * i))
                    act.activation(m_hi[:, p], ga_in[:, p], ACT.Copy).then_inc(m_hi_done, 1)
                    act.wait_ge(m_hi_done, 2 * i + p + 1)
                    act.dma_start(m_hi_d[bass.ds((2 * i + p) * P, P), :], m_hi[:, p].bitcast(F32))\
                       .then_inc(m_out[p], 16)
                    act.wait_ge(m_lo_done, 2 * i + p + 1 + 2)
                    act.dma_start(m_lo_d[bass.ds((2 * i + p) * P, P), :], m_lo[:, p].bitcast(F32))\
                       .then_inc(m_out[p], 16)

            act.wait_ge(proj_done, group("head", H - 1, 4, 1))
            with act.Fori(0, KD // 2 - 1) as i:
                merge_hi(i, False)
            merge_hi(KD // 2 - 1, True)
            act.wait_ge(rows_in, 16 * 7)
            with act.Fori(0, TT // 2) as i:
                for s in range(2):
                    n = 2 * i + s
                    act.wait_ge(x1_done, past(2 + 2 * n + 2))
                    act.activation(sq2[:], x1[:, bass.ds(n, 1)].rearrange("p o d -> p (o d)"), ACT.Square,
                                   accum_out=stat2[:, 0, bass.ds(n, 1)]).then_inc(x1_squared, 1)
                    act.wait_ge(x1_mean, n + 1)
                    act.activation(stat2[:, 1, bass.ds(n, 1)], stat2[:, 2, bass.ds(n, 1)], ACT.Sqrt)\
                       .then_inc(x1_root, 1)
                    act.wait_ge(h2_done, n + 1)
                    act.dma_start(h2_d[bass.ds(n * P, P), :], h2[:, s]).then_inc(h2_out[s], 16)
                    act.wait_ge(logits_done, past(n))
                    for half in range(2):
                        act.wait_ge(h2_turned, past(2 + 2 * n + half + 1))
                        act.activation(h2T[:, s, 4 * half:4 * half + 4].rearrange("p k t -> p (k t)"),
                                       ps[:, 4 + half], ACT.Copy).then_inc(h2T_done, 1)
            act.wait_ge(r_step, R_GEXP)
            act.activation(g_exp[:], g_cand[:], ACT.Exp).then_inc(r_exp, 1)
            act.wait_ge(r_step, R_EEXP)
            act.activation(r_small[:, 8], r_small[:, 7], ACT.Exp).then_inc(r_exp, 1)
            act.wait_ge(h2_out[0], past(16 * TT // 2))
            act.wait_ge(h2_out[1], past(16 * TT // 2))

            def copy_xT(b, s):
                for half in range(2):
                    act.wait_ge(xT_mm, 2 * b + half + 1)
                    act.activation(xT[:, s, 4 * half:4 * half + 4].rearrange("p k t -> p (k t)"), ps[:, half],
                                   ACT.Copy).then_inc(xT_done, 1)

            def block_act(b, s):
                for part in range(2):
                    act.wait_ge(gu_mm, 4 + 4 * b + 2 * part + 1)
                    act.wait_ge(hid_done, past(2 * b + part - (1 if part else 0)))
                    act.activation(gate_act[:, part * 2 * P:(part + 1) * 2 * P], ps[:, 2 * part, 0:2 * P], ACT.Silu)\
                       .then_inc(gate_silu, 1)
                for part in range(2):
                    act.wait_ge(hT_mm, past(2 * b + part + 1))
                    act.activation(hidT[:, 2 * part:2 * part + 2].rearrange("p f t -> p (f t)"),
                                   ps[:, 4 + part, 0:2 * P], ACT.Copy).then_inc(hT_done, 1)
                copy_xT(b + 1, 1 - s)
                act.wait_ge(dn_mm, 2 + 2 * b + 1)
                act.wait_ge(y_out[s], past(y_count(b, s)))
                act.activation(y_sb[:, s, 0:HALF], ps[:, 6], ACT.Copy).then_inc(y_copied[0], 1)
                act.wait_ge(y_copied[0], past(b + 1))
                act.wait_ge(y_copied[1], past(b + 1))
                act.dma_start(y_d[bass.ds(b * P, P), :], y_sb[:, s]).then_inc(y_out[s], 16)

            act.wait_ge(ids_ready, 2)
            copy_xT(0, 0)
            with act.Fori(0, NE // 2) as i:
                for s in range(2):
                    block_act(2 * i + s, s)
            count = over_blocks(act, lambda b, s, j: block_act(b, s))
            for s in range(2):
                act.wait_ge(y_out[s], past(16 * (NE // 2) + 16 * ((count + 1 - s) // 2)))
            act.sem_inc(y_all, 1)
            act.wait_ge(rows_in, 16 * 9)
            for n in range(TT + 1):
                if n < TT:
                    act.wait_ge(yg_in[n % Y_AHEAD], 32 * (n // Y_AHEAD) + 32)
                    act.activation(y_g[:, 0, n % Y_AHEAD], y_g[:, 0, n % Y_AHEAD], ACT.Copy,
                                   scale=wts[:, 0, n:n + 1]).then_inc(y_scaled, 1)
                if n >= 1:
                    m = n - 1
                    act.wait_ge(y_summed, m + 1)
                    act.activation(y_sq[:], y_acc[:, m % 2], ACT.Square, accum_out=stat3[:, 0, m:m + 1])\
                       .then_inc(x1_squared, 1)
                    act.wait_ge(x1_mean, TT + m + 1)
                    act.activation(stat3[:, 1, m:m + 1], stat3[:, 2, m:m + 1], ACT.Sqrt).then_inc(x1_root, 1)

        @block.vector
        def _(dve):
            def ada_sum(buf, chunk):
                for k in range(KD):
                    if k == 0:
                        ins = dve.tensor_scalar(buf[:, 0], buf[:, 0], c_act[:, 0:1], None, ALU.mult)
                    else:
                        dve.wait_ge(ada_step, KD * chunk + k)
                        ins = dve.scalar_tensor_tensor(out=buf[:, 0], in0=buf[:, k], scalar=c_act[:, k:k + 1],
                                                       in1=buf[:, 0], op0=ALU.mult, op1=ALU.add)
                    ins.then_inc(ada_step, 1)

            dve.wait_ge(cols_ready, 3)
            for n in range(4):
                dve.wait_ge(ada_in[n % 3], 16 * (n // 3 + 1))
                ada_sum(ada_chunks[n], n)
            dve.wait_ge(cols_ready, 2)
            dve.wait_ge(ada_used, 4)
            flat = mod[:].rearrange("p a k -> p (a k)")
            dve.tensor_tensor(flat[:, 0:2 * KD], ps[:, 7, 0:2 * KD], params[:, 3 * KD:5 * KD], ALU.add)\
               .then_inc(mod_ready, 1)
            dve.wait_ge(mod_ready, 1)
            dve.scalar_tensor_tensor(out=scale1[:], in0=mod[:, 1], scalar=1.0, in1=params[:, KD:2 * KD],
                                     op0=ALU.add, op1=ALU.mult).then_inc(mod_ready, 1)
            dve.wait_ge(gate_w_split, 1)
            dve.tensor_tensor(w_gate_lo[:], w_gate[:], w_gate_hi[:], ALU.subtract).then_inc(gate_w_split, 1)
            dve.wait_ge(mod_ready, 2)
            def x_norm(i, s):
                n = 2 * i + s
                col = bass.ds(n, 1)
                dve.wait_ge(x_squared, n + 1)
                dve.tensor_scalar(ssq[:, 2, col], ssq[:, 0, col], 1.0 / D, EPS, ALU.mult, ALU.add).then_inc(x_mean, 1)
                dve.wait_ge(x_root, n + 1)
                dve.reciprocal(ssq[:, 2, col], ssq[:, 1, col]).then_inc(conv_step, 1)
                dve.wait_ge(conv_step, n + 1)
                if not isinstance(n, int) or n >= 2:
                    dve.wait_ge(x_turned, past(2 * n - 2))
                dve.tensor_scalar(x_n[:, s], x_t[:, s], ssq[:, 2, col], None, ALU.mult).then_inc(x_normed, 1)

            def h_sum(i, s):
                n = 2 * i + s
                dve.wait_ge(h_hi_done, past(n))
                dve.wait_ge(h_lo_done, past(n))
                for k in range(KD):
                    if k % 4 == 0:
                        dve.wait_ge(x_turned, past(2 * n + k // 4 + 1))
                    dve.tensor_scalar(h_tmp[:, k], ps[:, 2 * s + k // 4, (k % 4) * P:(k % 4 + 1) * P],
                                      scale1[:, k:k + 1], mod[:, 0, k:k + 1], ALU.mult, ALU.add).then_inc(h_summed, 1)

            def h_low(i, s):
                n = 2 * i + s
                dve.wait_ge(h_hi_done, past(n + 1))
                dve.wait_ge(h_summed, past(8 * n + 8))
                dve.tensor_tensor(h_lo[:, :, bass.ds(n * P, P)], h_tmp[:], h_hi[:, :, bass.ds(n * P, P)],
                                  ALU.subtract).then_inc(h_lo_done, 1)

            x_norm(0, 0)
            with dve.Fori(0, TT // 2 - 1) as i:
                for s in range(2):
                    h_sum(i, s)
                    x_norm(i + s, 1 - s)
                    h_low(i, s)
            h_sum(TT // 2 - 1, 0)
            x_norm(TT // 2 - 1, 1)
            h_low(TT // 2 - 1, 0)
            h_sum(TT // 2 - 1, 1)
            h_low(TT // 2 - 1, 1)
            split_w_lo(dve, "conv", 0, 0)
            dve.wait_ge(gate_logits, 3)
            dve.wait_ge(params_in, 16 * 10)
            lg = ps[:, 2, 0:TT * 2 * H].rearrange("p (t z h) -> p z t h", t=TT, z=2)
            dve.tensor_copy(graw[:, 0], lg[:, 0]).then_inc(gate_raw, 1)
            dve.tensor_tensor(graw[:, 1], lg[:, 1],
                              dt_row[:, 1:2].to_broadcast([P, TT, H]), ALU.add).then_inc(gate_raw, 1)
            dve.wait_ge(gate_raw, 2)
            dve.scalar_tensor_tensor(out=gtmp[:, 1], in0=graw[:, 1], scalar=-1.0, in1=graw[:, 1],
                                     op0=ALU.mult, op1=ALU.max).then_inc(gate_step, 1)
            dve.wait_ge(gate_exp, 1)
            dve.tensor_scalar(gtmp[:, 0], gtmp[:, 0], 1.0, None, ALU.add).then_inc(gate_step, 1)
            dve.wait_ge(gate_step, 2)
            dve.reciprocal(gates[:, G_BETA], gtmp[:, 0]).then_inc(gate_step, 1)
            dve.wait_ge(gate_step, 3)
            dve.tensor_scalar(gates[:, G_NBETA], gates[:, G_BETA], -1.0, None, ALU.mult).then_inc(gate_step, 1)
            dve.wait_ge(gate_exp, 4)
            dve.scalar_tensor_tensor(out=gtmp[:, 0], in0=graw[:, 1], scalar=0.0, in1=gtmp[:, 2],
                                     op0=ALU.max, op1=ALU.add).then_inc(gate_step, 1)
            dve.wait_ge(gate_step, 5)
            dve.scalar_tensor_tensor(out=gates[:, G_LOG], in0=gtmp[:, 0], scalar=-1.0,
                                     in1=dt_row[:, 0:1].to_broadcast([P, TT, H]),
                                     op0=ALU.mult, op1=ALU.mult).then_inc(gate_step, 1)
            dve.wait_ge(gate_exp, 5)
            dve.tensor_tensor(gates[:, G_KBG], gates[:, G_KBG], gates[:, G_BETA], ALU.mult).then_inc(gate_step, 1)
            dve.wait_ge(gate_step, 7)
            dve.wait_ge(gate_exp, 7)
            dve.memset(prod[:, 0:SC_TAPS - 1], 0.0).then_inc(gates_done, 1)
            CS = TT
            taps = [params[:, 9 * KD + t * KD:9 * KD + (t + 1) * KD] for t in range(SC_TAPS)]
            with dve.Fori(0, KD) as i:
                split_w_lo(dve, "conv", i, 1)
                split_w_lo(dve, "conv", i, 2)
                for n in range(2):
                    cols = slice(n * HALF, (n + 1) * HALF)
                    dve.wait_ge(sc_copied, past(2 * i + n + 1))
                    dve.wait_ge(proj_done, group("conv", i, 1, n))
                    dve.tensor_tensor(prod[:, SC_TAPS - 1 + n * HALF:SC_TAPS - 1 + (n + 1) * HALF], ps[:, 2 + n],
                                      sc_sb[:, cols], ALU.mult).then_inc(prod_done, 1)
                dve.wait_ge(prod_done, past(2 * i + 2))
                dve.tensor_scalar(sc_acc[:], prod[:, 0:T], taps[0][:, bass.ds(i, 1)], None, ALU.mult)\
                   .then_inc(conv_step, 1)
                for t in range(1, SC_TAPS):
                    dve.wait_ge(conv_step, CS + SC_TAPS * i + t)
                    dve.scalar_tensor_tensor(out=sc_acc[:], in0=prod[:, t:t + T], scalar=taps[t][:, bass.ds(i, 1)],
                                             in1=sc_acc[:], op0=ALU.mult, op1=ALU.add).then_inc(conv_step, 1)
                split_w_lo(dve, *next_tile("conv", i, 2))
                dve.wait_ge(ada_in[2], 16 * i + 32)
                ada_sum(ada_b, i + 4)
                dve.wait_ge(conv_step, CS + SC_TAPS * i + SC_TAPS)
                dve.wait_ge(s_hi_done, past(i))
                for n in range(2):
                    cols = slice(n * HALF, (n + 1) * HALF)
                    dve.wait_ge(proj_done, group("conv", i, 2, n))
                    dve.tensor_tensor(sc_y[:, cols], ps[:, 4 + n], sc_acc[:, cols], ALU.mult).then_inc(sc_y_done, 1)
                dve.wait_ge(s_hi_done, past(i + 1))
                dve.wait_ge(sc_y_done, past(2 * i + 2))
                dve.tensor_tensor(s_lo[:, bass.ds(i, 1)].rearrange("p a t -> p (a t)"), sc_y[:],
                                  s_hi[:, bass.ds(i, 1)].rearrange("p a t -> p (a t)"), ALU.subtract)\
                   .then_inc(s_lo_done, 1)
            dve.wait_ge(ada_used, 2 * N_MOD)
            dve.tensor_tensor(flat[:, 2 * KD:], ps[:, 7, 2 * KD:N_MOD * KD], params[:, 5 * KD:9 * KD], ALU.add)\
               .then_inc(mod_ready, 1)
            dve.wait_ge(mod_ready, 3)
            dve.scalar_tensor_tensor(out=mod[:, 4], in0=mod[:, 4], scalar=1.0, in1=params[:, 2 * KD:3 * KD],
                                     op0=ALU.add, op1=ALU.mult).then_inc(mod_ready, 1)
            with dve.Fori(0, KD) as i:
                split_w_lo(dve, "gate_b", i, 1)
                split_w_lo(dve, *next_tile("gate_b", i, 1))
                dve.wait_ge(mb_out, past(16 * i))
                for n in range(2):
                    cols = slice(n * HALF, (n + 1) * HALF)
                    dve.wait_ge(gb_sig, past(2 * i + n + 1))
                    dve.wait_ge(proj_done, group("gate_b", i, 1, n))
                    dve.tensor_tensor(sc_y[:, cols], ps[:, 2 + n], sc_sb[:, cols], ALU.mult).then_inc(mb_done, 1)
            split_w_lo(dve, "head", 0, 1)
            dve.wait_ge(mb_out, past(16 * KD))
            dve.memset(conv_in[:, :, 0:QPAD], 0.0)
            with dve.Fori(0, H) as h:
                one = bass.ds(h, 1)

                def conv(p, slot, dst):
                    dve.wait_ge(bank_free, 2 + 10 * h + 2 * p + 2)
                    for t in range(QKV_TAPS):
                        if t > 0:
                            dve.wait_ge(hconv_step, 16 * h + 4 * p + t)
                        conv_tap(p, slot, dst, t, 0, T)

                def conv_tap(p, slot, dst, t, lo, hi):
                    src, w = conv_in[:, slot, t + lo:t + hi], hconv[:, t, p:p + 1]
                    if t == 0:
                        dve.tensor_scalar(dst[:, lo:hi], src, w, None, ALU.mult).then_inc(hconv_step, 1)
                    else:
                        dve.scalar_tensor_tensor(out=dst[:, lo:hi], in0=src, scalar=w, in1=dst[:, lo:hi],
                                                 op0=ALU.mult, op1=ALU.add).then_inc(hconv_step, 1)

                def conv_v_half(t, half):
                    if t == 0:
                        dve.wait_ge(bank_free, 2 + 10 * h + 6)
                    else:
                        dve.wait_ge(hconv_step, 16 * h + 8 + 2 * t + half - 1)
                    conv_tap(2, 0, vv, t, half * HALF, (half + 1) * HALF)

                dve.wait_ge(o_copied, past(TT * h))
                dve.tensor_copy(hgate[:], gates[:, :, :, one].rearrange("p a t h -> p a (t h)")).then_inc(hgate_done, 1)
                dve.tensor_copy(hconv[:], conv_w[:, :, :, one].rearrange("p a t h -> p a (t h)"))\
                   .then_inc(hgate_done, 1)
                dve.memset(S[:], 0.0).then_inc(s_ready, 1)
                dve.wait_ge(hgate_done, 2 * h + 2)
                conv(0, 0, qk[:, 0])
                split_w_lo(dve, "head", h, 2)
                conv(1, 1, qk[:, 1])
                split_w_lo(dve, "head", h, 3)
                dve.wait_ge(decay_exp, 4 * h + 4)
                dve.tensor_tensor(decay[:], decay[:], incl[:, None, :].to_broadcast([P, TT, P]), ALU.mult)
                split_w_lo(dve, "head", h, 4)
                dve.wait_ge(inv_root, 3 * h + 1)
                dve.tensor_tensor(qk[:, 1], qk[:, 1], intra[:].rearrange("p t i -> p (t i)"), ALU.mult)\
                   .then_inc(qk_normed, 1)
                dve.wait_ge(inv_root, 3 * h + 2)
                dve.scalar_tensor_tensor(out=qk[:, 0], in0=qk[:, 0], scalar=float(P) ** -0.5, in1=norm[:],
                                         op0=ALU.mult, op1=ALU.mult).then_inc(qk_normed, 1)
                for n, bank in enumerate((6, 2)):
                    dve.wait_ge(kk_mm, 2 * h + n + 1)
                    pair = ps[:, bank:bank + 2].rearrange("p b (t z i) -> p (b t) z i", z=2, i=P)
                    tiles = slice(4 * n, 4 * n + 4)
                    dve.tensor_tensor(kk_decay[:, tiles], pair[:, :, 1], decay[:, tiles], ALU.mult)\
                       .then_inc(kk_done, 1)
                    dve.tensor_tensor(intra[:, tiles], pair[:, :, 0], decay[:, tiles], ALU.mult).then_inc(kk_done, 1)
                dve.wait_ge(qk_normed, 2 * h + 2)
                dve.tensor_tensor(q_dec[:].rearrange("p t i -> p (t i)"), qk[:, 0],
                                  grow[:].rearrange("p t i -> p (t i)"), ALU.mult).then_inc(q_dec_done, 1)
                for n, t in enumerate((4, 5, 6, 7, 0, 1, 2, 3)):
                    if n == 0:
                        dve.wait_ge(kt_mm, 2 * h + 2)
                    if n == 4:
                        dve.wait_ge(k_bg_done, TT * h + 4)
                    dve.tensor_scalar(k_dec[:, t], ps[:, 4 + t // 4, (t % 4) * P:(t % 4 + 1) * P],
                                      hgate[:, G_KDEC, t:t + 1], None, ALU.mult).then_inc(k_dec_done, 1)
                NL = len(LEVELS)
                for n in range(NL):
                    for a in range(2):
                        dve.wait_ge(lx_mm, 2 * NL * h + 2 * n + a + 1)
                        for t in range(4 * a, 4 * a + 4):
                            last = dve.scalar_tensor_tensor(
                                out=LX[:, t], in0=ps[:, 6 + a, (t % 4) * P:(t % 4 + 1) * P],
                                scalar=hgate[:, G_NBETA, t:t + 1], in1=level_mask[:, n], op0=ALU.mult, op1=ALU.mult)
                        last.then_inc(lx_done, 1)
                    if n < QKV_TAPS:
                        conv_v_half(n, 0)
                    for a in range(2):
                        tiles = slice(4 * a, 4 * a + 4)
                        if n == 0:
                            dve.wait_ge(lx_done, 2 * NL * h + a + 1)
                        elif n < NL - 1:
                            dve.wait_ge(xl_mm, 2 * (NL - 2) * h + 2 * (n - 1) + a + 1)
                        dve.wait_ge(yl_mm, 2 * NL * h + 2 * n + a + 1)
                        if n < NL - 1:
                            x_even = blocks_of(X[:, tiles].rearrange("p t i -> p (t i)"), n, 0)
                            if n == 0:
                                change = blocks_of(LX[:, tiles].rearrange("p t i -> p (t i)"), n, 0)
                            else:
                                change = ps[:, 4 + a, 0:2 * P].rearrange("p (m r) -> p m r", r=LEVELS[n])
                            dve.tensor_tensor(x_even, x_even, change, ALU.add).then_inc(x_upd, 1)
                        y_odd = blocks_of(Y[:, tiles].rearrange("p t i -> p (t i)"), n, 1)
                        dve.tensor_tensor(y_odd, y_odd, ps[:, 2 + a, 0:2 * P]
                                          .rearrange("p (m r) -> p m r", r=LEVELS[n]), ALU.add).then_inc(y_upd, 1)
                        if n < QKV_TAPS and a == 0:
                            conv_v_half(n, 1)
                for t in range(TT):
                    dve.wait_ge(ds_mm, TT * h + t + 1)
                    dve.scalar_tensor_tensor(out=S[:], in0=S[:], scalar=hgate[:, G_LAST, t:t + 1],
                                             in1=ps[:, 2, P:2 * P], op0=ALU.mult, op1=ALU.add).then_inc(s_ready, 1)
                    if t == 6:
                        split_w_lo(dve, *next_tile("head", h, 4))
                split_w_lo(dve, "head", h + 1, 1)
                dve.wait_ge(inv_root, 3 * h + 3)
                dve.wait_ge(o_copied, past(TT * h + TT))
                dve.scalar_tensor_tensor(out=o_raw[:], in0=o_raw[:], scalar=params[:, 12 * KD:12 * KD + 1],
                                         in1=norm[:], op0=ALU.mult, op1=ALU.mult).then_inc(o_step, 1)
                dve.wait_ge(o_step, 2 * h + 1)
                dve.tensor_tensor(o_raw[:], o_raw[:], z_act[:], ALU.mult).then_inc(o_step, 1)
                dve.wait_ge(o_hi_done, 2 * h + 1)
                dve.wait_ge(o_step, 2 * h + 2)
                dve.tensor_tensor(o_lo[:], o_raw[:], o_hi[:], ALU.subtract).then_inc(o_hi_done, 1)

            def merge_lo(i, last):
                for p in range(2):
                    if not last:
                        split_w_lo(dve, "merge", i + 1, p)
                    step = 3 * (2 * i + p)
                    dve.wait_ge(wo_hi_done, 2 * i + p + 1)
                    dve.tensor_tensor(wo_lo[:, :, bass.ds((2 * i + p) * P, P)], w_raw[:, 2],
                                      wo_hi[:, :, bass.ds((2 * i + p) * P, P)], ALU.subtract).then_inc(wo_lo_done, 1)
                    dve.wait_ge(ga_sig, 2 * i + p + 1)
                    for half in range(2):
                        cols = slice(half * HALF, (half + 1) * HALF)
                        dve.wait_ge(proj_done, group("merge", i, p, half))
                        dve.tensor_tensor(ga_in[:, p, cols], ps[:, 2 * p + half], ga_in[:, p, cols], ALU.mult)\
                           .then_inc(m_step, 1)
                    dve.wait_ge(m_step, past(step + 2))
                    dve.wait_ge(mb_arrived[p], 16 * i + 16)
                    dve.tensor_tensor(ga_in[:, p], ga_in[:, p], mb_in[:, p], ALU.add).then_inc(m_step, 1)
                    dve.wait_ge(m_hi_done, 2 * i + p + 1)
                    dve.wait_ge(m_out[p], past(32 * i))
                    dve.tensor_tensor(m_lo[:, p], ga_in[:, p], m_hi[:, p], ALU.subtract).then_inc(m_lo_done, 1)

            with dve.Fori(0, KD // 2 - 1) as i:
                merge_lo(i, False)
            merge_lo(KD // 2 - 1, True)
            dve.wait_ge(rows_in, 16 * 7)
            with dve.Fori(0, TT // 2) as i:
                for s in range(2):
                    n = 2 * i + s
                    tile = x1[:, bass.ds(n, 1)].rearrange("p o d -> p (o d)")
                    dve.wait_ge(xr_in[s], 16 * i + 16)
                    for half in range(2):
                        cols = slice(half * HALF, (half + 1) * HALF)
                        dve.wait_ge(out_mm, past(2 + 2 * n + half + 1))
                        dve.tensor_tensor(tile[:, cols], ps[:, 2 * s + half], gt1_row[:, cols], ALU.mult)\
                           .then_inc(x1_scaled, 1)
                    for half in range(2):
                        cols = slice(half * HALF, (half + 1) * HALF)
                        dve.wait_ge(x1_scaled, 2 * n + half + 1)
                        dve.tensor_tensor(tile[:, cols], tile[:, cols], xr[:, s, cols], ALU.add).then_inc(x1_done, 1)
                    col = bass.ds(n, 1)
                    dve.wait_ge(x1_squared, n + 1)
                    dve.tensor_scalar(stat2[:, 2, col], stat2[:, 0, col], 1.0 / D, EPS, ALU.mult, ALU.add)\
                       .then_inc(x1_mean, 1)
                    dve.wait_ge(x1_root, n + 1)
                    dve.reciprocal(stat2[:, 2, col], stat2[:, 1, col]).then_inc(x1_inv, 1)
                    dve.wait_ge(x1_inv, n + 1)
                    dve.wait_ge(h2_turned, past(2 * n))
                    dve.wait_ge(h2_out[s], past(16 * i))
                    dve.scalar_tensor_tensor(out=h2[:, s], in0=tile, scalar=stat2[:, 2, col], in1=g2_row[:],
                                             op0=ALU.mult, op1=ALU.mult).then_inc(h2_scaled, 1)
                    dve.wait_ge(h2_scaled, n + 1)
                    dve.tensor_tensor(h2[:, s], h2[:, s], sh2_row[:], ALU.add).then_inc(h2_done, 1)
            dve.wait_ge(logits_done, past(TT))
            dve.wait_ge(iotas, 1)
            steps = [0]

            def link(ins):
                steps[0] += 1
                ins.then_inc(r_step, 1)
                dve.wait_ge(r_step, steps[0])

            def over_groups(x):
                return x[:, :, None].to_broadcast([P, TT, NG])

            def over_experts(x):
                return x[:, :, None].to_broadcast([P, TT, NE])

            def first_max(one, cand, values, iota, best, at_):
                n = values.shape[2]
                link(dve.tensor_reduce(best, values, AX.X, ALU.max))
                link(dve.tensor_tensor(cand, values, best[:, :, None].to_broadcast([P, TT, n]), ALU.is_equal))
                link(dve.scalar_tensor_tensor(out=cand, in0=cand, scalar=-1000.0,
                                              in1=iota[:, None, :].to_broadcast([P, TT, n]),
                                              op0=ALU.mult, op1=ALU.add))
                link(dve.tensor_reduce(at_, cand, AX.X, ALU.min))
                link(dve.tensor_tensor(one, cand, at_[:, :, None].to_broadcast([P, TT, n]), ALU.is_equal))

            def of_pair(dst, one, table):
                link(dve.tensor_tensor(e_tmp[:], one[:], table, ALU.mult))
                link(dve.tensor_reduce(dst, e_tmp[:], AX.X, ALU.add))

            S_ = [r_small[:, n] for n in range(16)]
            link(dve.tensor_tensor(logits[:], ps[:, 6, 0:TT * (NG + NE)].rearrange("p (t n) -> p t n", t=TT),
                                   b_route[:, None, :].to_broadcast([P, TT, NG + NE]), ALU.add))
            first_max(g_one[:], g_cand[:], logits[:, :, 0:NG], iota_g, S_[0], S_[1])
            link(dve.tensor_tensor(g_cand[:], logits[:, :, 0:NG], over_groups(S_[0]), ALU.subtract))
            assert steps[0] == R_GEXP
            link(dve.tensor_scalar(g_one[:], g_one[:], -1.0, None, ALU.add))
            link(dve.scalar_tensor_tensor(
                out=e_log[:].rearrange("p t (g e) -> p t g e", g=NG),
                in0=g_one[:, :, :, None].to_broadcast([P, TT, NG, NE // NG]), scalar=HUGE,
                in1=logits[:, :, NG:].rearrange("p t (g e) -> p t g e", g=NG), op0=ALU.mult, op1=ALU.add))
            first_max(e_one[0][:], e_cand[:], e_log[:], iota_e, S_[3], S_[4])
            link(dve.scalar_tensor_tensor(out=e_log[:], in0=e_one[0][:], scalar=-HUGE, in1=e_log[:],
                                          op0=ALU.mult, op1=ALU.add))
            first_max(e_one[1][:], e_cand[:], e_log[:], iota_e, S_[5], S_[6])
            link(dve.tensor_tensor(S_[7], S_[5], S_[3], ALU.subtract))
            assert steps[0] == R_EEXP
            link(dve.tensor_tensor(e_both[:], e_one[0][:], e_one[1][:], ALU.add))
            link(dve.memset(e_before[:, 0], 0.0))
            for t in range(TT):
                link(dve.tensor_tensor(e_before[:, t + 1], e_before[:, t], e_both[:, t], ALU.add))
            assert steps[0] == R_BOTH
            dve.wait_ge(r_exp, 2)
            link(dve.tensor_reduce(S_[2], g_exp[:], AX.X, ALU.add))
            link(dve.scalar_tensor_tensor(out=S_[9], in0=S_[8], scalar=1.0, in1=S_[2], op0=ALU.add, op1=ALU.mult))
            link(dve.reciprocal(wts[:, 0], S_[9]))
            link(dve.tensor_tensor(wts[:, 1], wts[:, 0], S_[8], ALU.mult))
            dve.wait_ge(counts_mm, 1)
            count = ps[:, 7, TT * NE:(TT + 1) * NE]
            link(dve.tensor_tensor(over_tmp[:], count[:, :, None].to_broadcast([P, NE, MAX_OVER]),
                                   mults[:, None, :].to_broadcast([P, NE, MAX_OVER]), ALU.is_gt))
            link(dve.tensor_reduce(over_cum[:, 0], over_tmp[:], AX.X, ALU.add))
            link(dve.tensor_copy(e_tmp[:, 0], over_cum[:, 0]))
            src, step = 0, 1
            while step < NE:
                link(dve.tensor_copy(over_cum[:, 1 - src, 0:step], over_cum[:, src, 0:step]))
                link(dve.tensor_tensor(over_cum[:, 1 - src, step:], over_cum[:, src, step:],
                                       over_cum[:, src, 0:NE - step], ALU.add))
                src, step = 1 - src, 2 * step
            link(dve.tensor_tensor(over_cum[:, 1 - src], over_cum[:, src], e_tmp[:, 0], ALU.subtract))
            first = over_cum[:, 1 - src]
            m_tmp = over_tmp[:].rearrange("p e b -> p (e b)")[:, 0:TT * MAX_OVER].rearrange("p (t b) -> p t b", t=TT)
            for k in range(TOP_K):
                of_pair(S_[10], e_one[k], ps[:, 7, 0:TT * NE].rearrange("p (t e) -> p t e", t=TT))
                link(dve.tensor_scalar(S_[10], S_[10], -1.0, None, ALU.add))
                link(dve.tensor_tensor(m_tmp, S_[10][:, :, None].to_broadcast([P, TT, MAX_OVER]),
                                       mults[:, None, :].to_broadcast([P, TT, MAX_OVER]), ALU.is_ge))
                link(dve.tensor_reduce(S_[11], m_tmp, AX.X, ALU.add))
                of_pair(S_[12], e_one[k], iota_e[:, None, :].to_broadcast([P, TT, NE]))
                of_pair(S_[13], e_one[k], first[:, None, :].to_broadcast([P, TT, NE]))
                link(dve.tensor_tensor(S_[13], S_[13], S_[11], ALU.add))
                link(dve.scalar_tensor_tensor(out=S_[13], in0=S_[13], scalar=float(NE - 1), in1=S_[12],
                                              op0=ALU.add, op1=ALU.subtract))
                link(dve.tensor_scalar(S_[14], S_[11], 1.0, None, ALU.min))
                link(dve.tensor_tensor(S_[13], S_[13], S_[14], ALU.mult))
                link(dve.tensor_tensor(S_[12], S_[12], S_[13], ALU.add))
                link(dve.tensor_tensor(S_[12], S_[12], S_[11], ALU.subtract))
                link(dve.scalar_tensor_tensor(out=S_[12], in0=S_[12], scalar=float(P), in1=S_[10],
                                              op0=ALU.mult, op1=ALU.add))
                link(dve.tensor_copy(slot_i[:, k], S_[12]))
                dve.sem_inc(slots_ready, 1)
            link(dve.memset(over_f[:], 0.0))
            link(dve.tensor_copy(over_f[:, 0:1], over_cum[:, src, NE - 1:NE]))
            link(dve.tensor_tensor(over_tmp[:].rearrange("p e b -> p (e b)").rearrange("p (b e) -> p b e", b=MAX_OVER),
                                   over_cum[:, src, None, :].to_broadcast([P, MAX_OVER, NE]),
                                   iota_b[:, 0:MAX_OVER, None].to_broadcast([P, MAX_OVER, NE]), ALU.is_le))
            link(dve.tensor_reduce(over_f[:, 1:1 + MAX_OVER], over_tmp[:].rearrange("p e b -> p (e b)")
                                   .rearrange("p (b e) -> p b e", b=MAX_OVER), AX.X, ALU.add))
            link(dve.tensor_scalar(over_f[:, 1:1 + MAX_OVER], over_f[:, 1:1 + MAX_OVER], float(NE - 1), None, ALU.min))
            link(dve.tensor_copy(over[:], over_f[:]))
            dve.wait_ge(ids_turned, 1)
            dve.tensor_copy(ids[:], ps[:, 7, 0:BLOCKS]).then_inc(ids_ready, 1)
            dve.wait_ge(ids_ready, 1)
            dve.sem_inc(ids_ready, 1)

            def next_ids(b, s):
                dve.tensor_copy(ids_now[:, s, 0:1], ids[:, bass.ds(b, 1)]).then_inc(ids_now_ready, 1)

            def block_dve(b, s):
                dve.wait_ge(xT_mm, 2 * b + 2)
                next_ids(b + 1, 1 - s)
                for part in range(2):
                    dve.wait_ge(gate_silu, 2 * b + part + 1)
                    dve.wait_ge(gu_mm, 4 + 4 * b + 2 * part + 2)
                    dve.wait_ge(hT_mm, past(2 * b))
                    cols = slice(part * 2 * P, (part + 1) * 2 * P)
                    dve.tensor_tensor(hid[:, cols], ps[:, 2 * part + 1, 0:2 * P], gate_act[:, cols], ALU.mult)\
                       .then_inc(hid_done, 1)
                dve.wait_ge(dn_mm, 2 + 2 * b + 2)
                dve.wait_ge(y_out[s], past(y_count(b, s)))
                dve.tensor_copy(y_sb[:, s, HALF:D], ps[:, 7]).then_inc(y_copied[1], 1)

            dve.tensor_copy(ids_now[:, 0, 0:1], ids[:, 0:1]).then_inc(ids_now_ready, 1)
            with dve.Fori(0, NE // 2) as i:
                for s in range(2):
                    block_dve(2 * i + s, s)
            over_blocks(dve, lambda b, s, j: block_dve(b, s))
            dve.wait_ge(y_all, 1)
            dve.wait_ge(rows_in, 16 * 9)
            for n in range(TT + 1):
                if n < TT:
                    s = n % 2
                    dve.wait_ge(yg_in[n % Y_AHEAD], 32 * (n // Y_AHEAD) + 32)
                    if n >= 2:
                        dve.wait_ge(res_done, n - 1)
                    dve.wait_ge(y_scaled, n + 1)
                    dve.scalar_tensor_tensor(out=y_acc[:, s], in0=y_g[:, 1, n % Y_AHEAD], scalar=wts[:, 1, n:n + 1],
                                             in1=y_g[:, 0, n % Y_AHEAD], op0=ALU.mult, op1=ALU.add)\
                        .then_inc(acc_step, 2)
                    dve.wait_ge(acc_step, 3 * n + 2)
                    dve.tensor_tensor(y_acc[:, s], y_acc[:, s], gt2_row[:], ALU.mult).then_inc(acc_step, 1)
                if n >= 1:
                    m = n - 1
                    dve.wait_ge(x1_squared, TT + m + 1)
                    dve.tensor_scalar(stat3[:, 2, m:m + 1], stat3[:, 0, m:m + 1], 1.0 / D, EPS, ALU.mult, ALU.add)\
                       .then_inc(x1_mean, 1)
                    dve.wait_ge(x1_root, TT + m + 1)
                    dve.reciprocal(stat3[:, 2, m:m + 1], stat3[:, 1, m:m + 1]).then_inc(x1_inv, 1)
                    dve.wait_ge(x1_inv, TT + m + 1)
                    if m >= 2:
                        dve.wait_ge(res_out[m % 2], 16 * (m // 2))
                    dve.scalar_tensor_tensor(out=res[:, m % 2], in0=y_acc[:, m % 2], scalar=stat3[:, 2, m:m + 1],
                                             in1=nf_row[:], op0=ALU.mult, op1=ALU.mult).then_inc(res_done, 1)

        @block.tensor
        def _(pe):
            for semaphore in ahead:
                pe.sem_inc(semaphore, 1)
            pe.sem_inc(proj_done, 2 * SLOTS)
            pe.sem_inc(w_hi_done, SLOTS)
            pe.sem_inc(w_lo_done, SLOTS)
            pe.sem_inc(bank_free, 2)
            pe.sem_inc(m_lo_done, 2)
            pe.sem_inc(out_mm, 2)
            pe.sem_inc(x1_done, 2)
            pe.sem_inc(h2_turned, 2)
            pe.sem_inc(gu_mm, 4)
            pe.sem_inc(dn_mm, 2)
            pe.wait_ge(masks_done, N_MASKS)
            pe.wait_ge(params_in, 16 * 10)
            pe.transpose(ps[:, 0, 0:97], rows_a[:], ident[0:97, 0:97])
            pe.transpose(ps[:, 1, 0:96], rows_b[:], ident[0:96, 0:96]).then_inc(rows_turned, 1)
            pe.wait_ge(cols_ready, 3)

            def ada_chunk(buf, chunk):
                pe.wait_ge(ada_step, KD * chunk + KD)
                for m in range(4):
                    last = pe.matmul(ps[:, 7, bass.ds(chunk * 4 + m, 1)], buf[:, 0, m * P:(m + 1) * P], ones[:, 0:1],
                                     start=True, stop=True)
                last.then_inc(ada_used, 1)

            for n in range(4):
                ada_chunk(ada_chunks[n], n)
            with pe.Fori(0, TT // 2) as i:
                for s in range(2):
                    n = 2 * i + s
                    pe.wait_ge(x_normed, n + 1)
                    pe.wait_ge(h_summed, past(16 * i))
                    for k in range(KD):
                        last = pe.transpose(ps[:, 2 * s + k // 4, (k % 4) * P:(k % 4 + 1) * P],
                                            x_n[:, s, k * P:(k + 1) * P], ident[:])
                        if k % 4 == 3:
                            last.then_inc(x_turned, 1)
            pe.wait_ge(h_lo_done, past(TT))
            pe.wait_ge(h_hi_done, past(TT))
            pe.wait_ge(gate_w_split, 2)
            for half in range(2):
                for k in range(KD):
                    for part in range(3):
                        lhs = w_gate_lo if part == 0 else w_gate_hi
                        rhs = h_lo if part == 1 else h_hi
                        last = pe.matmul(ps[0:2 * H, 4 + half], lhs[:, k], rhs[:, k, half * HALF:(half + 1) * HALF],
                                         start=(k == 0 and part == 0), stop=(k == KD - 1 and part == 2))
                last.then_inc(gate_logits, 1)
            pe.wait_ge(gate_w_split, 4)
            for t in range(TT):
                last = pe.transpose(ps[:, 2, t * 2 * H:(t + 1) * 2 * H], gate_rows[:, t * P:(t + 1) * P],
                                    ident[0:2 * H, 0:2 * H])
            last.then_inc(gate_logits, 1)
            pe.wait_ge(gate_step, 6)
            g_flat = gates[:, G_LOG].rearrange("p t h -> p (t h)")
            for n, mask in enumerate((incl, later, ones)):
                last = pe.matmul(ps[:, 3, n * TT * H:(n + 1) * TT * H], mask[:], g_flat, start=True, stop=True)
            last.then_inc(gate_logits, 1)
            pe.wait_ge(gate_exp, 7)
            pe.wait_ge(gates_done, 1)
            with pe.Fori(0, KD) as i:
                for p, (freed, per) in enumerate(((sc_copied, 2), (prod_done, 2), (sc_y_done, 2))):
                    wait_w(pe, "conv", i, p)
                    pe.wait_ge(freed, past(per * i))
                    for n in range(2):
                        last = project(pe, ps[:, 2 * p + n], "conv", p, h_hi, h_lo, n)
                        last.then_inc(proj_done, 1)
                ada_chunk(ada_b, i + 4)
            pe.wait_ge(s_lo_done, KD)
            pe.wait_ge(s_hi_done, past(KD))
            pe.wait_ge(mod_ready, 4)
            pe.transpose(ps[0:N_MOD * KD, 7, 0:P], mod[:].rearrange("p a k -> p (a k)"), ident[:])\
              .then_inc(rows_turned, 1)
            with pe.Fori(0, KD) as i:
                for p, freed in enumerate((gb_sig, mb_done)):
                    wait_w(pe, "gate_b", i, p)
                    pe.wait_ge(freed, past(2 * i))
                    for n in range(2):
                        last = project(pe, ps[:, 2 * p + n], "gate_b", p, (h_hi, s_hi)[p], (h_lo, s_lo)[p], n)
                        last.then_inc(proj_done, 1)
            pe.wait_ge(mb_done, past(2 * KD))
            NL = len(LEVELS)
            with pe.Fori(0, H) as h:
                def head_tile(p):
                    wait_w(pe, "head", h, p)
                    for half in range(2):
                        pe.wait_ge(bank_free, 2 + 10 * h + 2 * p + half - 1)
                        project(pe, ps[:, half], "head", p, h_hi, h_lo, half).then_inc(proj_done, 1)

                def square_sums(n, banks, src):
                    pe.wait_ge(squared, 3 * h + n + 1)
                    for half in range(2):
                        pe.matmul(ps[:, banks + half], ones[:], src[:, half * HALF:(half + 1) * HALF],
                                  start=True, stop=True).then_inc(norm_mm, 1)

                lx_flat = LX[:].rearrange("p t i -> p (t i)")
                head_tile(0)
                head_tile(1)
                pe.wait_ge(pool_rows, 2 * h + 2)
                pe.wait_ge(root_done, past(6 * h))
                for n in range(4):
                    src = (X, Y)[n // 2]
                    for t in range(4):
                        last = pe.matmul(ps[:, 4 + n, t * P:(t + 1) * P], src[:, (n % 2) * 4 + t], incl[:],
                                         start=True, stop=True)
                    last.then_inc(decay_mm, 1)
                wait_w(pe, "head", h, 2)
                pe.wait_ge(bank_free, 2 + 10 * h + 3)
                project(pe, ps[:, 0], "head", 2, h_hi, h_lo, 0).then_inc(proj_done, 1)
                pe.wait_ge(decay_exp, 4 * h + 4)
                square_sums(0, 4, lx_flat)
                square_sums(1, 6, kk_decay[:].rearrange("p t i -> p (t i)"))
                pe.wait_ge(bank_free, 2 + 10 * h + 4)
                project(pe, ps[:, 1], "head", 2, h_hi, h_lo, 1).then_inc(proj_done, 1)
                pe.wait_ge(root_done, past(6 * h + 2))
                pe.wait_ge(qk_normed, 2 * h + 1)
                for t in range(TT):
                    last = pe.transpose(ps[:, 4 + t // 4, (t % 4) * P:(t % 4 + 1) * P],
                                        qk[:, 1, t * P:(t + 1) * P], ident[:])
                    if t % 4 == 3:
                        last.then_inc(kt_mm, 1)
                pe.wait_ge(qk_normed, 2 * h + 2)
                pe.wait_ge(root_done, past(6 * h + 4))
                for n, bank in enumerate((6, 2)):
                    for t in range(4):
                        tok = slice((4 * n + t) * P, (4 * n + t + 1) * P)
                        last = pe.matmul(ps[:, bank + t // 2, (t % 2) * 2 * P:(t % 2 + 1) * 2 * P],
                                         qk[:, 1, tok], qk[:, :, tok], start=True, stop=True)
                    last.then_inc(kk_mm, 1)
                pe.wait_ge(xy_init, 2 * h + 2)
                for n in range(NL):
                    for a in range(2):
                        if n == 0:
                            pe.wait_ge(kk_done, 4 * h + 4)
                        else:
                            pe.wait_ge(x_upd, 2 * (NL - 1) * h + 2 * (n - 1) + a + 1)
                        for t in range(4 * a, 4 * a + 4):
                            lx = ps[:, 6 + a, (t % 4) * P:(t % 4 + 1) * P]
                            if n == 0:
                                last = pe.transpose(lx, kk_decay[:, t], ident[:])
                            else:
                                last = pe.matmul(lx, kk_decay[:, t], X[:, t], start=True, stop=True)
                        last.then_inc(lx_mm, 1)
                    if n == NL - 1:
                        pe.wait_ge(silu_done, 3 * h + 3)
                        for t in range(TT):
                            last = pe.transpose(ps[:, 4 + t // 4, (t % 4) * P:(t % 4 + 1) * P],
                                                vv[:, t * P:(t + 1) * P], ident[:])
                            if t % 4 == 3:
                                last.then_inc(vt_mm, 1)
                    for a in range(2):
                        pe.wait_ge(lx_done, 2 * NL * h + 2 * n + a + 1)
                        if n > 0:
                            pe.wait_ge(y_upd, 2 * NL * h + 2 * (n - 1) + a + 1)
                        if n == 1 and a == 0:
                            pe.wait_ge(k_bg_done, TT * h + TT)
                            pe.wait_ge(k_dec_done, TT * h + TT)
                        if 0 < n < NL - 1:
                            for t in range(4 * a, 4 * a + 4):
                                last = pe.matmul(half_dst(4 + a, t, n), Y[:, t], blocks_of(LX[:, t], n, 0),
                                                 start=True, stop=True)
                            last.then_inc(xl_mm, 1)
                        for t in range(4 * a, 4 * a + 4):
                            last = pe.matmul(half_dst(2 + a, t, n), LX[:, t], blocks_of(Y[:, t], n, 1),
                                             start=True, stop=True)
                        last.then_inc(yl_mm, 1)
                for a in range(2):
                    pe.wait_ge(y_upd, 2 * NL * h + 2 * (NL - 1) + a + 1)
                    for t in range(4 * a, 4 * a + 4):
                        last = pe.matmul(ps[:, 6 + a, (t % 4) * P:(t % 4 + 1) * P], k_bg[:, t], Y[:, t],
                                         start=True, stop=True)
                    last.then_inc(w_mm, 1)
                pe.wait_ge(q_dec_done, past(h + 1))
                pe.wait_ge(v_beta_done, TT * h + TT)

                def filler(n):
                    p, half, quarter = 3 + n // 8, n // 4 % 2, n % 4
                    if quarter == 0:
                        wait_w(pe, "head", h, p)
                        pe.wait_ge(bank_free, 2 + 10 * h + 2 * p + half - 1)
                    last = project(pe, ps[:, half], "head", p, h_hi, h_lo, half, ks=range(2 * quarter, 2 * quarter + 2))
                    if quarter == 3:
                        last.then_inc(proj_done, 1)

                for t in range(TT):
                    pe.wait_ge(s_ready, (TT + 1) * h + t + 1)
                    if t % 4 == 0:
                        pe.wait_ge(w_neg_done, 2 * h + t // 4 + 1)
                    pe.matmul(ps[:, 2, 0:P], Y[:, t], v_beta[:, t], start=True, stop=False)
                    pe.matmul(ps[:, 2, 0:P], w_neg[:, t], S[:], start=False, stop=True).then_inc(vn_mm, 1)
                    if t >= 2:
                        pe.wait_ge(o_copied, past(TT * h + t - 1))
                    o_t = ps[:, 3 + t % 2, 0:P]
                    pe.matmul(o_t, S[:], q_dec[:, t], start=True, stop=False)
                    filler(2 * t)
                    pe.wait_ge(vn_done, TT * h + t + 1)
                    pe.matmul(ps[:, 2, P:2 * P], k_dec[:, t], v_new[:, t % 2], start=True, stop=True)\
                      .then_inc(ds_mm, 1)
                    pe.matmul(o_t, v_new[:, t % 2], intra[:, t], start=False, stop=True).then_inc(o_mm, 1)
                    filler(2 * t + 1)
                square_sums(2, 4, lx_flat)
            pe.wait_ge(o_in, 32)
            pe.wait_ge(root_done, past(6 * H))
            with pe.Fori(0, KD // 2) as i:
                for p in range(2):
                    wait_w(pe, "merge", i, p)
                    pe.wait_ge(m_step, past(6 * i + 3 * p - 3 * p))
                    for half in range(2):
                        project(pe, ps[:, 2 * p + half], "merge", p, s_hi, s_lo, half).then_inc(proj_done, 1)
            def project_out(n, s):
                pe.wait_ge(mt_in[s], 16 * n - 16 * s + 32)
                pe.wait_ge(x1_done, past(2 * n))
                for half in range(2):
                    for k in range(KD):
                        for part in range(3):
                            lhs = mt_lo if part == 0 else mt_hi
                            rhs = wo_lo if part == 1 else wo_hi
                            last = pe.matmul(ps[:, 2 * s + half], lhs[:, s, k], rhs[:, k, half * HALF:(half + 1) * HALF],
                                             start=(k == 0 and part == 0), stop=(k == KD - 1 and part == 2))
                    last.then_inc(out_mm, 1)

            def route(n, s):
                pe.wait_ge(h2_done, n + 1)
                pe.wait_ge(h2T_done, past(2 * n))
                for k in range(KD):
                    last = pe.transpose(ps[:, 4 + k // 4, (k % 4) * P:(k % 4 + 1) * P], h2[:, s, k * P:(k + 1) * P],
                                        ident[:])
                    if k % 4 == 3:
                        last.then_inc(h2_turned, 1)
                pe.wait_ge(h2T_done, past(2 * n + 2))
                for k in range(KD):
                    last = pe.matmul(ps[:, 6, bass.ds(n * (NG + NE), NG + NE)], h2T[:, s, k], w_route[:, k],
                                     start=(k == 0), stop=(k == KD - 1))
                last.then_inc(logits_done, 1)

            pe.wait_ge(m_step, past(3 * KD))
            pe.wait_ge(wo_lo_done, past(KD))
            project_out(0, 0)
            pe.wait_ge(rows_in, 16 * 7)
            with pe.Fori(0, TT // 2 - 1) as i:
                project_out(2 * i + 1, 1)
                route(2 * i, 0)
                project_out(2 * i + 2, 0)
                route(2 * i + 1, 1)
            project_out(TT - 1, 1)
            route(TT - 2, 0)
            route(TT - 1, 1)
            pe.wait_ge(r_step, R_BOTH)
            pe.matmul(ps[:, 7, 0:TT * NE], incl[:], e_both[:].rearrange("p t e -> p (t e)"), start=True, stop=False)
            pe.matmul(ps[:, 7, 0:TT * NE], ones[:], e_before[:, 0:TT].rearrange("p t e -> p (t e)"),
                      start=False, stop=True)
            pe.matmul(ps[:, 7, TT * NE:(TT + 1) * NE], ones[:], e_before[:, TT], start=True, stop=True)\
              .then_inc(counts_mm, 1)
            pe.wait_ge(id_rows_in, 16)
            pe.wait_ge(slots_ready, TOP_K)
            pe.transpose(ps[:, 7, 0:BLOCKS], id_rows[:], ident[0:BLOCKS, 0:BLOCKS]).then_inc(ids_turned, 1)

            def turn_rows(b, s, first=False):
                pe.wait_ge(xg_in[s], y_count(b, s) + 16)
                for k in range(KD):
                    last = pe.transpose(ps[:, k // 4, (k % 4) * P:(k % 4 + 1) * P], xg[:, s, k * P:(k + 1) * P],
                                        ident[:])
                    if k % 4 == 3:
                        last.then_inc(xT_mm, 1)

            def block_pe(b, s):
                wa, wb, wc = ew[s]

                def up(part, which):
                    for k in range(KD):
                        last = pe.matmul(ps[:, 2 * part + which, 0:2 * P], xT[:, s, k],
                                         (wa, wb)[which][:, k, part * 2 * P:(part + 1) * 2 * P],
                                         start=(k == 0), stop=(k == KD - 1))
                    last.then_inc(gu_mm, 1)

                def turn_hidden(part):
                    pe.wait_ge(hid_done, past(2 * b + part + 1))
                    for f in range(2):
                        col = (2 * part + f) * P
                        last = pe.transpose(ps[:, 4 + part, f * P:(f + 1) * P], hid[:, col:col + P], ident[:])
                    last.then_inc(hT_mm, 1)

                def down(part):
                    pe.wait_ge(hT_done, 2 * b + part + 1)
                    for half in range(2):
                        for f in range(2 * part, 2 * part + 2):
                            last = pe.matmul(ps[:, 6 + half], hidT[:, f], wc[:, f, half * HALF:(half + 1) * HALF],
                                             start=(f == 0), stop=(f == FT - 1))
                        if part == 1:
                            last.then_inc(dn_mm, 1)

                pe.wait_ge(xT_done, 2 * b + 2)
                pe.wait_ge(ew_in[s][0], y_count(b, s) + 16)
                up(0, 0)
                pe.wait_ge(ew_in[s][1], y_count(b, s) + 16)
                up(0, 1)
                up(1, 0)
                turn_hidden(0)
                up(1, 1)
                pe.wait_ge(ew_in[s][2], y_count(b, s) + 16)
                pe.wait_ge(y_copied[0], past(b))
                pe.wait_ge(y_copied[1], past(b))
                down(0)
                turn_hidden(1)
                turn_rows(b + 1, 1 - s)
                down(1)

            pe.wait_ge(ids_ready, 2)
            turn_rows(0, 0)
            with pe.Fori(0, NE // 2) as i:
                for s in range(2):
                    block_pe(2 * i + s, s)
            over_blocks(pe, lambda b, s, j: block_pe(b, s))


_INS = ['x', 'c', 'w_ada', 'b_ada', 'norm1_g', 'w_in', 'conv_qkv_w', 'a_log', 'dt_bias', 'onorm_g', 'w_proj_a',
        'conv_sc_w', 'w_proj_b', 'w_out', 'norm2_g', 'w_group', 'b_group', 'w_expert', 'b_expert', 'w1', 'w3', 'w2',
        'normf_g']
_OUTS = [((1, 1024, 1024), 'float32')]


def kernel(**inputs):
    import numpy as _np
    import concourse.bacc as _bacc
    from concourse import mybir as _mybir
    from concourse.bass_utils import run_bass_kernel_spmd as _run

    nc = _bacc.Bacc("TRN2", target_bir_lowering=False, num_devices=1)
    arrays, args = {}, []
    for name in _INS:
        a = _np.ascontiguousarray(inputs[name])
        arrays[f"in_{name}_dram"] = a
        args.append(nc.dram_tensor(f"in_{name}_dram", a.shape, _mybir.dt.from_np(a.dtype), kind="ExternalInput").ap())
    for i, (shape, dtype) in enumerate(_OUTS):
        dt = _mybir.dt.from_np(_np.dtype(dtype))
        args.append(nc.dram_tensor(f"out_{i}_dram", shape, dt, kind="ExternalOutput").ap())
    decoder_block(nc, *args)
    r = _run(nc, [arrays], core_ids=[0])
    got = tuple(r.results[0][f"out_{i}_dram"] for i in range(len(_OUTS)))
    return got[0]
```
